# Optimizing a Trainium2 kernel written in Bass

```python
import math
import jax, jax.numpy as jnp
from jax import lax
import numpy as np

D_MODEL = 2048
BATCH = 1
SEQ = 256
DEPTH = 1

CHUNK = 64
EPS = 1e-6

S5_GROUPS = 32
S5_GROUP_DIM = 16
S5_WIDTH = S5_GROUPS * S5_GROUP_DIM
S5_STATE = 64
S5_DT_MIN = 1e-3
S5_DT_MAX = 1e-1

HG_HEADS = 6
HG_DK = 128
HG_DV = 128
HG_KEY_WIDTH = HG_HEADS * HG_DK
HG_WIDTH = HG_HEADS * HG_DV

ML_HEADS = 4
ML_DH = 192
ML_WIDTH = ML_HEADS * ML_DH
ML_CONV = 4

MIX_WIDTH = S5_WIDTH + HG_WIDTH + ML_WIDTH
N_BRANCH = 3

FFN_DIM = 5632
FFN_CONV = 3

IN_WIDTHS = (S5_WIDTH,
             HG_KEY_WIDTH, HG_KEY_WIDTH,
             HG_WIDTH, HG_WIDTH,
             ML_WIDTH, ML_WIDTH, ML_WIDTH,
             ML_HEADS, ML_HEADS,
             N_BRANCH * D_MODEL)
IN_TOTAL = 12040


def _split_points():
    pts, acc = [], 0
    for w in IN_WIDTHS[:-1]:
        acc += w
        pts.append(acc)
    return pts

def rms_norm(x, g):
    xf = x.astype(jnp.float32)
    y = xf * lax.rsqrt(jnp.mean(xf * xf, axis=-1, keepdims=True) + EPS)
    return (y * g.astype(jnp.float32)).astype(x.dtype)

def causal_dwconv(x, w, b):
    k, c = w.shape[0], x.shape[-1]
    y = lax.conv_general_dilated(x, w[:, None, :].astype(x.dtype), window_strides=(1,),
                                 padding=((k - 1, 0),), dimension_numbers=('NWC', 'WIO', 'NWC'),
                                 feature_group_count=c)
    return y + b.astype(x.dtype)

def to_chunks(t, n_heads, d):
    bsz, seq = t.shape[0], t.shape[1]
    return t.reshape(bsz, seq // CHUNK, CHUNK, n_heads, d).transpose(1, 0, 3, 2, 4)

def from_chunks(t):
    nc, bsz, h, l, d = t.shape
    return t.transpose(1, 0, 3, 2, 4).reshape(bsz, nc * l, h, d)

def s5_mixer(u, lam_re, lam_im, log_dt, b_re, b_im, c_re, c_im, d_skip, w_glu, b_glu):
    bsz, seq, _ = u.shape
    f32 = jnp.float32
    uf = u.astype(f32).reshape(bsz, seq, S5_GROUPS, S5_GROUP_DIM)
    dt = jnp.exp(log_dt.astype(f32))[:, None]
    lr, li = lam_re.astype(f32), lam_im.astype(f32)
    mag = jnp.exp(lr * dt)
    ar, ai = mag * jnp.cos(li * dt), mag * jnp.sin(li * dt)
    den = lr * lr + li * li
    cr = ((ar - 1.0) * lr + ai * li) / den
    ci = (ai * lr - (ar - 1.0) * li) / den
    br_, bi_ = b_re.astype(f32), b_im.astype(f32)
    bbr = cr[..., None] * br_ - ci[..., None] * bi_
    bbi = cr[..., None] * bi_ + ci[..., None] * br_
    xr = jnp.einsum('bsgp,gnp->bsgn', uf, bbr)
    xi = jnp.einsum('bsgp,gnp->bsgn', uf, bbi)
    ar_f = jnp.broadcast_to(ar, xr.shape)
    ai_f = jnp.broadcast_to(ai, xr.shape)

    def combine(e1, e2):
        a1r, a1i, x1r, x1i = e1
        a2r, a2i, x2r, x2i = e2
        return (a2r * a1r - a2i * a1i, a2r * a1i + a2i * a1r,
                a2r * x1r - a2i * x1i + x2r, a2r * x1i + a2i * x1r + x2i)

    _, _, sr, si = lax.associative_scan(combine, (ar_f, ai_f, xr, xi), axis=1)
    y = (jnp.einsum('bsgn,gpn->bsgp', sr, c_re.astype(f32))
         - jnp.einsum('bsgn,gpn->bsgp', si, c_im.astype(f32))
         + d_skip.astype(f32).reshape(S5_GROUPS, S5_GROUP_DIM) * uf)
    y = jax.nn.gelu(y.reshape(bsz, seq, S5_WIDTH))
    y = y * jax.nn.sigmoid(y @ w_glu.astype(f32) + b_glu.astype(f32))
    return y.astype(u.dtype)

def hgrn2_mixer(q_in, f_in, i_in, g_in, lb, norm_g):
    bsz, seq, _ = q_in.shape
    f32 = jnp.float32
    q = jax.nn.silu(q_in.astype(f32))
    lbf = lb.astype(f32)
    f = lbf + (1.0 - lbf) * jax.nn.sigmoid(f_in.astype(f32))
    logf = jnp.log(f)
    k = 1.0 - f
    v = i_in.astype(f32)
    qc, kc = to_chunks(q, HG_HEADS, HG_DK), to_chunks(k, HG_HEADS, HG_DK)
    vc, gc = to_chunks(v, HG_HEADS, HG_DV), to_chunks(logf, HG_HEADS, HG_DK)
    causal = jnp.tril(jnp.ones((CHUNK, CHUNK), dtype=bool))

    def step(state, xs):
        qb, kb, vb, gb = xs
        cum = jnp.cumsum(gb, axis=2)
        last = cum[:, :, -1:, :]
        inter = jnp.einsum('bhtk,bhkv->bhtv', qb * jnp.exp(cum), state)
        diff = cum[:, :, :, None, :] - cum[:, :, None, :, :]
        decay = jnp.exp(jnp.where(causal[:, :, None], diff, -jnp.inf))
        scores = jnp.einsum('bhtk,bhsk,bhtsk->bhts', qb, kb, decay)
        out = inter + jnp.einsum('bhts,bhsv->bhtv', scores, vb)
        new_state = (jnp.exp(last[:, :, 0, :])[..., None] * state
                     + jnp.einsum('bhsk,bhsv->bhkv', kb * jnp.exp(last - cum), vb))
        return new_state, out

    s0 = jnp.zeros((bsz, HG_HEADS, HG_DK, HG_DV), f32)
    _, o = lax.scan(step, s0, (qc, kc, vc, gc))
    o = rms_norm(from_chunks(o), norm_g.reshape(HG_HEADS, HG_DV))
    o = o.reshape(bsz, seq, HG_WIDTH) * jax.nn.silu(g_in.astype(f32))
    return o.astype(q_in.dtype)

def mlstm_mixer(cx, v_in, o_in, ig_in, fg_in, conv_w, conv_b, w_qk, b_ig, b_fg, norm_g):
    bsz, seq, _ = cx.shape
    f32 = jnp.float32
    ca = jax.nn.silu(causal_dwconv(cx, conv_w, conv_b)).reshape(bsz, seq, ML_HEADS, ML_DH)
    qk = jnp.einsum('bshd,hde->bshe', ca, w_qk.astype(ca.dtype)).astype(f32)
    q = qk[..., :ML_DH].reshape(bsz, seq, ML_WIDTH)
    k = (qk[..., ML_DH:] * (ML_DH ** -0.5)).reshape(bsz, seq, ML_WIDTH)
    v = v_in.astype(f32)
    ig = (ig_in + b_ig).astype(f32)
    lf = jax.nn.log_sigmoid((fg_in + b_fg).astype(f32))
    qc, kc, vc = to_chunks(q, ML_HEADS, ML_DH), to_chunks(k, ML_HEADS, ML_DH), to_chunks(v, ML_HEADS, ML_DH)
    nch = seq // CHUNK
    icc = ig.reshape(bsz, nch, CHUNK, ML_HEADS).transpose(1, 0, 3, 2)
    fcc = lf.reshape(bsz, nch, CHUNK, ML_HEADS).transpose(1, 0, 3, 2)
    causal = jnp.tril(jnp.ones((CHUNK, CHUNK), dtype=bool))

    def step(carry, xs):
        cmat, nvec, m = carry
        qb, kb, vb, ib, fb = xs
        bcum = jnp.cumsum(fb, axis=-1)
        dmat = jnp.where(causal, bcum[..., :, None] - bcum[..., None, :] + ib[..., None, :], -jnp.inf)
        inter_log = bcum + m[..., None]
        m_t = jnp.maximum(inter_log, jnp.max(dmat, axis=-1))
        w_inter = jnp.exp(inter_log - m_t)
        w_intra = jnp.exp(dmat - m_t[..., None]) * jnp.einsum('bhtd,bhsd->bhts', qb, kb)
        num = (w_inter[..., None] * jnp.einsum('bhtk,bhkv->bhtv', qb, cmat)
               + jnp.einsum('bhts,bhsv->bhtv', w_intra, vb))
        den = w_inter * jnp.einsum('bhtk,bhk->bht', qb, nvec) + jnp.sum(w_intra, axis=-1)
        h = num / jnp.maximum(jnp.abs(den), jnp.exp(-m_t))[..., None]
        m_new = m_t[..., -1]
        decay = jnp.exp(bcum[..., -1] + m - m_new)
        ws = jnp.exp(bcum[..., -1:] - bcum + ib - m_new[..., None])
        c_new = decay[..., None, None] * cmat + jnp.einsum('bhs,bhsk,bhsv->bhkv', ws, kb, vb)
        n_new = decay[..., None] * nvec + jnp.einsum('bhs,bhsk->bhk', ws, kb)
        return (c_new, n_new, m_new), h

    init = (jnp.zeros((bsz, ML_HEADS, ML_DH, ML_DH), f32),
            jnp.zeros((bsz, ML_HEADS, ML_DH), f32),
            jnp.zeros((bsz, ML_HEADS), f32))
    _, h = lax.scan(step, init, (qc, kc, vc, icc, fcc))
    h = rms_norm(from_chunks(h), norm_g.reshape(ML_HEADS, ML_DH))
    h = h.reshape(bsz, seq, ML_WIDTH) * jax.nn.sigmoid(o_in.astype(f32))
    return h.astype(cx.dtype)

def conv_ffn(h, w_up, conv_w, conv_b, w_down):
    up = causal_dwconv(h @ w_up, conv_w, conv_b)
    a, b = up[..., :FFN_DIM], up[..., FFN_DIM:]
    return (jax.nn.silu(a) * b) @ w_down

def first_inputs(seed: int = 0) -> dict:
    key = jax.random.key(seed)
    ks = jax.random.split(key, 32)
    f32 = jnp.float32
    L, G, N, P = DEPTH, S5_GROUPS, S5_STATE, S5_GROUP_DIM

    def nrm(k, shape, scale):
        return scale * jax.random.normal(k, shape, f32)

    n_idx = jnp.arange(N, dtype=f32)
    return {
        'x': nrm(ks[0], (BATCH, SEQ, D_MODEL), 1.0),
        'mix_norm': 1.0 + nrm(ks[1], (L, D_MODEL), 0.02),
        'w_in': nrm(ks[2], (L, D_MODEL, IN_TOTAL), D_MODEL ** -0.5),
        's5_lam_re': -0.5 + nrm(ks[3], (L, G, N), 0.01),
        's5_lam_im': math.pi * n_idx + nrm(ks[4], (L, G, N), 0.01),
        's5_log_dt': jax.random.uniform(ks[5], (L, G), f32, math.log(S5_DT_MIN), math.log(S5_DT_MAX)),
        's5_b_re': nrm(ks[6], (L, G, N, P), (2 * P) ** -0.5),
        's5_b_im': nrm(ks[7], (L, G, N, P), (2 * P) ** -0.5),
        's5_c_re': nrm(ks[8], (L, G, P, N), N ** -0.5),
        's5_c_im': nrm(ks[9], (L, G, P, N), N ** -0.5),
        's5_d': nrm(ks[10], (L, S5_WIDTH), 1.0),
        's5_w_glu': nrm(ks[11], (L, S5_WIDTH, S5_WIDTH), S5_WIDTH ** -0.5),
        's5_b_glu': nrm(ks[12], (L, S5_WIDTH), 0.02),
        'hg_lower_bounds': nrm(ks[13], (L, HG_KEY_WIDTH), 1.0),
        'hg_norm': 1.0 + nrm(ks[14], (L, HG_WIDTH), 0.02),
        'ml_conv_w': nrm(ks[15], (L, ML_CONV, ML_WIDTH), 0.5),
        'ml_conv_b': nrm(ks[16], (L, ML_WIDTH), 0.02),
        'ml_w_qk': nrm(ks[17], (L, ML_HEADS, ML_DH, 2 * ML_DH), ML_DH ** -0.5),
        'ml_b_ig': nrm(ks[18], (L, ML_HEADS), 0.1),
        'ml_b_fg': jnp.linspace(3.0, 6.0, ML_HEADS, dtype=f32)[None, :] + nrm(ks[19], (L, ML_HEADS), 0.01),
        'ml_norm': 1.0 + nrm(ks[20], (L, ML_WIDTH), 0.02),
        'w_branch': nrm(ks[21], (L, MIX_WIDTH, D_MODEL), (MIX_WIDTH / N_BRANCH) ** -0.5),
        'w_out': nrm(ks[22], (L, D_MODEL, D_MODEL), D_MODEL ** -0.5),
        'ffn_norm': 1.0 + nrm(ks[23], (L, D_MODEL), 0.02),
        'ffn_w_up': nrm(ks[24], (L, D_MODEL, 2 * FFN_DIM), D_MODEL ** -0.5),
        'ffn_conv_w': nrm(ks[25], (L, FFN_CONV, 2 * FFN_DIM), FFN_CONV ** -0.5),
        'ffn_conv_b': nrm(ks[26], (L, 2 * FFN_DIM), 0.02),
        'ffn_w_down': nrm(ks[27], (L, FFN_DIM, D_MODEL), FFN_DIM ** -0.5),
        'final_norm': 1.0 + nrm(ks[28], (D_MODEL,), 0.02),
    }

def first_block(x, mix_norm, w_in, s5_lam_re, s5_lam_im, s5_log_dt, s5_b_re, s5_b_im, s5_c_re, s5_c_im,
              s5_d, s5_w_glu, s5_b_glu, hg_lower_bounds, hg_norm, ml_conv_w, ml_conv_b, ml_w_qk,
              ml_b_ig, ml_b_fg, ml_norm, w_branch, w_out, ffn_norm, ffn_w_up, ffn_conv_w, ffn_conv_b,
              ffn_w_down, final_norm):
    lbs = jax.nn.softmax(hg_lower_bounds.astype(jnp.float32), axis=0)
    lbs = jnp.cumsum(lbs, axis=0) - lbs[0:1]
    splits = _split_points()
    r_a, r_b = S5_WIDTH, S5_WIDTH + HG_WIDTH
    for l in range(DEPTH):
        h = rms_norm(x, mix_norm[l])
        (u_a, q_b, f_b, i_b, og_b, cx_c, v_c, o_c, ig_c, fg_c, gates) = jnp.split(h @ w_in[l], splits, axis=-1)
        y_a = s5_mixer(u_a, s5_lam_re[l], s5_lam_im[l], s5_log_dt[l], s5_b_re[l], s5_b_im[l],
                       s5_c_re[l], s5_c_im[l], s5_d[l], s5_w_glu[l], s5_b_glu[l])
        y_b = hgrn2_mixer(q_b, f_b, i_b, og_b, lbs[l], hg_norm[l])
        y_c = mlstm_mixer(cx_c, v_c, o_c, ig_c, fg_c, ml_conv_w[l], ml_conv_b[l], ml_w_qk[l],
                          ml_b_ig[l], ml_b_fg[l], ml_norm[l])
        wb = w_branch[l]
        g_a, g_b, g_c = (gates[..., :D_MODEL], gates[..., D_MODEL:2 * D_MODEL], gates[..., 2 * D_MODEL:])
        merged = (jax.nn.sigmoid(g_a) * (y_a @ wb[:r_a])
                  + jax.nn.sigmoid(g_b) * (y_b @ wb[r_a:r_b])
                  + jax.nn.sigmoid(g_c) * (y_c @ wb[r_b:]))
        x = x + merged @ w_out[l]
        x = x + conv_ffn(rms_norm(x, ffn_norm[l]), ffn_w_up[l], ffn_conv_w[l], ffn_conv_b[l], ffn_w_down[l])
    return rms_norm(x, final_norm)


_first_inputs = first_inputs


def first_inputs(seed=0):
    import zlib

    import numpy as np

    out = dict(_first_inputs(seed))
    spreads = {}
    factors = {'mix_norm': 3.129,
     's5_lam_re': 64.0,
     's5_lam_im': 30.752,
     's5_log_dt': 32.408,
     's5_b_re': 44.208,
     's5_b_im': 44.712,
     's5_c_re': 43.576,
     's5_c_im': 43.92,
     's5_b_glu': 64.0,
     'hg_norm': 8.0,
     'ml_conv_b': 3.147,
     'ml_b_ig': 64.0,
     'ml_norm': 64.0,
     'ffn_norm': 11.756,
     'ffn_conv_b': 11.839,
     'final_norm': 7.458}
    for name, (base, spread) in spreads.items():
        noise = np.random.default_rng([zlib.crc32(name.encode()), seed]).standard_normal(out[name].shape)
        drawn = base * np.exp(spread * noise) if base else spread * noise
        out[name] = __import__('jax').numpy.asarray(drawn.astype(out[name].dtype))
    for name, factor in factors.items():
        out[name] = (out[name] * factor).astype(out[name].dtype)
    return out


_narrow_inputs = first_inputs


def first_inputs(seed=0):
    out = dict(_narrow_inputs(seed))
    wider = {'s5_w_glu': 3.14, 's5_b_glu': 5.24, 'hg_norm': 5.31, 'final_norm': 3.08}
    for name, times in wider.items():
        mean = out[name].mean()
        out[name] = (mean + times * (out[name] - mean)).astype(out[name].dtype)
    return out


Q_BLOCK = 128
D_PLE = 256

POOL_WIDTH = D_MODEL // 2
POOL_WINDOWS = (2, 4, 8, 16)
POOL_GROUPS = len(POOL_WINDOWS)
POOL_GROUP_WIDTH = POOL_WIDTH // POOL_GROUPS

V_HEAD = 128
MLA_HEADS = (D_MODEL // 2) // V_HEAD
MLA_WIDTH = MLA_HEADS * V_HEAD
QK_NOPE = 128
QK_ROPE = 64
QK_HEAD = QK_NOPE + QK_ROPE
Q_LORA = 512
KV_LORA = 512
ROPE_THETA = 10000.0

MIX_WIDTH_2 = POOL_WIDTH + MLA_WIDTH
IN_COLS = POOL_WIDTH + Q_LORA + KV_LORA + QK_ROPE

PEER_HEADS = 8
PEER_NKEYS = 128
PEER_EXPERTS = PEER_NKEYS * PEER_NKEYS
PEER_DKEY = 256
PEER_HALF = PEER_DKEY // 2
PEER_TOPK = 16
PEER_TOK_BLOCK = 128


def rms_norm_2(x, g):
    xf = x.astype(jnp.float32)
    y = xf * lax.rsqrt(jnp.mean(xf * xf, axis=-1, keepdims=True) + EPS)
    return (y * g.astype(jnp.float32)).astype(x.dtype)

def apply_rope(x, cos, sin):
    half = QK_ROPE // 2
    xf = x.astype(jnp.float32)
    x1, x2 = xf[..., :half], xf[..., half:]
    return jnp.concatenate([x1 * cos - x2 * sin, x2 * cos + x1 * sin], axis=-1).astype(x.dtype)

def pool_mixer(xp, w_pool, pool_scale):
    B, S, _ = xp.shape
    xf = xp.reshape(B, S, POOL_GROUPS, POOL_GROUP_WIDTH).astype(jnp.float32)
    cs = jnp.cumsum(xf, axis=1)
    t = jnp.arange(S)
    outs = []
    for g, w in enumerate(POOL_WINDOWS):
        csg = cs[:, :, g]
        lower = jnp.pad(csg, ((0, 0), (w, 0), (0, 0)))[:, :S]
        cnt = jnp.minimum(t + 1, w).astype(jnp.float32)[None, :, None]
        outs.append((csg - lower) / cnt - xf[:, :, g])
    d = jnp.stack(outs, axis=2).astype(xp.dtype)
    y = jnp.einsum('bsgc,gcd->bsgd', d, w_pool)
    return y.reshape(B, S, POOL_WIDTH) * pool_scale

def mla(c_q, c_kv, k_rope, positions, q_lat_gain, kv_lat_gain, w_uq, w_ukv, q_norm_gain, k_norm_gain):
    B, S, _ = c_q.shape
    q = (rms_norm_2(c_q, q_lat_gain) @ w_uq).reshape(B, S, MLA_HEADS, QK_HEAD)
    kv = (rms_norm_2(c_kv, kv_lat_gain) @ w_ukv).reshape(B, S, MLA_HEADS, QK_NOPE + V_HEAD)
    k_nope, v = kv[..., :QK_NOPE], kv[..., QK_NOPE:]
    k = jnp.concatenate([k_nope, jnp.broadcast_to(k_rope[:, :, None, :], (B, S, MLA_HEADS, QK_ROPE))], axis=-1)
    q = rms_norm_2(q, q_norm_gain)
    k = rms_norm_2(k, k_norm_gain)
    inv_freq = ROPE_THETA ** (-jnp.arange(0, QK_ROPE, 2, dtype=jnp.float32) / QK_ROPE)
    ang = positions.astype(jnp.float32)[:, :, None] * inv_freq
    cos, sin = jnp.cos(ang)[:, :, None, :], jnp.sin(ang)[:, :, None, :]
    q = jnp.concatenate([q[..., :QK_NOPE], apply_rope(q[..., QK_NOPE:], cos, sin)], axis=-1)
    k = jnp.concatenate([k[..., :QK_NOPE], apply_rope(k[..., QK_NOPE:], cos, sin)], axis=-1)

    nb = S // Q_BLOCK
    qb = q.reshape(B, nb, Q_BLOCK, MLA_HEADS, QK_HEAD).transpose(1, 0, 2, 3, 4)
    k_chunk = jnp.arange(S) // CHUNK
    scale = QK_HEAD ** -0.5

    def attend(args):
        q_blk, blk = args
        q_chunk = (blk * Q_BLOCK + jnp.arange(Q_BLOCK)) // CHUNK
        s = jnp.einsum('bqhd,bkhd->bhqk', q_blk, k, preferred_element_type=jnp.float32) * scale
        s = jnp.where(k_chunk[None, :] <= q_chunk[:, None], s, -jnp.inf)
        pr = jax.nn.softmax(s, axis=-1).astype(v.dtype)
        return jnp.einsum('bhqk,bkhd->bqhd', pr, v)

    o = lax.map(attend, (qb, jnp.arange(nb)))
    return o.transpose(1, 0, 2, 3, 4).reshape(B, S, MLA_WIDTH)

def peer(xn, w_pq, sub_k1, sub_k2, expert_u, expert_v):
    B, S, D = xn.shape
    q = (xn @ w_pq).reshape(B, S, PEER_HEADS, 2, PEER_HALF)
    s1 = jnp.einsum('bshd,hnd->bshn', q[..., 0, :], sub_k1, preferred_element_type=jnp.float32)
    s2 = jnp.einsum('bshd,hnd->bshn', q[..., 1, :], sub_k2, preferred_element_type=jnp.float32)
    v1, i1 = lax.top_k(s1, PEER_TOPK)
    v2, i2 = lax.top_k(s2, PEER_TOPK)
    cand = (v1[..., :, None] + v2[..., None, :]).reshape(B, S, PEER_HEADS, PEER_TOPK * PEER_TOPK)
    vs, ci = lax.top_k(cand, PEER_TOPK)
    e1 = jnp.take_along_axis(i1, ci // PEER_TOPK, axis=-1)
    e2 = jnp.take_along_axis(i2, ci % PEER_TOPK, axis=-1)
    eidx = e1 * PEER_NKEYS + e2
    gates = jax.nn.softmax(vs, axis=-1).astype(xn.dtype)

    T = B * S
    nblk = T // PEER_TOK_BLOCK
    kk = PEER_HEADS * PEER_TOPK
    xt = xn.reshape(nblk, PEER_TOK_BLOCK, D)
    it = eidx.reshape(nblk, PEER_TOK_BLOCK, kk)
    gt = gates.reshape(nblk, PEER_TOK_BLOCK, kk)

    def block(args):
        xb, ib, gb = args
        act = jax.nn.gelu(jnp.einsum('tkd,td->tk', expert_u[ib], xb))
        return jnp.einsum('tk,tkd->td', act * gb, expert_v[ib])

    return lax.map(block, (xt, it, gt)).reshape(B, S, D)

def second_inputs(seed: int = 0) -> dict:
    key = jax.random.key(seed)
    ks = jax.random.split(key, 24)
    f32 = jnp.float32

    def nrm(k, shape, scale):
        return jax.random.normal(k, shape, f32) * scale

    def gain(k, n):
        return 1.0 + 0.02 * jax.random.normal(k, (DEPTH, n), f32)

    x = jax.random.normal(ks[0], (BATCH, SEQ, D_MODEL), f32)
    p = jax.random.normal(ks[1], (DEPTH, BATCH, SEQ, D_PLE), f32)
    offs = jax.random.randint(ks[2], (BATCH, 1), 0, 4096, dtype=jnp.int32)
    positions = offs + jnp.arange(SEQ, dtype=jnp.int32)[None, :]
    return {
        "x": x,
        "p": p,
        "positions": positions,
        "mix_norm_gain": gain(ks[3], D_MODEL),
        "w_in": nrm(ks[4], (DEPTH, D_MODEL, IN_COLS), D_MODEL ** -0.5),
        "w_pool": nrm(ks[5], (DEPTH, POOL_GROUPS, POOL_GROUP_WIDTH, POOL_GROUP_WIDTH), POOL_GROUP_WIDTH ** -0.5),
        "pool_scale": 1.0 + 0.1 * jax.random.normal(ks[6], (DEPTH, POOL_WIDTH), f32),
        "q_lat_gain": gain(ks[7], Q_LORA),
        "kv_lat_gain": gain(ks[8], KV_LORA),
        "w_uq": nrm(ks[9], (DEPTH, Q_LORA, MLA_HEADS * QK_HEAD), Q_LORA ** -0.5),
        "w_ukv": nrm(ks[10], (DEPTH, KV_LORA, MLA_HEADS * (QK_NOPE + V_HEAD)), KV_LORA ** -0.5),
        "q_norm_gain": gain(ks[11], QK_HEAD),
        "k_norm_gain": gain(ks[12], QK_HEAD),
        "w_out": nrm(ks[13], (DEPTH, MIX_WIDTH_2, D_MODEL), MIX_WIDTH_2 ** -0.5),
        "ffn_norm_gain": gain(ks[14], D_MODEL),
        "w_pq": nrm(ks[15], (DEPTH, D_MODEL, PEER_HEADS * PEER_DKEY), D_MODEL ** -0.5),
        "sub_k1": nrm(ks[16], (DEPTH, PEER_HEADS, PEER_NKEYS, PEER_HALF), PEER_HALF ** -0.5),
        "sub_k2": nrm(ks[17], (DEPTH, PEER_HEADS, PEER_NKEYS, PEER_HALF), PEER_HALF ** -0.5),
        "expert_u": nrm(ks[18], (DEPTH, PEER_EXPERTS, D_MODEL), D_MODEL ** -0.5),
        "expert_v": nrm(ks[19], (DEPTH, PEER_EXPERTS, D_MODEL), PEER_HEADS ** -0.5),
        "ple_norm_gain": gain(ks[20], D_MODEL),
        "w_ple_gate": nrm(ks[21], (DEPTH, D_MODEL, D_MODEL), D_MODEL ** -0.5),
        "w_ple_proj": nrm(ks[22], (DEPTH, D_PLE, D_MODEL), D_PLE ** -0.5),
    }

def second_block(x, p, positions, mix_norm_gain, w_in, w_pool, pool_scale, q_lat_gain, kv_lat_gain,
              w_uq, w_ukv, q_norm_gain, k_norm_gain, w_out, ffn_norm_gain, w_pq, sub_k1, sub_k2,
              expert_u, expert_v, ple_norm_gain, w_ple_gate, w_ple_proj):
    h = x
    c0 = POOL_WIDTH
    c1 = c0 + Q_LORA
    c2 = c1 + KV_LORA
    for i in range(DEPTH):
        z = rms_norm_2(h, mix_norm_gain[i]) @ w_in[i]
        y_pool = pool_mixer(z[..., :c0], w_pool[i], pool_scale[i])
        y_mla = mla(z[..., c0:c1], z[..., c1:c2], z[..., c2:], positions,
                    q_lat_gain[i], kv_lat_gain[i], w_uq[i], w_ukv[i], q_norm_gain[i], k_norm_gain[i])
        h = h + jnp.concatenate([y_pool, y_mla], axis=-1) @ w_out[i]
        h = h + peer(rms_norm_2(h, ffn_norm_gain[i]), w_pq[i], sub_k1[i], sub_k2[i], expert_u[i], expert_v[i])
        gate = jax.nn.sigmoid(rms_norm_2(h, ple_norm_gain[i]) @ w_ple_gate[i])
        h = h + gate * (p[i] @ w_ple_proj[i])
    return h


def setup_inputs(seed=0):
    out = dict(first_inputs(seed))
    for name, value in second_inputs(seed + 1).items():
        if name != "x":
            out[name + "_2"] = value
    return out


def reference(
    x, mix_norm, w_in, s5_lam_re, s5_lam_im, s5_log_dt, s5_b_re, s5_b_im, s5_c_re, s5_c_im,
    s5_d, s5_w_glu, s5_b_glu, hg_lower_bounds, hg_norm, ml_conv_w, ml_conv_b, ml_w_qk, ml_b_ig,
    ml_b_fg, ml_norm, w_branch, w_out, ffn_norm, ffn_w_up, ffn_conv_w, ffn_conv_b, ffn_w_down,
    final_norm, p_2, positions_2, mix_norm_gain_2, w_in_2, w_pool_2, pool_scale_2, q_lat_gain_2,
    kv_lat_gain_2, w_uq_2, w_ukv_2, q_norm_gain_2, k_norm_gain_2, w_out_2, ffn_norm_gain_2,
    w_pq_2, sub_k1_2, sub_k2_2, expert_u_2, expert_v_2, ple_norm_gain_2, w_ple_gate_2,
    w_ple_proj_2,
):
    x = first_block(
        x, mix_norm, w_in, s5_lam_re, s5_lam_im, s5_log_dt, s5_b_re, s5_b_im, s5_c_re, s5_c_im,
        s5_d, s5_w_glu, s5_b_glu, hg_lower_bounds, hg_norm, ml_conv_w, ml_conv_b, ml_w_qk,
        ml_b_ig, ml_b_fg, ml_norm, w_branch, w_out, ffn_norm, ffn_w_up, ffn_conv_w, ffn_conv_b,
        ffn_w_down, final_norm,
    )
    return second_block(
        x, p_2, positions_2, mix_norm_gain_2, w_in_2, w_pool_2, pool_scale_2, q_lat_gain_2,
        kv_lat_gain_2, w_uq_2, w_ukv_2, q_norm_gain_2, k_norm_gain_2, w_out_2, ffn_norm_gain_2,
        w_pq_2, sub_k1_2, sub_k2_2, expert_u_2, expert_v_2, ple_norm_gain_2, w_ple_gate_2,
        w_ple_proj_2,
    )


_drawn_inputs = setup_inputs


def setup_inputs(seed=0):
    import zlib

    import numpy as np

    out = dict(_drawn_inputs(seed))
    spreads = {}
    factors = {'mix_norm_gain_2': 8.0,
     'pool_scale_2': 7.062,
     'q_lat_gain_2': 8.0,
     'kv_lat_gain_2': 8.0,
     'w_uq_2': 4.839,
     'w_ukv_2': 3.541,
     'q_norm_gain_2': 8.0,
     'k_norm_gain_2': 8.0,
     'ffn_norm_gain_2': 8.0,
     'expert_u_2': 2.759,
     'ple_norm_gain_2': 64.0,
     'p_2': 3.546,
     'w_ple_gate_2': 5.296,
     'w_ple_proj_2': 3.546}
    for name, (base, spread) in spreads.items():
        noise = np.random.default_rng([zlib.crc32(name.encode()), seed]).standard_normal(out[name].shape)
        drawn = base * np.exp(spread * noise) if base else spread * noise
        out[name] = __import__('jax').numpy.asarray(drawn.astype(out[name].dtype))
    for name, factor in factors.items():
        out[name] = (out[name] * factor).astype(out[name].dtype)
    return out
```

```python
from contextlib import ExitStack

import numpy as np

import concourse.bass as bass
from concourse import mybir

F32 = mybir.dt.float32
I32 = mybir.dt.int32
U32 = mybir.dt.uint32
ALU = mybir.AluOpType
ACT = mybir.ActivationFunctionType
AX = mybir.AxisListType

P = 128
T = 256
D = 2048
KD = D // P
EPS = 1e-6
SLOTS = 4
BANK = 512
S5_TILES = 16
HG = 6
MH, MD = 4, 192
FT = 44
AH = 8
PH = 8
TOPK = 16
NK = 128
NEG = -1e30
TWO_PI = 2 * np.pi
PI_A = 6.28125
PI_B = float(np.float32(np.round((TWO_PI - PI_A) * 2 ** 21) / 2 ** 21))
PI_C = float(np.float32(TWO_PI - PI_A - PI_B))
ROUND = 1.5 * 2 ** 23

PANELS = {}
_n = 0
for _name, _k in (("u", 4), ("s5", 1), ("q", 6), ("f", 6), ("i", 6), ("og", 6), ("glu", 1), ("cx", 6),
                  ("v", 6), ("o", 6), ("if", 1), ("ga", 8), ("qk", 2), ("ga2", 8), ("gb", 16), ("merge", 32),
                  ("wout", 16), ("up", 2 * FT), ("down", FT), ("in2", 17), ("pool", 1), ("uq", 2),
                  ("uqr", 1), ("ukn", 2), ("ukv", 2), ("wout2", 16), ("pq", 16), ("subk", 1),
                  ("eu", NK), ("ev", NK), ("pp", 2), ("pg", 16)):
    PANELS[_name] = _n
    _n += _k
NPANELS = _n

COL = {}
_n = 0
for _name, _k in (("mix", 16), ("ffn", 16), ("final", 16), ("mix2", 16), ("ffn2", 16), ("ple", 16),
                  ("lam_re", 16), ("lam_im", 16), ("log_dt", 16), ("s5_d", 4), ("b_glu", 4),
                  ("hg_lb", 6), ("hg_norm", 6), ("conv_w", 24), ("conv_b", 6), ("ml_norm", 6),
                  ("b_ig", 1), ("b_fg", 1), ("fconv", 8 * FT), ("pool_scale", 8), ("q_lat", 4),
                  ("kv_lat", 4), ("qn_n", 1), ("qn_r", 1), ("kn_n", 1), ("kn_r", 1)):
    COL[_name] = _n
    _n += _k
NCOL = _n

CC = {}
_n = 0
for _name, _k in (("ident", P), ("ones", P), ("iota", P), ("invfreq", 1), ("perm", 64)):
    CC[_name] = _n
    _n += _k
NCONST = _n
MC = {}
_n = 0
for _name, _k in (("hgmask", 8 * P), ("causal", P), ("sel", MH * P), ("tidx", T), ("chunkmask", 3 * P),
                  ("invcnt", 4 * T)):
    MC[_name] = _n
    _n += _k
NMIX = _n
ARENA = 35392

OUT = {}
_n = 0
for _name, _k in (("z", 79), ("gc", 16), ("wout", 16), ("up", 2 * FT), ("in2", 17), ("wout2", 16),
                  ("pq", 16), ("eu", NK), ("pg", 16)):
    OUT[_name] = _n
    _n += _k


def head_parts(h):
    c, out = h * MD, []
    while c < (h + 1) * MD:
        n = min(P - c % P, (h + 1) * MD - c)
        out.append((c // P, c % P, n, c - h * MD))
        c += n
    return out


class Count:

    def __init__(self, eng, sem):
        self.eng, self.sem, self.base, self.i, self.per, self.k = eng, sem, 0, None, 0, 0

    def value(self):
        return self.base + self.k if self.i is None else self.i * self.per + (self.base + self.k)

    def mark(self, ins):
        ins.then_inc(self.sem, 1)
        self.k += 1

    def link(self, ins):
        self.mark(ins)
        self.eng.wait_ge(self.sem, self.value())

    def enter(self, i, per):
        self.base, self.k, self.i, self.per = self.base + self.k, 0, i, per

    def leave(self, times):
        assert self.k == self.per, (self.k, self.per)
        self.base, self.k, self.i = self.base + times * self.per, 0, None


def two_blocks_kernel(nc, xT, stream, params, consts, mixc, pT, pos, outT):
    ctx = ExitStack()
    with ctx:
        def sem(name):
            return ctx.enter_context(nc.semaphore(name))


        def sb(name, shape, dt=F32):
            return ctx.enter_context(nc.sbuf_tensor(name, shape, dt))

        ring = sb("ring", [P, SLOTS, D])
        res = sb("res", [P, KD * T])
        hn = sb("hn", [P, KD * T])
        par = sb("par", [P, NCOL])
        con = sb("con", [P, NCONST])
        rstd = sb("rstd", [P, T])
        cols = sb("cols", [P, 64])
        arena = sb("arena", [P, ARENA])
        ps = ctx.enter_context(nc.psum_tensor("ps", [P, 8, BANK], F32))

        def area(at, n, parts=P):
            assert at + n <= ARENA, (at, n)
            return arena[0:parts, at:at + n]

        Y0, W0 = 79 * T, 95 * T
        W1 = W0 + NMIX
        z = area(0, 79 * T)
        y = area(Y0, 16 * T)
        mixcon = area(W0, NMIX)

        def zt(k, n=1):
            return z[:, k * T:(k + n) * T]

        def yt(k, n=1):
            return y[:, k * T:(k + n) * T]

        def pc(name, k=0, n=1):
            return par[:, COL[name] + k:COL[name] + k + n]

        def mc(name, n, k=0, parts=P):
            return mixcon[0:parts, MC[name] + k:MC[name] + k + n]

        ident, ones, iota = (con[:, CC[c]:CC[c] + P] for c in ("ident", "ones", "iota"))
        ZU, ZQ, ZF, ZI, ZG, ZC, ZV, ZO, ZIF, ZGA, ZGB = 0, 4, 10, 16, 22, 28, 34, 40, 46, 47, 63

        G4 = 4 * T
        s5s = area(W1, 16 * 16)
        s5b = area(W1 + 256, 1024)
        s5c = area(W1 + 1280, 1024)
        s5w = [area(W1 + 2304 + k * G4, G4) for k in range(5)]
        s5re, s5im, s5sin, s5cos, s5tmp = s5w
        hk = zt(ZF, HG)
        hcum = area(W1, HG * T)
        hd = area(W1 + 1536, 8 * T)
        heq = area(W1 + 3584, 8 * T)
        hmk = area(W1 + 5632, 8 * P)
        hvt = area(W1 + 6656, T)
        hms = area(W1 + 6912, 3 * P)
        mca = area(W1, HG * T)
        mvt = area(W1 + 1536, 2 * HG * P)
        mrow = area(W1 + 3072, 6 * T, 4)
        macol = area(W1 + 4608, 2 * MH)
        mx = area(W1 + 4616, 3 * P)
        mp = area(W1 + 5000, 3 * P)
        men = area(W1 + 5384, T)
        mden = area(W1 + 5640, T)
        merged = area(4 * T, KD * T)
        mg = [area(W1 + k * T, T) for k in range(6)]
        gff = area(0, FT * T)
        fa, fb = area(FT * T, T), area(FT * T + T, T)
        at2 = 17 * T
        qn, kn, qrope, krope, rq, sq, vtm = (area(at2 + k * 2048, 2048) for k in range(7))
        rope = [area(at2 + 14336 + k * T, T, 64) for k in range(5)]
        posi = area(at2 + 14336 + 5 * T, T, 64).bitcast(I32)
        pb = [area(W1 + k * 2048, 2048) for k in range(3)]
        vsq = pb[0]
        sc = [area(W1 + k * 384, 384) for k in range(2)]
        pt = [area(W1 + 768 + k * 384, 384) for k in range(2)]
        sm = area(W1 + 1600, 8 * AH)
        A = area(0, NK * T)
        q2 = area(0, 16 * T)
        SCR = NK // 2 * T
        s12 = area(SCR, 2 * 16 * NK)
        cand = area(SCR + 4096, 2 * PH * 256)
        eqt = area(SCR + 8192, 2048)
        val = area(SCR + 10240, 512)
        vidx = area(SCR + 10752, 512).bitcast(U32)
        vidf = area(SCR + 11264, 512)
        cval = area(SCR + 11776, 256)
        cidx = area(SCR + 12032, 256).bitcast(U32)
        cdu = [area(SCR + 12288 + 256 * k, 256).bitcast(U32) for k in range(2)]
        cdf = [area(SCR + 12800 + 256 * k, 256) for k in range(2)]
        etm = area(SCR + 13312, 3 * T)
        gsum = area(SCR + 14080, 16)
        TAIL = NK * T
        et = area(TAIL, 3 * T)
        oh1 = area(TAIL + 768, 4 * P)
        oh2 = area(TAIL + 1280, 8 * P)
        pTs = area(TAIL + 1792, 2 * T)
        ppj = area(0, KD * T)
        gt = area(4096, 4 * T)

        x_in, par_in, con_in, mix_in, pos_in, p_in, out_st = (sem(s) for s in (
            "x_in", "par_in", "con_in", "mix_in", "pos_in", "p_in", "out_st"))
        landed = [sem(f"landed{s}") for s in range(SLOTS)]
        panel_done = sem("panel_done")
        evac_done = sem("evac_done")
        rms_sq, rms_ss, rms_ms, rms_rt, rms_out = (sem(s) for s in (
            "rms_sq", "rms_ss", "rms_ms", "rms_rt", "rms_out"))
        dve_step, act_step, pool_step = sem("dve_step"), sem("act_step"), sem("pool_step")
        S = {k: sem(k) for k in (
            "s5_ldt", "s5_dt", "s5_mi", "s5_ma", "s5_bcopied", "s5_angle", "s5_sin", "s5_bu", "s5_state", "s5_y",
            "s5_pre", "s5_gelu", "s5_glu", "s5_sig", "ya_done",
            "hg_lbx", "hg_lbe", "hg_sig", "hg_silu", "hg_f", "hg_ln", "hg_exp", "hg_decay", "hg_eq", "hg_ek",
            "hg_sc", "hg_masked", "hg_vt", "hg_vtc", "hg_o", "hg_oc", "hg_sq", "hg_ss", "hg_ms", "hg_rt",
            "yb_done", "ml_conv", "ml_ca", "ml_qk", "ml_qkc", "ml_ax", "ml_e", "ml_e1", "ml_ln", "ml_rows",
            "ml_at", "ml_atc", "ml_vt", "ml_vtc", "ml_bc", "ml_x", "ml_w", "ml_sc", "ml_p", "ml_nd", "ml_h",
            "ml_sq", "ml_ss", "ml_ms", "ml_rt", "ml_og", "yc_done", "sig_ab", "branch_read", "merged_done",
            "ff_silu", "ff_out", "res_done",
            "po_d", "po_y", "po_yc", "rp_angle", "rp_sin", "at_q", "at_qc", "at_sq", "at_ss", "at_ms", "at_rt",
            "at_qn", "at_rot", "at_rotc", "at_done", "at_s", "at_mx", "at_e", "at_p", "at_t", "at_tc", "at_o", "at_oc",
            "pk_s", "pk_sc", "pk_g", "pk_e", "pk_et", "pk_t", "pk_tc", "oh1_done", "oh2_done", "oh2_turn", "tok_mm", "tok_ev",
            "pp_out", "pp_ev", "out_ready")}

        block = ctx.enter_context(nc.Block())

        @block.sync
        def _(sp):
            sp.dma_start(par[:], params).then_inc(par_in, 16)
            sp.dma_start(con[:], consts).then_inc(con_in, 16)
            sp.dma_start(res[:], xT).then_inc(x_in, 16)
            for s in range(SLOTS):
                sp.dma_start(ring[:, s, :], stream[s]).then_inc(landed[s], 16)
            sp.dma_start(mixcon, mixc).then_inc(mix_in, 16)
            with sp.Fori(1, NPANELS // SLOTS) as r:
                for s in range(SLOTS):
                    sp.wait_ge(panel_done, r * SLOTS + (s - 3))
                    sp.dma_start(ring[:, s, :], stream[bass.ds(r * SLOTS + s, 1)].rearrange("a p n -> p (a n)")) \
                        .then_inc(landed[s], 16)
            for n in range(NPANELS // SLOTS * SLOTS, NPANELS):
                sp.wait_ge(panel_done, n - 3)
                sp.dma_start(ring[:, n % SLOTS, :], stream[n]).then_inc(landed[n % SLOTS], 16)
            for q in range(4):
                sp.wait_ge(S["out_ready"], 4 * q + 4)
                sp.dma_start(outT[:, q * 4 * T:(q + 1) * 4 * T], res[:, q * 4 * T:(q + 1) * 4 * T]).then_inc(out_st, 16)
            sp.wait_ge(out_st, 64)

        @block.tensor
        def _(pe):
            def arrive(n, i=None, per=0):
                v = 16 * (n // SLOTS + 1)
                pe.wait_ge(landed[n % SLOTS], v if i is None else i * (16 * per // SLOTS) + v)

            def slot(n, k, m=P, rows=slice(0, P)):
                return ring[rows, n % SLOTS, k * P:k * P + m]

            def project(n, p, src, i=None, pern=0, perp=0):
                arrive(n, i, pern)
                if i is not None:
                    pe.wait_ge(evac_done, i * perp + (p - 3))
                elif p >= 4:
                    pe.wait_ge(evac_done, p - 3)
                for k in range(KD):
                    mm = pe.matmul(ps[:, p % 4, 0:T], slot(n, k), src[:, k * T:(k + 1) * T],
                                   start=(k == 0), stop=(k == KD - 1))
                mm.then_inc(panel_done, 1)

            def project_loop(n, p, count, src):
                done = 4 if p == 0 else 0
                turns = (count - done) // 4
                for j in range(done):
                    project(n + j, p + j, src)
                if turns > 1:
                    with pe.Fori(0, turns) as i:
                        for j in range(done, done + 4):
                            project(n + j, p + j, src, i, 4, 4)
                    done += 4 * turns
                for j in range(done, count):
                    project(n + j, p + j, src)

            def sum_squares(r, sq, tiles, bank=4):
                for k in range(tiles):
                    if k % (tiles // 4) == 0:
                        pe.wait_ge(rms_sq, 4 * r + k // (tiles // 4) + 1)
                    mm = pe.matmul(ps[:, bank, 0:T], ones, sq[:, k * T:(k + 1) * T], start=(k == 0), stop=(k == tiles - 1))
                mm.then_inc(rms_ss, 1)

            def accumulate_all(n, count, src):
                def one(n, rhs, i=None, first=False, end=False):
                    arrive(n, i, 4)
                    for m in range(KD):
                        mm = pe.matmul(ps[:, m // 2, (m % 2) * T:(m % 2 + 1) * T], slot(n, m), rhs,
                                       start=first and m % 2 == 0, stop=end, skip_group_check=True)
                    mm.then_inc(panel_done, 1)
                one(n, src[:, 0:T], first=True)
                turns = (count - 2) // 4
                with pe.Fori(0, turns) as i:
                    for j in range(1, 5):
                        one(n + j, src[:, bass.ds(i * (4 * T) + j * T, T)], i)
                for k in range(1 + 4 * turns, count):
                    one(n + k, src[:, k * T:(k + 1) * T], end=(k == count - 1))

            pe.wait_ge(con_in, 16)
            sum_squares(0, hn, KD)
            pe.wait_ge(rms_out, 1)
            project_loop(PANELS["u"], 0, 4, hn)
            pe.wait_ge(S["s5_bcopied"], 1)
            pe.wait_ge(panel_done, PANELS["s5"])
            pe.sem_inc(panel_done, 1)

            def s5_inputs(g):
                pe.wait_ge(evac_done, g + 1)
                if g:
                    pe.wait_ge(S["s5_pre"], g)
                for j in range(4):
                    rows = slice(32 * j, 32 * j + 32)
                    for c in range(2):
                        mm = pe.matmul(ps[:, 4 + j, c * T:(c + 1) * T], s5b[rows, c * 512 + g * P:c * 512 + (g + 1) * P],
                                       zt(ZU + g)[rows, :], start=True, stop=True, skip_group_check=True)
                mm.then_inc(S["s5_bu"], 1)

            def s5_outputs(g):
                pe.wait_ge(S["s5_state"], g + 1)
                for j in range(4):
                    out = ps[32 * j:32 * j + 32, 4, 0:T]
                    at = (4 * g + j) * 32
                    pe.matmul(out, s5c[:, at:at + 32], s5re[:, j * T:(j + 1) * T], start=True, stop=False)
                    mm = pe.matmul(out, s5c[:, 512 + at:512 + at + 32], s5im[:, j * T:(j + 1) * T], start=False, stop=True)
                mm.then_inc(S["s5_y"], 1)

            for g in range(4):
                s5_inputs(g)
                project_loop(PANELS["q"] + 6 * g, ZQ + 6 * g, 6, hn)
                s5_outputs(g)
            n = PANELS["glu"]
            arrive(n)
            pe.wait_ge(S["s5_gelu"], 4)
            for m in range(4):
                for k in range(4):
                    mm = pe.matmul(ps[:, 4 + m, 0:T], slot(n, 4 * m + k), yt(k), start=(k == 0), stop=(k == 3))
                mm.then_inc(S["s5_glu"] if m < 3 else panel_done, 1)

            def hg_values(h):
                if h == 0:
                    pe.wait_ge(evac_done, ZG)
                    pe.wait_ge(S["ya_done"], 1)
                else:
                    pe.wait_ge(S["hg_masked"], 3 * h)
                for b in range(2):
                    mm = pe.transpose(ps[:, 6, b * P:(b + 1) * P], zt(ZI + h)[:, b * P:(b + 1) * P], ident)
                mm.then_inc(S["hg_vt"], 1)

            def hg_scores(h):
                pe.wait_ge(S["hg_eq"], h + 1)
                pe.wait_ge(S["hg_ek"], h + 1)
                pe.wait_ge(S["hg_vtc"], h + 1)
                if h:
                    pe.wait_ge(S["hg_oc"], h)
                for b in range(2):
                    for l in range(8):
                        at = l * T + b * P
                        lhs, rhs = hd[:, at:at + P], heq[:, at:at + P]
                        if l == 7:
                            at = h * T + b * P
                            lhs, rhs = hk[:, at:at + P], zt(ZQ, HG)[:, at:at + P]
                        mm = pe.matmul(ps[:, 4 + 2 * b + l // 4, (l % 4) * P:(l % 4 + 1) * P], lhs, rhs,
                                       start=True, stop=True, skip_group_check=True)
                    mm.then_inc(S["hg_sc"], 1)
                pe.wait_ge(S["hg_masked"], 3 * h + 1)
                pe.matmul(ps[:, 4, 0:P], hd[:, 7 * T:7 * T + P], heq[:, 7 * T + P:8 * T], start=True, stop=True) \
                    .then_inc(S["hg_sc"], 1)

            def hg_output(h):
                pe.wait_ge(S["hg_masked"], 3 * h + 3)
                pe.matmul(ps[:, 5, 0:P], hvt[:, 0:P], hms[:, 0:P], start=True, stop=True, skip_group_check=True)
                pe.matmul(ps[:, 5, P:T], hvt[:, P:T], hms[:, P:T], start=True, stop=False, skip_group_check=True)
                pe.matmul(ps[:, 5, P:T], hvt[:, 0:P], hms[:, T:T + P], start=False, stop=True,
                          skip_group_check=True).then_inc(S["hg_o"], 1)

            for h in range(HG):
                hg_values(h)
                hg_scores(h)
                project_loop(PANELS["cx"] + 3 * h, ZC + 3 * h, 3, hn)
                hg_output(h)
            project_loop(PANELS["if"], ZIF, 1, hn)
            pe.wait_ge(S["hg_sq"], 1)
            for h in range(HG):
                mm = pe.matmul(ps[:, 4 + h // 2, (h % 2) * T:(h % 2 + 1) * T], ones, zt(ZF + h), start=True, stop=True,
                               skip_group_check=True)
            mm.then_inc(S["hg_ss"], 1)

            project_loop(PANELS["ga"], ZGA, 8, hn)
            pe.wait_ge(S["ml_ca"], 1)
            pe.wait_ge(S["yb_done"], 1)
            for c in range(2 * MH):
                h, half = c % MH, c // MH
                n = PANELS["qk"] + h // 2
                arrive(n)
                if c >= 4:
                    pe.wait_ge(S["ml_qkc"], c - 3)
                for mi, (tile, r0, rows, _) in enumerate(head_parts(h)):
                    for ki, (kt, k0, kr, _) in enumerate(head_parts(h)):
                        blk = (h % 2) * 8 + half * 4 + mi * 2 + ki
                        mm = pe.matmul(ps[r0:r0 + rows, 4 + c % 4, mi * T:(mi + 1) * T],
                                       slot(n, blk, rows, slice(k0, k0 + kr)), mca[k0:k0 + kr, kt * T:(kt + 1) * T],
                                       start=(ki == 0), stop=(ki == 1), skip_group_check=True)
                mm.then_inc(S["ml_qk"], 1)
            pe.wait_ge(S["ml_qk"], 2 * MH)
            pe.sem_inc(panel_done, 2)
            pe.wait_ge(S["ml_qkc"], 2 * MH)
            pe.wait_ge(S["ml_rows"], 1)
            for b in range(2):
                mm = pe.transpose(ps[:, 4, b * MH:(b + 1) * MH], mrow[:, 2 * T + b * P:2 * T + (b + 1) * P], ident[0:MH, 0:MH])
            mm.then_inc(S["ml_at"], 1)
            for k in range(HG):
                at = k // 3 * T
                if k >= 3:
                    pe.wait_ge(S["ml_vtc"], k - 2)
                for b in range(2):
                    mm = pe.transpose(ps[:, 5 + k % 3, at + b * P:at + (b + 1) * P], zt(ZV + k)[:, b * P:(b + 1) * P], ident)
                mm.then_inc(S["ml_vt"], 1)
            pe.wait_ge(S["ml_vtc"], HG)
            pe.wait_ge(S["ml_atc"], 1)

            def ml_scores(h):
                if h:
                    pe.wait_ge(S["ml_h"], 2 * h)
                sel = mc("sel", P, h * P, MH)
                pe.matmul(ps[:, 4, 0:T], sel, mrow[:, 4 * T:5 * T], start=True, stop=True, skip_group_check=True)
                pe.matmul(ps[:, 4, T:2 * T], sel, mrow[:, 5 * T:6 * T], start=True, stop=True,
                          skip_group_check=True).then_inc(S["ml_bc"], 1)
                for b in range(2):
                    for ki, (kt, k0, kr, _) in enumerate(head_parts(h)):
                        mm = pe.matmul(ps[:, 5, b * T:b * T + T - b * P],
                                       mca[k0:k0 + kr, kt * T + b * P:kt * T + (b + 1) * P],
                                       zt(ZC + kt)[k0:k0 + kr, b * P:T], start=(ki == 0), stop=(ki == 1),
                                       skip_group_check=True)
                mm.then_inc(S["ml_sc"], 1)

            def ml_sums(h):
                pe.wait_ge(S["ml_p"], h + 1)
                pe.matmul(ps[:, 6, 0:T], ones, mp[:, 0:T], start=True, stop=False, skip_group_check=True)
                pe.matmul(ps[:, 6, P:T], ones, mp[:, T:3 * P], start=False, stop=True, skip_group_check=True)
                for mi, (tile, r0, rows, _) in enumerate(head_parts(h)):
                    c = tile * P + r0
                    pe.matmul(ps[r0:r0 + rows, 7, mi * T:(mi + 1) * T], mvt[:, c:c + rows], mp[:, 0:T],
                              start=True, stop=False, skip_group_check=True)
                    mm = pe.matmul(ps[r0:r0 + rows, 7, mi * T + P:(mi + 1) * T], mvt[:, HG * P + c:HG * P + c + rows],
                                   mp[:, T:3 * P], start=False, stop=True, skip_group_check=True)
                mm.then_inc(S["ml_nd"], 1)

            for h in range(MH):
                ml_scores(h)
                project_loop(PANELS["ga2"] + 6 * h, ZGA + 8 + 6 * h, 6, hn)
                ml_sums(h)
            pe.wait_ge(S["ml_sq"], 1)
            for h in range(MH):
                for ki, (kt, k0, kr, _) in enumerate(head_parts(h)):
                    mm = pe.matmul(ps[:, 4 + h, 0:T], ones[k0:k0 + kr, :],
                                   mca[k0:k0 + kr, kt * T:(kt + 1) * T], start=(ki == 0), stop=(ki == 1),
                                   skip_group_check=True)
            mm.then_inc(S["ml_ss"], 1)

            def merge(m, i=None):
                n = PANELS["merge"] + 2 * m
                project(n, OUT["gc"] + m, hn, i, 8, 4)
                arrive(n + 1, i, 8)
                if m == 0:
                    pe.wait_ge(S["yc_done"], 1)
                if m >= 2:
                    pe.wait_ge(S["branch_read"], m - 1 if i is None else i * 4 + (m - 1))
                for k in range(KD):
                    part = 0 if k < 4 else 1 if k < 10 else 2
                    mm = pe.matmul(ps[:, 4 + 2 * (m % 2) + part // 2, (part % 2) * T:(part % 2 + 1) * T], slot(n + 1, k),
                                   yt(k), start=k in (0, 4, 10), stop=k in (3, 9, 15), skip_group_check=True)
                mm.then_inc(panel_done, 1)

            for m in range(4):
                merge(m)
            with pe.Fori(0, 3) as i:
                for m in range(4, 8):
                    merge(m, i)
            pe.wait_ge(S["merged_done"], KD)
            project_loop(PANELS["wout"], OUT["wout"], KD, merged)
            sum_squares(1, hn, KD)
            pe.wait_ge(rms_out, 2)

            project_loop(PANELS["up"], OUT["up"], 2 * FT, hn)
            pe.wait_ge(S["ff_out"], FT)
            pe.wait_ge(evac_done, OUT["in2"])
            accumulate_all(PANELS["down"], FT, gff)
            sum_squares(2, hn, KD)
            sum_squares(3, hn, KD)
            pe.wait_ge(rms_out, 4)

            project_loop(PANELS["in2"], OUT["in2"], 17, hn)
            n = PANELS["pool"]
            arrive(n)
            pe.wait_ge(S["po_d"], 1)
            for c in range(8):
                if c >= 4:
                    pe.wait_ge(S["po_yc"], c - 3)
                for k in range(2):
                    mm = pe.matmul(ps[:, 4 + c % 4, 0:T], slot(n, 2 * c + k), pb[2][:, (c // 2 * 2 + k) * T:(c // 2 * 2 + k + 1) * T],
                                   start=(k == 0), stop=(k == 1))
                mm.then_inc(S["po_y"] if c < 7 else panel_done, 1)
            pe.wait_ge(S["po_yc"], 8)
            sum_squares(4, sq, 4)
            sum_squares(5, sq[:, 4 * T:8 * T], 4, 5)
            pe.wait_ge(rms_out, 6)
            o = 0

            def small(n, blocks, src, m=P, width=P, last=False):
                nonlocal o
                if o >= 4:
                    pe.wait_ge(S["at_qc"], o - 3)
                for k in range(4):
                    at = (blocks * 4 + k) * width
                    mm = pe.matmul(ps[0:m, 4 + o % 4, 0:T], ring[:, n % SLOTS, at:at + m], src[:, k * T:(k + 1) * T],
                                   start=(k == 0), stop=(k == 3))
                mm.then_inc(S["at_q"], 1)
                o += 1
                if last:
                    pe.wait_ge(S["at_q"], o)
                    pe.sem_inc(panel_done, 1)

            for h in range(AH):
                arrive(PANELS["uq"] + h // 4)
                small(PANELS["uq"] + h // 4, h % 4, zt(8, 4), last=h % 4 == 3)
            arrive(PANELS["uqr"])
            for h in range(AH):
                small(PANELS["uqr"], h, zt(8, 4), m=64, width=64, last=h == 7)
            for h in range(AH):
                arrive(PANELS["ukn"] + h // 4)
                small(PANELS["ukn"] + h // 4, h % 4, zt(12, 4), last=h % 4 == 3)
            for c in range(2):
                n = PANELS["ukv"] + c
                arrive(n)
                for b in range(2):
                    pe.wait_ge(S["at_qc"], o - 3)
                    for k in range(4):
                        at = (12 + k) * T + b * P
                        mm = pe.matmul(ps[:, 4 + o % 4, :], z[:, at:at + P], ring[:, n % SLOTS, k * BANK:(k + 1) * BANK],
                                       start=(k == 0), stop=(k == 3))
                    mm.then_inc(S["at_q"], 1)
                    o += 1
                pe.wait_ge(S["at_q"], o)
                pe.sem_inc(panel_done, 1)
            for r in range(2):
                pe.wait_ge(S["at_qc"], o if r == 0 else o)
                if r:
                    pe.wait_ge(S["at_rotc"], 1)
                pe.wait_ge(S["at_sq"], r + 1)
                for h in range(AH):
                    out = ps[:, 4 + h // 2, (h % 2) * T:(h % 2 + 1) * T]
                    pe.matmul(out, ones, sq[:, h * T:(h + 1) * T], start=True, stop=False, skip_group_check=True)
                    mm = pe.matmul(out, ones[0:64, :], vsq[0:64, (h if r == 0 else 0) * T:((h if r == 0 else 0) + 1) * T],
                                   start=False, stop=True, skip_group_check=True)
                mm.then_inc(S["at_ss"], 1)
                pe.wait_ge(S["at_qn"], r + 1)
                if r == 0:
                    for c in range(4):
                        mm = pe.matmul(ps[0:64, 4 + c, :], con[0:64, CC["perm"]:CC["perm"] + 64], qrope[0:64, c * BANK:(c + 1) * BANK],
                                       start=True, stop=True)
                else:
                    mm = pe.matmul(ps[0:64, 4, 0:T], con[0:64, CC["perm"]:CC["perm"] + 64], rope[4], start=True, stop=True)
                mm.then_inc(S["at_rot"], 1)
            pe.wait_ge(S["at_done"], 1)

            def at_scores(h):
                u = h % 2
                if h >= 2:
                    pe.wait_ge(S["at_e"], 2 * h - 2)
                q, k, qq, kk = (a[:, h * T:(h + 1) * T] for a in (qn, kn, qrope, krope))
                bank = ps[:, 4 + u, :]
                for b in range(2):
                    out = bank[:, b * P:b * P + P + b * P]
                    pe.matmul(out, q[:, b * P:(b + 1) * P], k[:, 0:P + b * P], start=True, stop=False, skip_group_check=True)
                    mm = pe.matmul(out, qq[0:64, b * P:(b + 1) * P], kk[0:64, 0:P + b * P], start=False, stop=True,
                                   skip_group_check=True)
                mm.then_inc(S["at_s"], 1)

            def at_values(h):
                u = h % 2
                pe.wait_ge(S["at_p"], h + 1)
                if h:
                    pe.wait_ge(S["at_tc"], h)
                for c in range(3):
                    mm = pe.transpose(ps[:, 6, c * P:(c + 1) * P], sc[u][:, c * P:(c + 1) * P], ident)
                mm.then_inc(S["at_t"], 1)
                pe.wait_ge(S["at_tc"], h + 1)
                if h:
                    pe.wait_ge(S["at_oc"], h)
                pe.matmul(ps[:, 7, 0:T], vtm[:, h * P:(h + 1) * P], pt[u][:, 0:T], start=True, stop=False, skip_group_check=True)
                pe.matmul(ps[:, 7, P:T], vtm[:, 1024 + h * P:1024 + (h + 1) * P], pt[u][:, T:3 * P], start=False, stop=True,
                          skip_group_check=True).then_inc(S["at_o"], 1)

            at_scores(0)
            for h in range(AH):
                if h + 1 < AH:
                    at_scores(h + 1)
                at_values(h)
            pe.wait_ge(S["at_oc"], AH)
            project_loop(PANELS["wout2"], OUT["wout2"], KD, y)
            sum_squares(6, hn, KD)
            pe.wait_ge(rms_out, 7)

            project_loop(PANELS["pq"], OUT["pq"], KD, hn)
            n = PANELS["subk"]
            arrive(n)
            for b in range(2):
                if b:
                    pe.wait_ge(S["pk_sc"], 4)
                for c in range(16):
                    if c % 4 == 0 and b == 0:
                        pe.wait_ge(evac_done, OUT["eu"])
                    mm = pe.matmul(ps[:, 4 + c // 4, (c % 4) * P:(c % 4 + 1) * P], q2[:, c * T + b * P:c * T + (b + 1) * P],
                                   slot(n, c), start=True, stop=True, skip_group_check=True)
                    if c % 4 == 3 and (b, c) != (1, 15):
                        mm.then_inc(S["pk_s"], 1)
            mm.then_inc(panel_done, 1)
            project_loop(PANELS["eu"], OUT["eu"], NK // 2, hn)
            pe.wait_ge(S["pk_et"], 1)
            for k in range(3):
                for b in range(2):
                    mm = pe.transpose(ps[:, 4 + k, b * P:(b + 1) * P], etm[:, k * T + b * P:k * T + (b + 1) * P], ident)
            mm.then_inc(S["pk_t"], 1)
            project_loop(PANELS["eu"] + NK // 2, OUT["eu"] + NK // 2, NK // 2, hn)
            pe.wait_ge(S["pk_tc"], 1)

            def token(t, i=None):
                v = (lambda c: c if i is None else i * 16 + c)
                pe.wait_ge(S["oh1_done"], v(t + 1))
                pe.wait_ge(S["oh2_done"], v(t + 1))
                if t % 4 == 0 and t >= 16:
                    pe.wait_ge(S["tok_ev"], t // 4 - 3 if i is None else i * 4 + (t // 4 - 3))
                pe.matmul(ps[:, 4 + t // 4 % 4, (t % 4) * P:(t % 4 + 1) * P], oh2[:, (t % 8) * P:(t % 8 + 1) * P],
                          oh1[:, (t % 4) * P:(t % 4 + 1) * P], start=True, stop=True, skip_group_check=True) \
                    .then_inc(S["tok_mm"], 1)

            for t in range(16):
                token(t)
            with pe.Fori(0, T // 16 - 1) as i:
                for t in range(16, 32):
                    token(t, i)
            pe.wait_ge(S["tok_ev"], T // 4)
            accumulate_all(PANELS["ev"], NK, A)

            sum_squares(7, hn, KD)
            pe.wait_ge(rms_out, 8)
            pe.wait_ge(p_in, 16)
            for m in range(KD):
                n = PANELS["pp"] + m // 8
                arrive(n)
                for k in range(2):
                    mm = pe.matmul(ps[:, m // 2, (m % 2) * T:(m % 2 + 1) * T], slot(n, m % 8 * 2 + k), pTs[:, k * T:(k + 1) * T],
                                   start=(k == 0), stop=(k == 1), skip_group_check=True)
                if m % 8 == 7:
                    mm.then_inc(panel_done, 1)
            pe.wait_ge(S["pp_ev"], 8)
            project_loop(PANELS["pg"], OUT["pg"], KD, hn)

        @block.vector
        def _(dve):
            step = Count(dve, dve_step)
            evac = Count(dve, evac_done)
            L = step.link
            N = {}

            def tell(name, ins):
                if name not in N:
                    N[name] = Count(dve, S[name])
                N[name].link(ins)

            def tt(out, a, b, op):
                return dve.tensor_tensor(out, a, b, op)

            def ts(out, a, s1, s2, op0, op1=None):
                return dve.tensor_scalar(out, a, s1, s2, op0) if op1 is None else dve.tensor_scalar(out, a, s1, s2, op0, op1)

            def stt(out, a, s, b, op0, op1):
                return dve.scalar_tensor_tensor(out, a, s, b, op0, op1)

            rms_c = {k: Count(dve, s) for k, s in (("ms", rms_ms), ("out", rms_out))}

            def normalise(r, src, dst, gain, tiles, bank=4):
                dve.wait_ge(rms_ss, r + 1)
                rms_c["ms"].link(ts(rstd[:], ps[:, bank, 0:T], 1.0 / (tiles * P), EPS, ALU.mult, ALU.add))
                dve.wait_ge(rms_rt, r + 1)
                L(dve.reciprocal(rstd[:], rstd[:]))
                for k in range(tiles):
                    c = slice(k * T, (k + 1) * T)
                    last = stt(dst[:, c], src[:, c], pc(gain, k), rstd[:], ALU.mult, ALU.mult)
                    if k < tiles - 1:
                        step.mark(last)
                rms_c["out"].link(last)

            def reduce_angle(ang, turns):
                L(ts(turns, ang, 1 / TWO_PI, ROUND, ALU.mult, ALU.add))
                L(ts(turns, turns, ROUND, None, ALU.subtract))
                for part in (PI_A, PI_B, PI_C):
                    L(stt(ang, turns, -part, ang, ALU.mult, ALU.add))
                return ts(ang, ang, 3.1415925, -3.1415925, ALU.min, ALU.max)

            def add_residual(p, count):
                for j in range(4):
                    evac_add(p + j, j)
                with dve.Fori(0, count // 4 - 1) as i:
                    evac.enter(i, 4)
                    for j in range(4, 8):
                        evac_add(p + j, j, i)
                    evac.leave(count // 4 - 1)

            def evac_add(p, j, i=None):
                n = panel_of(p)
                if i is None:
                    dve.wait_ge(panel_done, n + 1)
                    c = res[:, j * T:(j + 1) * T]
                else:
                    dve.wait_ge(panel_done, i * 4 + (n + 1))
                    c = res[:, bass.ds(i * (4 * T) + j * T, T)]
                evac.link(tt(c, c, ps[:, p % 4, 0:T], ALU.add))

            def panel_of(p):
                return p - OUT["wout"] + PANELS["wout"] if p < OUT["up"] else p - OUT["wout2"] + PANELS["wout2"]

            dve.wait_ge(par_in, 16)
            dve.wait_ge(x_in, 16)
            s = [s5s[:, 16 * k:16 * k + 16] for k in range(16)]
            lr, li = pc("lam_re", 0, 16), pc("lam_im", 0, 16)
            dve.wait_ge(S["s5_dt"], 1)
            L(tt(s[1], lr, s[0], ALU.mult))
            L(tt(s[2], li, s[0], ALU.mult))
            tell("s5_mi", reduce_angle(s[2], s[5]))
            normalise(0, res, hn, "mix", KD)
            dve.wait_ge(S["s5_ma"], 1)
            L(stt(s[5], s[3], -2.0, s[3], ALU.mult, ALU.mult))
            L(ts(s[5], s[5], 1.0, None, ALU.add))
            L(tt(s[6], s[1], s[4], ALU.mult))
            L(tt(s[5], s[1], s[5], ALU.mult))
            L(ts(s[7], s[5], -1.0, None, ALU.add))
            L(tt(s[8], lr, lr, ALU.mult))
            L(tt(s[9], li, li, ALU.mult))
            L(tt(s[8], s[8], s[9], ALU.add))
            L(dve.reciprocal(s[8], s[8]))
            for out, a, b, op in ((s[9], s[7], s[6], ALU.add), (s[10], s[6], s[7], ALU.subtract)):
                L(tt(s[11], a, lr, ALU.mult))
                L(tt(s[12], b, li, ALU.mult))
                L(tt(out, s[11], s[12], op))
                L(tt(out, out, s[8], ALU.mult))
            n = PANELS["s5"]
            dve.wait_ge(landed[n % SLOTS], 16 * (n // SLOTS + 1))
            L(dve.tensor_copy(s5b, ring[:, n % SLOTS, 0:1024]))
            cre, cim = (ring[:, n % SLOTS, 1024 + 512 * k:1536 + 512 * k].rearrange("p (t c) -> p t c", c=32) for k in range(2))
            fr, fi = (s[k].unsqueeze(2).to_broadcast([P, 16, 32]) for k in (9, 10))
            ta, tb = (s5tmp[:, 512 * k:512 * k + 512].rearrange("p (t c) -> p t c", c=32) for k in range(2))
            o1, o2 = (s5c[:, 512 * k:512 * k + 512].rearrange("p (t c) -> p t c", c=32) for k in range(2))
            L(tt(ta, cre, fr, ALU.mult))
            L(tt(tb, cim, fi, ALU.mult))
            L(tt(o1, ta, tb, ALU.subtract))
            L(tt(ta, cre, fi, ALU.mult))
            L(tt(tb, cim, fr, ALU.mult))
            L(stt(s5c[:, 512:1024], s5tmp[:, 0:512], -1.0, s5tmp[:, 512:1024], ALU.mult, ALU.subtract))
            tell("s5_bcopied", dve.tensor_copy(s5tmp[:, 0:1], s5c[:, 0:1]))

            dve.wait_ge(mix_in, 16)
            vr, vi = (ps[:, 4:8, k * T:(k + 1) * T] for k in range(2))

            def quad(a):
                return a.rearrange("p (t c) -> p t c", c=T)

            for g in range(4):
                for j in range(4):
                    L(ts(s5re[:, j * T:(j + 1) * T], mc("tidx", T), s[2][:, 4 * g + j:4 * g + j + 1], None, ALU.mult))
                tell("s5_angle", reduce_angle(s5re, s5im))
                dve.wait_ge(S["s5_sin"], g + 1)
                L(stt(s5cos, s5tmp, -2.0, s5tmp, ALU.mult, ALU.mult))
                L(ts(s5cos, s5cos, 1.0, None, ALU.add))
                dve.wait_ge(S["s5_bu"], g + 1)
                L(tt(quad(s5re), vr, quad(s5cos), ALU.mult))
                L(tt(quad(s5tmp), vi, quad(s5sin), ALU.mult))
                L(tt(s5re, s5re, s5tmp, ALU.add))
                L(tt(quad(s5im), vi, quad(s5cos), ALU.mult))
                L(tt(quad(s5tmp), vr, quad(s5sin), ALU.mult))
                L(tt(s5im, s5im, s5tmp, ALU.subtract))
                for w in (s5re, s5im):
                    for j in range(4):
                        c = w[:, j * T:(j + 1) * T]
                        mag = s[1][:, 4 * g + j:4 * g + j + 1].to_broadcast([P, T])
                        L(dve.tensor_tensor_scan(c, mag, c, 0.0, ALU.mult, ALU.add))
                L(tt(s5tmp, s5re, s5sin, ALU.mult))
                L(tt(s5re, s5re, s5cos, ALU.mult))
                L(tt(s5sin, s5im, s5sin, ALU.mult))
                L(tt(s5re, s5re, s5sin, ALU.subtract))
                L(tt(s5im, s5im, s5cos, ALU.mult))
                tell("s5_state", tt(s5im, s5im, s5tmp, ALU.add))
                dve.wait_ge(S["s5_y"], g + 1)
                tell("s5_pre", stt(s5tmp[:, 0:T], zt(ZU + g), pc("s5_d", g), ps[:, 4, 0:T], ALU.mult, ALU.add))
            dve.wait_ge(S["s5_sig"], 4)
            tell("ya_done", tt(yt(0, 4), yt(0, 4), s5sin, ALU.mult))

            c6 = [cols[:, 6 * k:6 * k + 6] for k in range(5)]
            tell("hg_lbx", tt(c6[0], pc("hg_lb", 0, 6), pc("hg_lb", 0, 6), ALU.subtract))
            dve.wait_ge(S["hg_lbe"], 1)
            L(dve.reciprocal(c6[2], c6[1]))
            L(tt(c6[2], c6[2], c6[1], ALU.mult))
            L(tt(c6[3], c6[2], c6[2], ALU.subtract))
            L(ts(c6[4], c6[3], -1.0, 1.0, ALU.mult, ALU.add))
            dve.wait_ge(S["hg_sig"], 1)
            for h in range(HG):
                L(ts(zt(ZF + h), zt(ZF + h), c6[4][:, h:h + 1], c6[3][:, h:h + 1], ALU.mult, ALU.add))
            tell("hg_f", ts(hcum, hk, 2.0 ** -63, None, ALU.max))
            L(ts(hk, hk, -1.0, 1.0, ALU.mult, ALU.add))
            dve.wait_ge(S["hg_ln"], 1)
            one = ones[:, 0:1].to_broadcast([P, 64])
            for c in range(HG * 4):
                w = hcum[:, 64 * c:64 * c + 64]
                L(dve.tensor_tensor_scan(w, one, w, 0.0, ALU.mult, ALU.add))
            dve.wait_ge(S["hg_silu"], 1)
            for h in range(HG):
                cum = hcum[:, h * T:(h + 1) * T]
                for l in range(7):
                    m = 32 >> l if l < 6 else 64
                    v = cum.rearrange("p (a b m) -> p a b m", b=2, m=m)
                    d = hd[:, l * T:(l + 1) * T].rearrange("p (a b m) -> p a b m", b=2, m=m)
                    ref = v[:, :, 0, m - 1:m].to_broadcast([P, T // (2 * m), m])
                    if l < 6:
                        step.mark(tt(d[:, :, 1, :], v[:, :, 1, :], ref, ALU.subtract))
                    else:
                        step.mark(dve.tensor_copy(d[:, :, 1, :], v[:, :, 1, :]))
                    step.mark(tt(d[:, :, 0, :], ref, v[:, :, 0, :], ALU.subtract))
                d = hd[:, 7 * T:8 * T]
                step.mark(dve.tensor_copy(d[:, 128:192], cum[:, 128:192]))
                step.mark(ts(d[:, 192:256], cum[:, 192:256], cum[:, 191:192], None, ALU.add))
                step.mark(ts(d[:, 64:128], cum[:, 64:128], -1.0, cum[:, 127:128], ALU.mult, ALU.add))
                L(ts(d[:, 0:64], cum[:, 0:64], -1.0, cum[:, 63:64], ALU.mult, ALU.add))
                tell("hg_exp", ts(d[:, 0:64], d[:, 0:64], cum[:, 127:128], None, ALU.add))
                dve.wait_ge(S["hg_decay"], h + 1)
                tell("hg_eq", tt(heq.rearrange("p (l t) -> p l t", t=T), hd.rearrange("p (l t) -> p l t", t=T),
                                 zt(ZQ + h).unsqueeze(1).to_broadcast([P, 8, T]), ALU.mult))
                for b in range(2):
                    dve.wait_ge(S["hg_sc"], 3 * h + b + 1)
                    L(tt(hmk.rearrange("p (l t) -> p l t", t=BANK), ps[:, 4 + 2 * b:6 + 2 * b, :],
                         mc("hgmask", 8 * P).rearrange("p (l t) -> p l t", t=BANK), ALU.mult))
                    tell("hg_masked", dve.tensor_reduce(hms[:, b * P:(b + 1) * P], hmk.rearrange("p (l t) -> p t l", t=P),
                                                        AX.X, ALU.add))
                dve.wait_ge(S["hg_sc"], 3 * h + 3)
                tell("hg_masked", dve.tensor_copy(hms[:, T:3 * P], ps[:, 4, 0:P]))
                dve.wait_ge(S["hg_o"], h + 1)
                tell("hg_oc", dve.tensor_copy(yt(4 + h), ps[:, 5, 0:T]))
            dve.wait_ge(S["hg_ss"], 1)
            r6 = heq[:, 0:HG * T]
            tell("hg_ms", ts(r6.rearrange("p (a t) -> p a t", t=BANK), ps[:, 4:7, :], 1.0 / P, EPS, ALU.mult, ALU.add))
            dve.wait_ge(S["hg_rt"], 1)
            L(dve.reciprocal(r6, r6))
            for h in range(HG):
                L(stt(yt(4 + h), yt(4 + h), pc("hg_norm", h), r6[:, h * T:(h + 1) * T], ALU.mult, ALU.mult))
            tell("yb_done", tt(yt(4, 6), yt(4, 6), zt(ZG, 6), ALU.mult))

            for k in range(6):
                x, w = zt(ZC + k), mca[:, k * T:(k + 1) * T]
                dve.wait_ge(evac_done, ZC + k + 1)
                L(ts(w, x, pc("conv_w", 18 + k), pc("conv_b", k), ALU.mult, ALU.add))
                for d in range(1, 4):
                    last = stt(w[:, d:T], x[:, 0:T - d], pc("conv_w", (3 - d) * 6 + k), w[:, d:T], ALU.mult, ALU.add)
                    if (k, d) == (5, 3):
                        tell("ml_conv", last)
                    else:
                        L(last)
            dve.wait_ge(evac_done, ZIF + 1)
            r = [mrow[:, k * T:(k + 1) * T] for k in range(6)]
            L(ts(r[0], zt(ZIF)[32:36, :], par[32:36, COL["b_fg"]:COL["b_fg"] + 1], None, ALU.add))
            L(ts(r[3], r[0], -1.0, None, ALU.mult))
            tell("ml_ax", tt(r[1], r[0], r[3], ALU.max))
            dve.wait_ge(S["ml_e"], 1)
            tell("ml_e1", ts(r[1], r[1], 1.0, None, ALU.add))
            L(ts(r[0], r[0], 0.0, None, ALU.min))
            dve.wait_ge(S["ml_ln"], 1)
            L(tt(r[0], r[0], r[1], ALU.subtract))
            L(dve.tensor_tensor_scan(r[1], ones[0:MH, 0:1].to_broadcast([MH, T]), r[0], 0.0, ALU.mult, ALU.add))
            L(stt(r[2], zt(ZIF)[0:MH, :], par[0:MH, COL["b_ig"]:COL["b_ig"] + 1], r[1], ALU.add, ALU.subtract))
            L(dve.tensor_tensor_scan(r[3], r[2], r[2], 0.0, ALU.max, ALU.max))
            L(ts(r[4], r[3], -1.0, None, ALU.mult))
            tell("ml_rows", stt(r[5], r[1], -1.0, r[3], ALU.mult, ALU.subtract))
            dve.wait_ge(S["ml_at"], 1)
            tell("ml_atc", dve.tensor_copy(macol, ps[:, 4, 0:2 * MH]))
            for h in range(MH):
                dve.wait_ge(S["ml_bc"], h + 1)
                L(tt(mx[:, 0:P], ps[:, 4, 0:P], mc("causal", P), ALU.add))
                L(dve.tensor_copy(mx[:, P:T], ps[:, 4, P:T]))
                tell("ml_x", tt(mx[:, T:3 * P], ps[:, 4, P:T], mc("causal", P), ALU.add))
                dve.wait_ge(S["ml_w"], h + 1)
                dve.wait_ge(S["ml_sc"], h + 1)
                tell("ml_p", tt(mp, mx, ps[:, 5, 0:3 * P], ALU.mult))
                dve.wait_ge(S["ml_nd"], h + 1)
                L(ts(mden, ps[:, 6, 0:T], -1.0, None, ALU.mult))
                L(tt(mden, mden, ps[:, 6, 0:T], ALU.max))
                L(tt(mden, mden, men, ALU.max))
                L(dve.reciprocal(mden, mden))
                for mi, (tile, r0, rows, _) in enumerate(head_parts(h)):
                    tell("ml_h", tt(yt(10 + tile)[r0:r0 + rows, :], ps[r0:r0 + rows, 7, mi * T:(mi + 1) * T],
                                    mden[r0:r0 + rows, :], ALU.mult))
            dve.wait_ge(S["ml_ss"], 1)
            r4 = mvt[:, 0:MH * T]
            tell("ml_ms", ts(r4.rearrange("p (a t) -> p a t", t=T), ps[:, 4:8, 0:T], 1.0 / MD, EPS, ALU.mult, ALU.add))
            dve.wait_ge(S["ml_rt"], 1)
            L(dve.reciprocal(r4, r4))
            for h in range(MH):
                for tile, r0, rows, _ in head_parts(h):
                    yy = yt(10 + tile)[r0:r0 + rows, :]
                    L(stt(yy, yy, par[r0:r0 + rows, COL["ml_norm"] + tile:COL["ml_norm"] + tile + 1],
                          r4[r0:r0 + rows, h * T:(h + 1) * T], ALU.mult, ALU.mult))
            dve.wait_ge(S["ml_og"], 1)
            tell("yc_done", tt(yt(10, 6), yt(10, 6), zt(ZO, 6), ALU.mult))

            dve.wait_ge(S["sig_ab"], 1)
            N["branch_read"], N["merged_done"] = Count(dve, S["branch_read"]), Count(dve, S["merged_done"])

            def merge(m, i=None):
                v = (lambda c, per: c if i is None else i * per + c)
                gate = (lambda k: zt(k + m) if i is None else z[:, bass.ds(i * (4 * T) + (k + m) * T, T)])
                out = merged[:, m * T:(m + 1) * T] if i is None else merged[:, bass.ds(i * (4 * T) + m * T, T)]
                a, b = ps[:, 4 + 2 * (m % 2), 0:T], ps[:, 4 + 2 * (m % 2), T:2 * T]
                dve.wait_ge(panel_done, v(PANELS["merge"] + 2 * m + 2, 8))
                L(tt(mg[0], a, gate(ZGA), ALU.mult))
                L(tt(mg[1], b, gate(ZGB), ALU.mult))
                dve.wait_ge(evac_done, v(OUT["gc"] + m + 1, 4))
                tell("branch_read", tt(mg[2], ps[:, 5 + 2 * (m % 2), 0:T], mg[3 + m % 2], ALU.mult))
                L(tt(mg[0], mg[0], mg[1], ALU.add))
                tell("merged_done", tt(out, mg[0], mg[2], ALU.add))

            for m in range(4):
                merge(m)
            with dve.Fori(0, 3) as i:
                cs = (step, N["branch_read"], N["merged_done"])
                for c, per in zip(cs, (12, 4, 4)):
                    c.enter(i, per)
                for m in range(4, 8):
                    merge(m, i)
                for c in cs:
                    c.leave(3)
            dve.wait_ge(evac_done, OUT["wout"])
            evac.base = OUT["wout"]
            add_residual(OUT["wout"], KD)
            normalise(1, res, hn, "ffn", KD)

            N["ff_out"] = Count(dve, S["ff_out"])

            def ffn_pair(u, i):
                for half, f in ((0, fa), (1, fb)):
                    p = OUT["up"] + 2 * u + half
                    w = (lambda c: par[:, bass.ds(i * 16 + (COL["fconv"] + 8 * u + 4 * half + c), 1)])
                    x = ps[:, p % 4, 0:T]
                    dve.wait_ge(panel_done, i * 4 + (PANELS["up"] + 2 * u + half + 1))
                    L(ts(f, x, w(2), w(3), ALU.mult, ALU.add))
                    L(stt(f[:, 1:T], x[:, 0:T - 1], w(1), f[:, 1:T], ALU.mult, ALU.add))
                    evac.link(stt(f[:, 2:T], x[:, 0:T - 2], w(0), f[:, 2:T], ALU.mult, ALU.add))
                dve.wait_ge(S["ff_silu"], i * 2 + (u + 1))
                tell("ff_out", tt(gff[:, bass.ds(i * (2 * T) + u * T, T)], fa, fb, ALU.mult))

            with dve.Fori(0, FT // 2) as i:
                for c, per in ((step, 8), (evac, 4), (N["ff_out"], 2)):
                    c.enter(i, per)
                for u in range(2):
                    ffn_pair(u, i)
                for c in (step, evac, N["ff_out"]):
                    c.leave(FT // 2)

            def add_all(n):
                dve.wait_ge(panel_done, n)
                for b in range(8):
                    c = res[:, b * BANK:(b + 1) * BANK]
                    tell("res_done", tt(c, c, ps[:, b, :], ALU.add))

            add_all(PANELS["down"] + FT)
            normalise(2, res, res, "final", KD)
            normalise(3, res, hn, "mix2", KD)

            dve.wait_ge(evac_done, OUT["in2"] + 8)
            src = z
            for k in range(4):
                dst, d, a = pb[k % 2], 1 << k, 2 * k
                s3 = src[:, a * T:8 * T].rearrange("p (c t) -> p c t", t=T)
                d3 = dst[:, a * T:8 * T].rearrange("p (c t) -> p c t", t=T)
                L(tt(d3[:, :, d:T], s3[:, :, d:T], s3[:, :, 0:T - d], ALU.add))
                L(dve.tensor_copy(d3[:, :, 0:d], s3[:, :, 0:d]))
                c = slice(a * T, (a + 2) * T)
                cnt = mc("invcnt", T, k * T).unsqueeze(1).to_broadcast([P, 2, T])
                L(tt(pb[2][:, c].rearrange("p (c t) -> p c t", t=T), dst[:, c].rearrange("p (c t) -> p c t", t=T), cnt, ALU.mult))
                last = tt(pb[2][:, c], pb[2][:, c], z[:, c], ALU.subtract)
                if k < 3:
                    L(last)
                else:
                    tell("po_d", last)
                src = dst
            for c in range(8):
                if c < 7:
                    dve.wait_ge(S["po_y"], c + 1)
                else:
                    dve.wait_ge(panel_done, PANELS["pool"] + 1)
                tell("po_yc", ts(yt(c), ps[:, 4 + c % 4, 0:T], pc("pool_scale", c), None, ALU.mult))
            normalise(4, zt(8, 4), zt(8, 4), "q_lat", 4, 4)
            normalise(5, zt(12, 4), zt(12, 4), "kv_lat", 4, 5)
            ang, turns, cos, sin, kro = rope
            dve.wait_ge(pos_in, 16)
            L(dve.tensor_copy(ang, posi))
            L(ts(ang, ang, con[0:64, CC["invfreq"]:CC["invfreq"] + 1], None, ALU.mult))
            tell("rp_angle", reduce_angle(ang, turns))
            dve.wait_ge(S["rp_sin"], 1)
            L(stt(cos, cos, -2.0, cos, ALU.mult, ALU.mult))
            L(ts(cos, cos, 1.0, None, ALU.add))
            for o in range(28):
                dve.wait_ge(S["at_q"], o + 1)
                bank = ps[:, 4 + o % 4, :]
                if o < 8:
                    out, x = qn[:, o * T:(o + 1) * T], bank[:, 0:T]
                elif o < 16:
                    out, x = qrope[0:64, (o - 8) * T:(o - 7) * T], bank[0:64, 0:T]
                elif o < 24:
                    out, x = kn[:, (o - 16) * T:(o - 15) * T], bank[:, 0:T]
                else:
                    c, b = divmod(o - 24, 2)
                    out, x = vtm[:, b * 1024 + c * BANK:b * 1024 + (c + 1) * BANK], bank
                tell("at_qc", dve.tensor_copy(out, x))
            qr3, kr3, rq3 = (a[0:64, :].rearrange("p (h t) -> p h t", t=T) for a in (qrope, krope, rq))
            cb, sbr = (a.unsqueeze(1).to_broadcast([64, AH, T]) for a in (cos, sin))
            for r in range(2):
                dve.wait_ge(S["at_ss"], r + 1)
                tell("at_ms", ts(rq.rearrange("p (a t) -> p a t", t=BANK), ps[:, 4:8, :], 1.0 / 192, EPS, ALU.mult, ALU.add))
                dve.wait_ge(S["at_rt"], r + 1)
                L(dve.reciprocal(rq, rq))
                if r == 0:
                    L(stt(qn, qn, pc("qn_n"), rq, ALU.mult, ALU.mult))
                    tell("at_qn", stt(qrope[0:64, :], qrope[0:64, :], par[0:64, COL["qn_r"]:COL["qn_r"] + 1], rq[0:64, :], ALU.mult, ALU.mult))
                    dve.wait_ge(S["at_rot"], 1)
                    rot = ps[0:64, 4:8, :].rearrange("p a (c t) -> p (a c) t", t=T)
                    tell("at_rotc", tt(kr3, rot, sbr, ALU.mult))
                    L(tt(qr3, qr3, cb, ALU.mult))
                    L(tt(qr3, qr3, kr3, ALU.add))
                else:
                    L(stt(kn, kn, pc("kn_n"), rq, ALU.mult, ALU.mult))
                    tell("at_qn", ts(kro, zt(16)[0:64, :], par[0:64, COL["kn_r"]:COL["kn_r"] + 1], None, ALU.mult))
                    dve.wait_ge(S["at_rot"], 2)
                    L(tt(ang, ps[0:64, 4, 0:T], sin, ALU.mult))
                    L(tt(kro, kro, cos, ALU.mult))
                    L(tt(kro, kro, ang, ALU.add))
                    tell("at_done", tt(kr3, kro.unsqueeze(1).to_broadcast([64, AH, T]), rq3, ALU.mult))
            scale = 192 ** -0.5
            for h in range(AH):
                u, k = h % 2, sm[:, 8 * h:8 * h + 8]
                dve.wait_ge(S["at_s"], h + 1)
                if h >= 2:
                    dve.wait_ge(S["at_t"], h - 1)
                L(tt(sc[u], ps[:, 4 + u, 0:384], mc("chunkmask", 384), ALU.add))
                L(dve.tensor_reduce(k[:, 0:1], sc[u][:, 0:P], AX.X, ALU.max))
                L(dve.tensor_reduce(k[:, 1:2], sc[u][:, P:384], AX.X, ALU.max))
                tell("at_mx", ts(k[:, 2:4], k[:, 0:2], -scale, None, ALU.mult))
                dve.wait_ge(S["at_e"], 2 * h + 2)
                L(dve.reciprocal(k[:, 6:8], k[:, 4:6]))
                L(ts(sc[u][:, 0:P], sc[u][:, 0:P], k[:, 6:7], None, ALU.mult))
                tell("at_p", ts(sc[u][:, P:384], sc[u][:, P:384], k[:, 7:8], None, ALU.mult))
                if h:
                    dve.wait_ge(S["at_o"], h)
                    tell("at_oc", dve.tensor_copy(yt(7 + h), ps[:, 7, 0:T]))
            dve.wait_ge(S["at_o"], AH)
            tell("at_oc", dve.tensor_copy(yt(15), ps[:, 7, 0:T]))
            dve.wait_ge(evac_done, OUT["wout2"])
            evac.base, evac.k = OUT["wout2"], 0
            add_residual(OUT["wout2"], KD)
            normalise(6, res, hn, "ffn2", KD)

            def top16(vals, idx, src):
                L(dve.max(vals[:, 0:8], src))
                L(dve.max_index(idx[:, 0:8], vals[:, 0:8], src))
                L(dve.match_replace(src, vals[:, 0:8], src, -3e38))
                L(dve.max(vals[:, 8:16], src))
                L(dve.max_index(idx[:, 8:16], vals[:, 8:16], src))

            for b in range(2):
                for c in range(16):
                    k = 16 * b + c
                    if c % 4 == 0:
                        dve.wait_ge(S["pk_sc"], 4 * b + c // 4 + 1)
                    top16(val[:, 16 * k:16 * k + 16], vidx[:, 16 * k:16 * k + 16], s12[:, k * NK:(k + 1) * NK])
                v4 = val[:, 256 * b:256 * b + 256].rearrange("p (h s k) -> p h s k", s=2, k=16)
                cb4 = cand[:, 2048 * b:2048 * b + 2048].rearrange("p (h i j) -> p h i j", i=16, j=16)
                L(tt(cb4, v4[:, :, 0, :].unsqueeze(3).to_broadcast([P, PH, 16, 16]),
                     v4[:, :, 1, :].unsqueeze(2).to_broadcast([P, PH, 16, 16]), ALU.add))
                for h in range(PH):
                    k = PH * b + h
                    top16(cval[:, 16 * k:16 * k + 16], cidx[:, 16 * k:16 * k + 16], cand[:, 256 * k:256 * k + 256])
            c3 = cval.rearrange("p (h k) -> p h k", k=16)
            top = cval.rearrange("p (h k) -> p h k", k=16)[:, :, 0:1]
            L(dve.tensor_copy(gsum.unsqueeze(2), top))
            tell("pk_g", tt(c3, c3, gsum.unsqueeze(2).to_broadcast([P, 16, 16]), ALU.subtract))
            L(ts(cdu[0], cidx, 4, None, ALU.logical_shift_right))
            L(ts(cdu[1], cidx, 15, None, ALU.bitwise_and))
            L(dve.tensor_copy(cdf[0], cdu[0]))
            L(dve.tensor_copy(cdf[1], cdu[1]))
            L(dve.tensor_copy(vidf, vidx))
            e3 = eqt.rearrange("p (a j) -> p a j", j=16)
            e4 = eqt.rearrange("p (h k j) -> p h k j", k=16, j=16)
            for half in range(2):
                for b in range(2):
                    L(tt(e3, cdf[half][:, P * b:P * b + P].unsqueeze(2).to_broadcast([P, P, 16]),
                         iota[:, 0:16].unsqueeze(1).to_broadcast([P, P, 16]), ALU.is_equal))
                    i4 = vidf[:, 256 * b:256 * b + 256].rearrange("p (h s k) -> p h s k", s=2, k=16)[:, :, half, :]
                    L(tt(e4, e4, i4.unsqueeze(2).to_broadcast([P, PH, 16, 16]), ALU.mult))
                    L(dve.tensor_reduce(etm[:, half * T + b * P:half * T + (b + 1) * P], e3, AX.X, ALU.add))
            dve.wait_ge(S["pk_e"], 1)
            L(dve.tensor_reduce(gsum, c3, AX.X, ALU.add))
            L(dve.reciprocal(gsum, gsum))
            tell("pk_et", tt(etm[:, 2 * T:3 * T].rearrange("p (h k) -> p h k", k=16), c3,
                             gsum.unsqueeze(2).to_broadcast([P, 16, 16]), ALU.mult))
            dve.wait_ge(S["pk_t"], 1)
            for k in range(2):
                L(dve.tensor_copy(et[:, k * T:(k + 1) * T], ps[:, 4 + k, 0:T]))
            tell("pk_tc", dve.tensor_copy(et[:, 2 * T:3 * T], ps[:, 6, 0:T]))

            N["oh1_done"], N["tok_ev"] = Count(dve, S["oh1_done"]), Count(dve, S["tok_ev"])
            a3 = A.rearrange("p (e t) -> p t e", t=T)

            def rows(g, i=None):
                if g:
                    dve.wait_ge(S["tok_mm"], 4 * g if i is None else i * 16 + 4 * g)
                for t in range(4 * g, 4 * g + 4):
                    e = (lambda k: et[:, k * T + t:k * T + t + 1] if i is None else et[:, bass.ds(i * 16 + (k * T + t), 1)])
                    N["oh1_done"].mark(ts(oh1[:, t % 4 * P:(t % 4 + 1) * P], iota, e(0), e(2), ALU.is_equal, ALU.mult))

            def weigh(g, i=None):
                c = a3[:, 4 * g:4 * g + 4, :] if i is None else a3[:, bass.ds(i * 16 + 4 * g, 4), :]
                N["tok_ev"].mark(tt(c, c, ps[:, 4 + g % 4, :].rearrange("p (t e) -> p t e", e=P), ALU.mult))

            dve.wait_ge(evac_done, OUT["pg"])
            rows(0)
            for g in range(3):
                rows(g + 1)
                weigh(g)
            with dve.Fori(0, T // 16 - 1) as i:
                N["oh1_done"].enter(i, 16)
                N["tok_ev"].enter(i, 4)
                for g in range(3, 7):
                    rows(g + 1, i)
                    weigh(g, i)
                N["oh1_done"].leave(T // 16 - 1)
                N["tok_ev"].leave(T // 16 - 1)
            dve.wait_ge(S["tok_mm"], T)
            weigh(T // 4 - 1)
            add_all(PANELS["ev"] + NK)
            normalise(7, res, hn, "ple", KD)
            for b in range(8):
                dve.wait_ge(panel_done, PANELS["pp"] + b // 4 + 1)
                tell("pp_ev", dve.tensor_copy(ppj[:, b * BANK:(b + 1) * BANK], ps[:, b, :]))
            N["out_ready"] = Count(dve, S["out_ready"])
            with dve.Fori(0, KD // 4) as i:
                step.enter(i, 4)
                N["out_ready"].enter(i, 4)
                for j in range(4):
                    dve.wait_ge(evac_done, i * 4 + (OUT["pg"] + j + 1))
                    c, r = (a[:, bass.ds(i * (4 * T) + j * T, T)] for a in (ppj, res))
                    L(tt(c, c, gt[:, j * T:(j + 1) * T], ALU.mult))
                    tell("out_ready", tt(r, r, c, ALU.add))
                step.leave(KD // 4)
                N["out_ready"].leave(KD // 4)

        @block.scalar
        def _(act):
            step = Count(act, act_step)
            evac = Count(act, evac_done)
            sq_c, rt_c = Count(act, rms_sq), Count(act, rms_rt)
            N = {}

            def tell(name, ins):
                if name not in N:
                    N[name] = Count(act, S[name])
                N[name].link(ins)

            def fn(out, x, f, **kw):
                return act.activation(out, x, f, **kw)

            def squares(src, dst, tiles):
                for q in range(4):
                    c = slice(q * tiles // 4 * T, (q + 1) * tiles // 4 * T)
                    sq_c.link(fn(dst[:, c], src[:, c], ACT.Square))

            def root(r):
                act.wait_ge(rms_ms, r + 1)
                rt_c.link(fn(rstd[:], rstd[:], ACT.Sqrt))

            def read_outputs(n, p, count, dst, at):
                turns = count // 4 if count >= 8 else 0
                if turns:
                    with act.Fori(0, turns) as i:
                        evac.enter(i, 4)
                        for j in range(4):
                            act.wait_ge(panel_done, i * 4 + (n + j + 1))
                            evac.link(fn(dst[:, bass.ds(i * (4 * T) + (at + j) * T, T)], ps[:, (p + j) % 4, 0:T], ACT.Copy))
                        evac.leave(turns)
                for j in range(4 * turns, count):
                    act.wait_ge(panel_done, n + j + 1)
                    evac.link(fn(dst[:, (at + j) * T:(at + j + 1) * T], ps[:, (p + j) % 4, 0:T], ACT.Copy))

            s = [s5s[:, 16 * k:16 * k + 16] for k in range(5)]
            act.wait_ge(par_in, 16)
            tell("s5_dt", fn(s[0], pc("log_dt", 0, 16), ACT.Exp))
            act.wait_ge(x_in, 16)
            squares(res, hn, KD)
            root(0)
            act.wait_ge(S["s5_mi"], 1)
            step.link(fn(s[1], s[1], ACT.Exp))
            step.link(fn(s[3], s[2], ACT.Sin, scale=0.5))
            tell("s5_ma", fn(s[4], s[2], ACT.Sin))
            read_outputs(PANELS["u"], 0, 4, z, ZU)
            for g in range(4):
                act.wait_ge(S["s5_angle"], g + 1)
                step.link(fn(s5tmp, s5re, ACT.Sin, scale=0.5))
                tell("s5_sin", fn(s5sin, s5re, ACT.Sin))
                read_outputs(PANELS["q"] + 6 * g, ZQ + 6 * g, 6, z, ZQ + 6 * g)
                act.wait_ge(S["s5_pre"], g + 1)
                tell("s5_gelu", fn(yt(g), s5tmp[:, 0:T], ACT.Gelu_apprx_tanh))
            for m in range(4):
                if m < 3:
                    act.wait_ge(S["s5_glu"], m + 1)
                else:
                    act.wait_ge(panel_done, PANELS["glu"] + 1)
                tell("s5_sig", fn(s5sin[:, m * T:(m + 1) * T], ps[:, 4 + m, 0:T], ACT.Sigmoid, bias=pc("b_glu", m)))

            act.wait_ge(S["hg_lbx"], 1)
            tell("hg_lbe", fn(cols[:, 6:12], cols[:, 0:6], ACT.Exp))
            tell("hg_sig", fn(zt(ZF, HG), zt(ZF, HG), ACT.Sigmoid))
            tell("hg_silu", fn(zt(ZQ, HG), zt(ZQ, HG), ACT.Silu))
            step.link(fn(zt(ZG, HG), zt(ZG, HG), ACT.Silu))
            act.wait_ge(S["hg_f"], 1)
            tell("hg_ln", fn(hcum, hcum, ACT.Ln))
            for h in range(HG):
                act.wait_ge(S["hg_vt"], h + 1)
                if h:
                    act.wait_ge(S["hg_o"], h)
                tell("hg_vtc", fn(hvt, ps[:, 6, 0:T], ACT.Copy))
                act.wait_ge(S["hg_exp"], h + 1)
                tell("hg_decay", fn(hd, hd, ACT.Exp))
                read_outputs(PANELS["cx"] + 3 * h, ZC + 3 * h, 3, z, ZC + 3 * h)
            read_outputs(PANELS["if"], ZIF, 1, z, ZIF)
            act.wait_ge(S["hg_oc"], HG)
            tell("hg_sq", fn(zt(ZF, HG), yt(4, HG), ACT.Square))
            act.wait_ge(S["hg_ms"], 1)
            tell("hg_rt", fn(heq[:, 0:HG * T], heq[:, 0:HG * T], ACT.Sqrt))

            act.wait_ge(S["ml_conv"], 1)
            tell("ml_ca", fn(mca, mca, ACT.Silu))
            r1 = mrow[:, T:2 * T]
            act.wait_ge(S["ml_ax"], 1)
            tell("ml_e", fn(r1, r1, ACT.Exp, scale=-1.0))
            act.wait_ge(S["ml_e1"], 1)
            tell("ml_ln", fn(r1, r1, ACT.Ln))
            read_outputs(PANELS["ga"], ZGA, 8, z, ZGA)
            for c in range(2 * MH):
                h, half = c % MH, c // MH
                act.wait_ge(S["ml_qk"], c + 1)
                for mi, (tile, r0, rows, _) in enumerate(head_parts(h)):
                    x = ps[r0:r0 + rows, 4 + c % 4, mi * T:(mi + 1) * T]
                    dst = (mca[:, tile * T:(tile + 1) * T] if half else zt(ZC + tile))[r0:r0 + rows, :]
                    ins = fn(dst, x, ACT.Copy, scale=MD ** -0.5 if half else 1.0)
                    if mi == 0:
                        step.link(ins)
                    else:
                        tell("ml_qkc", ins)
            m3 = mvt.rearrange("p (b c) -> p b c", b=2)
            for k in range(HG):
                act.wait_ge(S["ml_vt"], k + 1)
                at = k // 3 * T
                tell("ml_vtc", fn(m3[:, :, k * P:(k + 1) * P], ps[:, 5 + k % 3, at:at + T].rearrange("p (b c) -> p b c", b=2), ACT.Copy))
            for h in range(MH):
                act.wait_ge(S["ml_x"], h + 1)
                step.link(fn(mx[:, 0:T], mx[:, 0:T], ACT.Exp, bias=macol[:, h:h + 1]))
                step.link(fn(mx[:, T:3 * P], mx[:, T:3 * P], ACT.Exp, bias=macol[:, MH + h:MH + h + 1]))
                tell("ml_w", fn(men, ps[:, 4, T:2 * T], ACT.Exp))
                read_outputs(PANELS["ga2"] + 6 * h, ZGA + 8 + 6 * h, 6, z, ZGA + 8 + 6 * h)
            act.wait_ge(S["ml_h"], 2 * MH)
            tell("ml_sq", fn(mca, yt(10, 6), ACT.Square))
            act.wait_ge(S["ml_ms"], 1)
            tell("ml_rt", fn(mvt[:, 0:MH * T], mvt[:, 0:MH * T], ACT.Sqrt))
            tell("ml_og", fn(zt(ZO, 6), zt(ZO, 6), ACT.Sigmoid))
            for k in range(4):
                ins = fn(zt(ZGA + 8 * k, 8), zt(ZGA + 8 * k, 8), ACT.Sigmoid)
                step.link(ins) if k < 3 else tell("sig_ab", ins)

            def gate(m, i=None):
                act.wait_ge(panel_done, PANELS["merge"] + 2 * m + 1 if i is None else i * 8 + (PANELS["merge"] + 2 * m + 1))
                if m >= 2:
                    act.wait_ge(S["branch_read"], m - 1 if i is None else i * 4 + (m - 1))
                evac.link(fn(mg[3 + m % 2], ps[:, (OUT["gc"] + m) % 4, 0:T], ACT.Sigmoid))

            for m in range(4):
                gate(m)
            with act.Fori(0, 3) as i:
                evac.enter(i, 4)
                for m in range(4, 8):
                    gate(m, i)
                evac.leave(3)
            act.wait_ge(evac_done, OUT["up"])
            squares(res, hn, KD)
            root(1)
            N["ff_silu"] = Count(act, S["ff_silu"])
            with act.Fori(0, FT // 2) as i:
                N["ff_silu"].enter(i, 2)
                for u in range(2):
                    act.wait_ge(evac_done, i * 4 + (OUT["up"] + 2 * u + 1))
                    tell("ff_silu", fn(fa, fa, ACT.Silu))
                N["ff_silu"].leave(FT // 2)
            act.wait_ge(S["res_done"], 8)
            squares(res, hn, KD)
            root(2)
            act.wait_ge(rms_out, 3)
            squares(res, hn, KD)
            root(3)

            evac.base, evac.k = OUT["in2"], 0
            read_outputs(PANELS["in2"], OUT["in2"], 17, z, 0)
            for r in range(2):
                squares(zt(8 + 4 * r, 4), sq[:, 4 * r * T:(4 * r + 4) * T], 4)
                root(4 + r)
            ang, _, cos, sin, _ = rope
            act.wait_ge(S["rp_angle"], 1)
            step.link(fn(cos, ang, ACT.Sin, scale=0.5))
            tell("rp_sin", fn(sin, ang, ACT.Sin))
            for r in range(2):
                act.wait_ge(S["at_qc"], 16 + 8 * r)
                if r:
                    act.wait_ge(S["at_ss"], 1)
                step.link(fn(sq, kn if r else qn, ACT.Square))
                if r:
                    tell("at_sq", fn(vsq[0:64, 0:T], zt(16)[0:64, :], ACT.Square))
                else:
                    tell("at_sq", fn(vsq[0:64, :], qrope[0:64, :], ACT.Square))
                act.wait_ge(S["at_ms"], r + 1)
                tell("at_rt", fn(rq, rq, ACT.Sqrt))
            for h in range(AH):
                u, k = h % 2, sm[:, 8 * h:8 * h + 8]
                act.wait_ge(S["at_mx"], h + 1)
                tell("at_e", fn(sc[u][:, 0:P], sc[u][:, 0:P], ACT.Exp, bias=k[:, 2:3], scale=192 ** -0.5, accum_out=k[:, 4:5]))
                tell("at_e", fn(sc[u][:, P:384], sc[u][:, P:384], ACT.Exp, bias=k[:, 3:4], scale=192 ** -0.5, accum_out=k[:, 5:6]))
                act.wait_ge(S["at_t"], h + 1)
                if h >= 2:
                    act.wait_ge(S["at_o"], h - 1)
                tell("at_tc", fn(pt[u], ps[:, 6, 0:384], ACT.Copy))
            act.wait_ge(evac_done, OUT["pq"])
            squares(res, hn, KD)
            root(6)
            evac.base, evac.k = OUT["pq"], 0
            read_outputs(PANELS["pq"], OUT["pq"], 16, q2, 0)
            for g in range(8):
                if g < 7:
                    act.wait_ge(S["pk_s"], g + 1)
                else:
                    act.wait_ge(panel_done, PANELS["subk"] + 1)
                tell("pk_sc", fn(s12[:, g * BANK:(g + 1) * BANK], ps[:, 4 + g % 4, :], ACT.Copy))

            def experts(e, count):
                with act.Fori(0, count // 4) as i:
                    evac.enter(i, 4)
                    for j in range(4):
                        act.wait_ge(panel_done, i * 4 + (PANELS["eu"] + e + j + 1))
                        evac.link(fn(A[:, bass.ds(i * (4 * T) + (e + j) * T, T)], ps[:, j, 0:T], ACT.Gelu_apprx_tanh))
                    evac.leave(count // 4)

            experts(0, 32)
            act.wait_ge(S["pk_g"], 1)
            tell("pk_e", fn(cval, cval, ACT.Exp))
            experts(32, 32)
            act.wait_ge(S["pk_tc"], 1)
            experts(64, 64)
            act.wait_ge(S["res_done"], 16)
            squares(res, hn, KD)
            root(7)

            def embed(m, i=None):
                v = (lambda c: c if i is None else i * 4 + c)
                act.wait_ge(panel_done, v(PANELS["pg"] + m + 1))
                if m >= 4:
                    act.wait_ge(S["out_ready"], v(m - 3))
                evac.link(fn(gt[:, m % 4 * T:(m % 4 + 1) * T], ps[:, m % 4, 0:T], ACT.Sigmoid))

            for m in range(4):
                embed(m)
            with act.Fori(0, 3) as i:
                evac.enter(i, 4)
                for m in range(4, 8):
                    embed(m, i)
                evac.leave(3)

        @block.gpsimd
        def _(pool):
            ek = Count(pool, S["hg_ek"])
            for h in range(HG):
                pool.wait_ge(S["hg_eq"], h + 1)
                ek.link(pool.tensor_tensor(hd.rearrange("p (l t) -> p l t", t=T), hd.rearrange("p (l t) -> p l t", t=T),
                                           hk[:, h * T:(h + 1) * T].unsqueeze(1).to_broadcast([P, 8, T]), ALU.mult))
            pool.wait_ge(S["merged_done"], KD)
            pool.dma_start(posi, pos).then_inc(pos_in, 16)
            o2 = Count(pool, S["oh2_done"])
            pool.wait_ge(S["pk_tc"], 1)

            def four(g, i=None):
                e = et[:, T + 4 * g:T + 4 * g + 4] if i is None else et[:, bass.ds(i * 8 + (T + 4 * g), 4)]
                if g >= 2:
                    pool.wait_ge(S["tok_mm"], 4 * g - 4 if i is None else i * 8 + (4 * g - 4))
                pstep.link(pool.tensor_copy(e4, e))
                pool.sem_inc(S["oh2_turn"], 1)
                for t in range(4):
                    c = (g % 2 * 4 + t) * P
                    o2.mark(pool.tensor_scalar(oh2[:, c:c + P], iota, e4[:, t:t + 1], None, ALU.is_equal))
                pool.wait_ge(o2.sem, o2.value())

            pstep, e4 = Count(pool, pool_step), cols[:, 32:36]
            for g in range(2):
                four(g)
            with pool.Fori(0, T // 8 - 1) as i:
                o2.enter(i, 8)
                pstep.enter(i, 2)
                for g in range(2, 4):
                    four(g, i)
                o2.leave(T // 8 - 1)
                pstep.leave(T // 8 - 1)
            pool.wait_ge(S["tok_mm"], T)
            pool.dma_start(pTs, pT).then_inc(p_in, 16)


def _tiles(v):
    return v.reshape(-1, P).T


def _columns(w, width=P):
    k, m = w.shape
    return w.reshape(k // P, P, m // width, width).transpose(2, 1, 0, 3).reshape(m // width, P, -1)


def _pack(blocks):
    a = blocks.transpose(1, 0, 2).reshape(P, -1)
    n = -(-a.shape[1] // D)
    out = np.zeros((n, P, D), a.dtype)
    for i in range(n):
        part = a[:, i * D:(i + 1) * D]
        out[i, :, :part.shape[1]] = part
    return out


def _layout(i):
    f32 = np.float32
    a = {k: np.asarray(v) for k, v in i.items()}
    a = {k: (v if k in ("x", "positions_2", "final_norm") else v[0]) for k, v in a.items()}
    stream = np.zeros((NPANELS, P, D), f32)

    def put(name, panels, at=0, step=1):
        n = PANELS[name] + at
        stream[n:n + step * len(panels):step] = panels

    w = a["w_in"]
    at = 0
    for name, n in (("u", 4), ("q", 6), ("f", 6), ("i", 6), ("og", 6), ("cx", 6), ("v", 6), ("o", 6)):
        put(name, _columns(w[:, at:at + n * P]))
        at += n * P
    gates = np.zeros((D, P), f32)
    gates[:, 0:4], gates[:, 32:36] = w[:, at:at + 4], w[:, at + 4:at + 8]
    put("if", _columns(gates))
    at += 8
    put("ga", _columns(w[:, at:at + D // 2]))
    put("ga2", _columns(w[:, at + D // 2:at + D]))
    put("gb", _columns(w[:, at + D:at + 2 * D]))
    put("merge", _columns(w[:, at + 2 * D:at + 3 * D]), 0, 2)
    put("merge", _columns(a["w_branch"]), 1, 2)
    b = np.zeros((2, P, 4, P), f32)
    c = np.zeros((2, P, 16, 32), f32)
    for k, (bn, cn) in enumerate((("s5_b_re", "s5_c_re"), ("s5_b_im", "s5_c_im"))):
        for g in range(32):
            j, gi = g // 2, g % 2
            r = 32 * (j % 4) + 16 * gi
            b[k, r:r + 16, j // 4, 64 * gi:64 * gi + 64] = a[bn][g].T
            c[k, 64 * gi:64 * gi + 64, j, 16 * gi:16 * gi + 16] = a[cn][g].T
    stream[PANELS["s5"]] = np.concatenate([b[0].reshape(P, -1), b[1].reshape(P, -1), c[0].reshape(P, -1), c[1].reshape(P, -1)], 1)
    put("glu", _pack(_columns(a["s5_w_glu"])))
    qk = np.zeros((32, P, P), f32)
    for h in range(MH):
        for half in range(2):
            for mi, (_, _, mr, m0) in enumerate(head_parts(h)):
                for ki, (_, k0, kr, c0) in enumerate(head_parts(h)):
                    qk[h * 8 + half * 4 + mi * 2 + ki, k0:k0 + kr, :mr] = \
                        a["ml_w_qk"][h, c0:c0 + kr, half * MD + m0:half * MD + m0 + mr]
    put("qk", _pack(qk))
    put("wout", _columns(a["w_out"]))
    f = FT * P
    put("up", _columns(a["ffn_w_up"][:, :f]), 0, 2)
    put("up", _columns(a["ffn_w_up"][:, f:]), 1, 2)
    put("down", a["ffn_w_down"].reshape(FT, P, D))
    w = a["w_in_2"]
    put("in2", _columns(w[:, :2048]))
    kr = np.zeros((D, P), f32)
    kr[:, :64] = w[:, 2048:]
    put("in2", _columns(kr), 16)
    wp = a["w_pool_2"].reshape(4, 2, P, 2, P)
    put("pool", _pack(wp.transpose(0, 3, 1, 2, 4).reshape(16, P, P)))
    uq = a["w_uq_2"].reshape(512, AH, 192)
    put("uq", _pack(_columns(uq[:, :, :P].reshape(512, -1))))
    put("uqr", _pack(_columns(uq[:, :, P:].reshape(512, -1), 64)))
    ukv = a["w_ukv_2"].reshape(512, AH, 256)
    put("ukn", _pack(_columns(ukv[:, :, :P].reshape(512, -1))))
    put("ukv", _columns(ukv[:, :, P:].reshape(512, -1), BANK))
    put("wout2", _columns(a["w_out_2"]))
    put("pq", _columns(a["w_pq_2"]))
    sk = np.stack([a["sub_k1_2"], a["sub_k2_2"]], 1).reshape(16, NK, P)
    put("subk", _pack(sk.transpose(0, 2, 1)))
    put("eu", _columns(a["expert_u_2"].T))
    put("ev", a["expert_v_2"].reshape(NK, P, D))
    put("pp", _pack(_columns(a["w_ple_proj_2"])))
    put("pg", _columns(a["w_ple_gate_2"]))

    par = np.zeros((P, NCOL), f32)

    def col(name, v, at=0):
        par[:v.shape[0], COL[name] + at:COL[name] + at + v.shape[1]] = v

    for name, src in (("mix", "mix_norm"), ("ffn", "ffn_norm"), ("final", "final_norm"), ("mix2", "mix_norm_gain_2"),
                      ("ffn2", "ffn_norm_gain_2"), ("ple", "ple_norm_gain_2"), ("s5_d", "s5_d"), ("b_glu", "s5_b_glu"),
                      ("hg_lb", "hg_lower_bounds"), ("hg_norm", "hg_norm"), ("conv_b", "ml_conv_b"), ("ml_norm", "ml_norm"),
                      ("pool_scale", "pool_scale_2"), ("q_lat", "q_lat_gain_2"), ("kv_lat", "kv_lat_gain_2")):
        col(name, _tiles(a[src]))
    col("lam_re", _tiles(a["s5_lam_re"].reshape(-1)))
    col("lam_im", _tiles(a["s5_lam_im"].reshape(-1)))
    col("log_dt", _tiles(np.repeat(a["s5_log_dt"], 64)))
    for t in range(4):
        col("conv_w", _tiles(a["ml_conv_w"][t]), 6 * t)
    col("b_ig", a["ml_b_ig"].reshape(4, 1))
    par[32:36, COL["b_fg"]] = a["ml_b_fg"]
    fc = np.concatenate([a["ffn_conv_w"], a["ffn_conv_b"][None]]).reshape(4, 2, FT, P)
    col("fconv", fc.transpose(3, 2, 1, 0).reshape(P, -1))
    for name, src in (("qn", "q_norm_gain_2"), ("kn", "k_norm_gain_2")):
        col(name + "_n", a[src][:P].reshape(P, 1))
        col(name + "_r", a[src][P:].reshape(64, 1))

    con = np.zeros((P, NCONST), f32)
    con[:, CC["ident"]:CC["ident"] + P] = np.eye(P)
    con[:, CC["ones"]:CC["ones"] + P] = 1
    con[:, CC["iota"]:CC["iota"] + P] = np.arange(P)
    con[:64, CC["invfreq"]] = np.tile(f32(10000.0) ** (-np.arange(0, 64, 2, dtype=f32) / f32(64)), 2)
    for m in range(32):
        con[m + 32, CC["perm"] + m] = -1
        con[m, CC["perm"] + m + 32] = 1
    mix = np.zeros((P, NMIX), f32)
    s, t = np.arange(P)[:, None], np.arange(P)[None]
    for l in range(8):
        m = 32 >> l if l < 6 else 64
        ok = (s // (2 * m) == t // (2 * m)) & (s % (2 * m) < m) & (t % (2 * m) >= m) if l < 7 else s == t
        mix[:, MC["hgmask"] + l * P:MC["hgmask"] + (l + 1) * P] = ok
    mix[:, MC["causal"]:MC["causal"] + P] = np.where(s <= t, 0, NEG)
    for h in range(MH):
        mix[h, MC["sel"] + h * P:MC["sel"] + (h + 1) * P] = 1
    mix[:, MC["tidx"]:MC["tidx"] + T] = np.arange(T)
    chunk = np.where(t // 64 <= s // 64, 0, NEG)
    mix[:, MC["chunkmask"]:MC["chunkmask"] + P] = chunk
    mix[:, MC["chunkmask"] + T:MC["chunkmask"] + T + P] = chunk
    for k in range(4):
        mix[:, MC["invcnt"] + k * T:MC["invcnt"] + (k + 1) * T] = 1 / np.minimum(np.arange(T) + 1, 2 << k).astype(f32)

    def channel_major(v):
        return np.ascontiguousarray(v.T.reshape(-1, P, T).transpose(1, 0, 2).reshape(P, -1))

    pos = np.ascontiguousarray(np.broadcast_to(a["positions_2"].astype(np.int32), (64, T)))
    return {"xT": channel_major(a["x"][0]), "stream": stream, "params": par, "consts": con, "mixc": mix,
            "pT": channel_major(a["p_2"][0]), "pos": pos}


_SHAPES = (("xT", (P, KD * T)), ("stream", (NPANELS, P, D)), ("params", (P, NCOL)), ("consts", (P, NCONST)),
           ("mixc", (P, NMIX)), ("pT", (P, 2 * T)), ("pos", (64, T)))


def kernel(**inputs):
    import concourse.bacc as _bacc
    from concourse.bass_utils import run_bass_kernel_spmd as _run

    nc = _bacc.Bacc("TRN2", target_bir_lowering=False, num_devices=1)
    args = [nc.dram_tensor(name, shape, I32 if name == "pos" else F32, kind="ExternalInput").ap() for name, shape in _SHAPES]
    args.append(nc.dram_tensor("outT", (P, KD * T), F32, kind="ExternalOutput").ap())
    two_blocks_kernel(nc, *args)
    r = _run(nc, [_layout(inputs)], core_ids=[0])
    out = r.results[0]["outT"]
    return np.ascontiguousarray(out.reshape(P, KD, T).transpose(2, 1, 0).reshape(1, T, D))
```

```python
from contextlib import ExitStack

import numpy as np

import concourse.bass as bass
from concourse import mybir

F32 = mybir.dt.float32
F32R = mybir.dt.float32r
I32 = mybir.dt.int32
U32 = mybir.dt.uint32
ALU = mybir.AluOpType
ACT = mybir.ActivationFunctionType
AX = mybir.AxisListType

P = 128
T = 256
D = 2048
KD = D // P
EPS = 1e-6
SLOTS = 2
QUARTER = D // 4
BANK = 512
S5_TILES = 16
HG = 6
MH, MD = 4, 192
FT = 44
AH = 8
PH = 8
TOPK = 16
NK = 128
NEG = -1e30
TWO_PI = 2 * np.pi
PI_A = 6.28125
PI_B = float(np.float32(np.round((TWO_PI - PI_A) * 2 ** 21) / 2 ** 21))
PI_C = float(np.float32(TWO_PI - PI_A - PI_B))
ROUND = 1.5 * 2 ** 23

GATES_1 = 13
GATES_HEAD = 3

PANELS = {}
_n = 0
for _name, _k in (("u", 4), ("s5", 1), ("q", 6), ("f", 6), ("i", 6), ("og", 6), ("cx", 2), ("glu", 1), ("cx2", 4),
                  ("v", 6), ("o", 6), ("if", 1), ("ga", GATES_1), ("qk", 2), ("ga2", 16 - GATES_1), ("gb", 16), ("merge", 32),
                  ("wout", 16), ("up", 2 * FT), ("down", FT), ("in2", 17), ("pool", 1), ("uq", 2),
                  ("uqr", 1), ("ukn", 2), ("ukv", 2), ("wout2", 16), ("pq", 16), ("subk", 1),
                  ("eu", NK), ("ev", NK), ("pp", 2), ("pg", 16)):
    PANELS[_name] = _n
    _n += _k
NPANELS = _n


def _runs():
    names, runs = list(PANELS) + [None], []
    for a, b in zip(names, names[1:]):
        first, end, split = PANELS[a], NPANELS if b is None else PANELS[b], a in SPLIT
        if runs and runs[-1][2] == split:
            runs[-1] = (runs[-1][0], end, split)
        else:
            runs.append((first, end, split))
    return runs


ML_FIRST, ML_HEADS, ML_PER_HEAD, ML_ALL = 2, 7, 3, 19 + GATES_1


def ml_panel(j):
    return PANELS["cx"] + j if j < ML_FIRST else PANELS["cx2"] + j - ML_FIRST


SPLIT = ("wout", "up", "down", "in2", "wout2", "pq", "eu", "ev", "pg")
RUNS = _runs()


def split_index(n):
    return sum(min(n, end) - first for first, end, split in RUNS if split and first < n)


def is_split(n):
    return any(split and first <= n < end for first, end, split in RUNS)


def split_before(n):
    return max((m for m in range(n) if is_split(m)), default=None)


XQ = {name: 4 * k for k, name in enumerate(("merged", "ffn", "mix2", "y", "ffn2", "ple"))}

COL = {}
_n = 0
for _name, _k in (("mix", 16), ("ffn", 16), ("final", 16), ("mix2", 16), ("ffn2", 16), ("ple", 16),
                  ("lam_re", 16), ("lam_im", 16), ("log_dt", 16), ("s5_d", 4), ("b_glu", 4),
                  ("hg_lb", 6), ("hg_norm", 6), ("conv_w", 24), ("conv_b", 6), ("ml_norm", 6),
                  ("b_ig", 1), ("b_fg", 1), ("fconv", 8 * FT), ("pool_scale", 8), ("q_lat", 4),
                  ("kv_lat", 4), ("qn_n", 1), ("qn_r", 1), ("kn_n", 1), ("kn_r", 1)):
    COL[_name] = _n
    _n += _k
NCOL = _n

CC = {}
_n = 0
for _name, _k in (("ident", P), ("ones", P), ("iota", P), ("invfreq", 1), ("perm", 64)):
    CC[_name] = _n
    _n += _k
NCONST = _n
MC = {}
_n = 0
for _name, _k in (("hgmask", 8 * P), ("causal", P), ("sel", MH * P), ("tidx", T), ("chunkmask", 3 * P),
                  ("invcnt", 4 * T)):
    MC[_name] = _n
    _n += _k
NMIX = _n
ARENA1 = 35472
ARENA2 = 31376

OUT = {}
_n = 0
for _name, _k in (("z", 79), ("gc", 16), ("wout", 16), ("up", 2 * FT), ("in2", 17), ("wout2", 16),
                  ("pq", 16), ("eu", NK), ("pg", 16)):
    OUT[_name] = _n
    _n += _k


def head_parts(h):
    c, out = h * MD, []
    while c < (h + 1) * MD:
        n = min(P - c % P, (h + 1) * MD - c)
        out.append((c // P, c % P, n, c - h * MD))
        c += n
    return out


class Count:

    def __init__(self, eng, sem):
        self.eng, self.sem, self.base, self.i, self.per, self.k = eng, sem, 0, None, 0, 0

    def value(self):
        return self.base + self.k if self.i is None else self.i * self.per + (self.base + self.k)

    def mark(self, ins):
        ins.then_inc(self.sem, 1)
        self.k += 1

    def link(self, ins):
        self.mark(ins)
        self.eng.wait_ge(self.sem, self.value())

    def enter(self, i, per):
        self.base, self.k, self.i, self.per = self.base + self.k, 0, i, per

    def leave(self, times):
        assert self.k == self.per, (self.k, self.per)
        self.base, self.k, self.i = self.base + times * self.per, 0, None


def two_blocks_kernel(nc, xT, stream, params, consts, mixc, pT, pos, outT):
    ctx = ExitStack()
    with ctx:
        def sem(name):
            return ctx.enter_context(nc.semaphore(name))


        def sb(name, shape, dt=F32):
            return ctx.enter_context(nc.sbuf_tensor(name, shape, dt))

        ring = sb("ring", [P, SLOTS, D])
        par = sb("par", [P, NCOL])
        con = sb("con", [P, NCONST])
        rstd = sb("rstd", [P, T])
        cols = sb("cols", [P, 64])
        with nc.sbuf_tensor("hn1", [P, D * 2], F32) as hn1, nc.sbuf_tensor("spare1", [P, 4096], F32), \
                nc.sbuf_tensor("arena1", [P, ARENA1], F32) as arena1:
            pass
        with nc.sbuf_tensor("below_mixcon", [P, 8192 + 95 * T], F32), nc.sbuf_tensor("mixcon", [P, NMIX], F32) as mixcon:
            pass
        whi, wlo = (sb(name, [P, D], F32R) for name in ("whi", "wlo"))
        with nc.sbuf_tensor("parked", [P, 8192], F32) as parked:
            res2 = parked[:, 2 * T:2 * T + KD * T]
            pTs = parked[:, 28 * T:30 * T]
        xhi, xlo = (sb(name, [P, KD * T], F32R) for name in ("xhi", "xlo"))
        with nc.sbuf_tensor("arena3", [P, ARENA2 + KD * T], F32) as arena3:
            pass
        arena2 = sb("arena2", [P, ARENA2])
        res = sb("res", [P, KD * T])
        thi = [xhi[:, k * T:(k + 1) * T] for k in range(2)]
        tlo = [xlo[:, (14 + k) * T:(15 + k) * T] for k in range(2)]
        ps = ctx.enter_context(nc.psum_tensor("ps", [P, 8, BANK], F32))

        def area(at, n, parts=P):
            assert at + n <= ARENA1, (at, n)
            return arena1[0:parts, at:at + n]

        def area2(at, n, parts=P):
            assert at + n <= ARENA2, (at, n)
            return arena2[0:parts, at:at + n]

        def area3(at, n, parts=P):
            assert at + n <= ARENA2 + KD * T, (at, n)
            return arena3[0:parts, at:at + n]

        def nx(n=KD):
            return area2(12288, n * T)

        Y0, W0 = 79 * T, 95 * T
        W1 = W0 + NMIX
        z = area(0, 79 * T)
        y = area(Y0, 16 * T)

        def zt(k, n=1):
            return z[:, k * T:(k + n) * T]

        def yt(k, n=1):
            return y[:, k * T:(k + n) * T]

        z2, y2 = area2(0, 17 * T), area2(W1 - 4096, KD * T)

        def z2t(k, n=1):
            return z2[:, k * T:(k + n) * T]

        def y2t(k, n=1):
            return y2[:, k * T:(k + n) * T]

        def pc(name, k=0, n=1):
            return par[:, COL[name] + k:COL[name] + k + n]

        def mc(name, n, k=0, parts=P):
            return mixcon[0:parts, MC[name] + k:MC[name] + k + n]

        ident, ones, iota = (con[:, CC[c]:CC[c] + P] for c in ("ident", "ones", "iota"))
        ZU, ZQ, ZF, ZI, ZG, ZC, ZV, ZO, ZIF, ZGA, ZGB = 0, 4, 10, 16, 22, 28, 34, 40, 46, 47, 63

        G4 = 4 * T
        s5s = area(W1, 16 * 16)
        s5b = area(W1 + 256, 1024)
        s5c = area(W1 + 1280, 1024)
        s5w = [area(W1 + 2304 + k * G4, G4) for k in range(5)]
        s5re, s5im, s5sin, s5cos, s5tmp = s5w
        hk = zt(ZF, HG)
        hcum = area(W1, HG * T)
        hd = area(W1 + 1536, 8 * T)
        heq = area(W1 + 3584, 8 * T)
        hmk = area(W1 + 5632, 8 * P)
        hvt = area(W1 + 6656, T)
        hms = area(W1 + 6912, 3 * P)
        mca = area(W1, HG * T)
        mvt = area(W1 + 1536, 2 * HG * P)
        mrow = area(W1 + 3072, 6 * T, 4)
        macol = area(W1 + 4608, 2 * MH)
        mx = area(W1 + 4616, 3 * P)
        mp = area(W1 + 5000, 3 * P)
        men = area(W1 + 5384, T)
        mden = area(W1 + 5640, T)
        merged = area(24 * T, KD * T)
        mg = [area(W1 + k * T, T) for k in range(6)]
        gff = area2(0, FT * T)
        fa, fb = area2(FT * T, T), area2(FT * T + T, T)
        at2 = 17 * T
        qn, kn, qrope, krope, rq, sq, vtm = (area2(at2 + k * 2048, 2048) for k in range(7))
        rope = [area2(at2 + 14336 + k * T, T, 64) for k in range(5)]
        posi = area2(at2 + 14336 + 5 * T, T, 64).bitcast(I32)
        pb = [qn, kn, qrope]
        W2 = W1 - 4096 + KD * T
        vsq = area2(W2, 2048)
        sc = [area2(W2 + k * 384, 384) for k in range(2)]
        pt = [area2(W2 + 768 + k * 384, 384) for k in range(2)]
        sm = area2(W2 + 1600, 8 * AH)
        A = area3(0, NK * T)
        q2 = area3(0, 16 * T)
        SCR = NK // 2 * T
        s12 = area3(SCR, 2 * 16 * NK)
        cand = area3(SCR + 4096, 2 * PH * 256)
        eqt = area3(SCR + 8192, 2048)
        val = area3(SCR + 10240, 512)
        vidx = area3(SCR + 10752, 512).bitcast(U32)
        vidf = area3(SCR + 11264, 512)
        cval = area3(SCR + 11776, 256)
        cidx = area3(SCR + 12032, 256).bitcast(U32)
        cdu = [area3(SCR + 12288 + 256 * k, 256).bitcast(U32) for k in range(2)]
        cdf = [area3(SCR + 12800 + 256 * k, 256) for k in range(2)]
        etm = area3(SCR + 13312, 3 * T)
        gsum = area3(SCR + 14080, 16)
        TAIL = NK * T
        et = area3(TAIL, 3 * T)
        oh1 = area3(TAIL + 768, 4 * P)
        oh2 = area3(TAIL + 1280, 8 * P)
        osq = area3(TAIL + 2304, 2 * P)
        ppj = area3(0, KD * T)
        gt = area3(4096, 4 * T)

        x_in, par_in, con_in, mix_in, pos_in, p_in, out_st = (sem(s) for s in (
            "x_in", "par_in", "con_in", "mix_in", "pos_in", "p_in", "out_st"))
        landed = [sem(f"landed{s}") for s in range(2 * SLOTS)]
        w_hi = sem("w_hi")
        w_lo_pool, w_lo_dve = sem("w_lo_pool"), sem("w_lo_dve")
        quarter_used = sem("quarter_used")
        x_hi = sem("x_hi")
        x_lo_pool, x_lo_dve = sem("x_lo_pool"), sem("x_lo_dve")
        tile_hi, tile_lo = sem("tile_hi"), sem("tile_lo")
        res_parked, res_back = sem("res_parked"), sem("res_back")
        panel_done = sem("panel_done")
        evac_done = sem("evac_done")
        rms_sq, rms_ss, rms_ms, rms_rt, rms_out = (sem(s) for s in (
            "rms_sq", "rms_ss", "rms_ms", "rms_rt", "rms_out"))
        dve_step, act_step, pool_step = sem("dve_step"), sem("act_step"), sem("pool_step")
        S = {k: sem(k) for k in (
            "s5_ldt", "s5_dt", "s5_mi", "s5_ma", "s5_bcopied", "s5_angle", "s5_sin", "s5_bu", "s5_state", "s5_y",
            "s5_pre", "s5_gelu", "s5_glu", "s5_sig", "ya_done",
            "hg_lbx", "hg_lbe", "hg_sig", "hg_silu", "hg_f", "hg_ln", "hg_exp", "hg_decay", "hg_eq", "hg_ek",
            "hg_sc", "hg_masked", "hg_vt", "hg_vtc", "hg_o", "hg_oc", "hg_sq", "hg_ss", "hg_ms", "hg_rt",
            "yb_done", "ml_conv", "ml_ca", "ml_qk", "ml_qkc", "ml_ax", "ml_e", "ml_e1", "ml_ln", "ml_rows",
            "ml_at", "ml_atc", "ml_vt", "ml_vtc", "ml_bc", "ml_x", "ml_w", "ml_sc", "ml_p", "ml_nd", "ml_h",
            "ml_sq", "ml_ss", "ml_ms", "ml_rt", "ml_og", "yc_done", "sig_ab", "branch_read", "merged_done",
            "ff_silu", "ff_out", "res_done",
            "po_d", "po_y", "po_yc", "rp_angle", "rp_sin", "at_q", "at_qc", "at_sq", "at_ss", "at_ms", "at_rt",
            "at_qn", "at_rot", "at_rotc", "at_done", "at_s", "at_mx", "at_e", "at_p", "at_t", "at_tc", "at_o", "at_oc",
            "pk_s", "pk_sc", "pk_g", "pk_e", "pk_et", "pk_t", "pk_tc", "oh1_done", "oh2_done", "oh2_turn", "oh2_act", "oh2_sq", "tok_mm", "tok_ev",
            "pp_out", "pp_ev", "out_ready")}

        def quarters(a, g):
            return a[:, g * QUARTER:(g + 1) * QUARTER]

        def turn(i, per, v):
            return v if i is None else i * per + v

        def wait_landed(eng, n, half, i=None, per=0):
            eng.wait_ge(landed[2 * (n % SLOTS) + half], turn(i, 16 * per // SLOTS, 16 * (n // SLOTS + 1)))

        def high_parts(act, n, i=None, per=0):
            s, before = split_index(n), split_before(n)
            for g in range(4):
                if g % 2 == 0:
                    wait_landed(act, n, g // 2, i, per)
                if before is not None and g < 3:
                    act.wait_ge(quarter_used, turn(i, 3 * per, 3 * (s - 1) + g + 1))
                elif before is not None:
                    act.wait_ge(panel_done, turn(i, per, before + 1))
                act.activation(quarters(whi, g), quarters(ring[:, n % SLOTS, :], g), ACT.Copy).then_inc(w_hi, 1)

        def rests(eng, n, i=None, per=0):
            first, done = (0, w_lo_pool) if eng is nc.gpsimd else (1, w_lo_dve)
            for g in (first, first + 2):
                eng.wait_ge(w_hi, turn(i, 4 * per, 4 * split_index(n) + g + 1))
                eng.tensor_tensor(quarters(wlo, g), quarters(ring[:, n % SLOTS, :], g), quarters(whi, g).bitcast(F32),
                                  ALU.subtract).then_inc(done, 1)

        def rests_loop(eng, n, count):
            turns = count // 4 if count >= 8 else 0
            if turns:
                with eng.Fori(0, turns) as i:
                    for j in range(4):
                        rests(eng, n + j, i, 4)
            for j in range(4 * turns, count):
                rests(eng, n + j)

        def x_high(act, name, q, src, i=None):
            c = slice(4 * q * T, 4 * (q + 1) * T) if i is None else bass.ds(i * (4 * T), 4 * T)
            act.activation(xhi[:, c], src[:, c], ACT.Copy).then_inc(x_hi, 1)

        def x_rest(eng, name, src, q):
            c = slice(4 * q * T, 4 * (q + 1) * T)
            eng.wait_ge(x_hi, XQ[name] + q + 1)
            eng.tensor_tensor(xlo[:, c], src[:, c], xhi[:, c].bitcast(F32), ALU.subtract) \
                .then_inc(x_lo_dve if q % 2 else x_lo_pool, 1)

        block = ctx.enter_context(nc.Block())

        @block.sync
        def _(sp):
            def fill(n, half=None, i=None):
                src = stream[n] if i is None else stream[bass.ds(i * 2 + n, 1)].rearrange("a p n -> p (a n)")
                for b in (0, 1) if half is None else (half,):
                    c = slice(b * D // 2, (b + 1) * D // 2)
                    sp.dma_start(ring[:, n % SLOTS, c], src[:, c]).then_inc(landed[2 * (n % SLOTS) + b], 16)

            def refill(n, split, i=None):
                if not split:
                    sp.wait_ge(panel_done, turn(i, 2, n - 1))
                    fill(n, None, i)
                    return
                for b in range(2):
                    v = turn(i, 4, 2 * split_index(n - 2) + b + 1)
                    sp.wait_ge(w_lo_pool, v)
                    sp.wait_ge(w_lo_dve, v)
                    fill(n, b, i)

            sp.dma_start(par[:], params).then_inc(par_in, 16)
            sp.dma_start(con[:], consts).then_inc(con_in, 16)
            sp.dma_start(res[:], xT).then_inc(x_in, 16)
            for n in range(SLOTS):
                fill(n)
            sp.dma_start(mixcon[:], mixc).then_inc(mix_in, 16)
            for first, end, split in RUNS:
                first, end = first + SLOTS, min(end + SLOTS, NPANELS)
                turns = (end - first) // 2 if end - first >= 4 else 0
                if turns:
                    with sp.Fori(0, turns) as i:
                        for n in range(first, first + 2):
                            refill(n, split, i)
                for n in range(first + 2 * turns, end):
                    refill(n, split)
            for q in range(4):
                sp.wait_ge(S["out_ready"], 4 * q + 4)
                sp.dma_start(outT[:, q * 4 * T:(q + 1) * 4 * T], res[:, q * 4 * T:(q + 1) * 4 * T]).then_inc(out_st, 16)
            sp.wait_ge(out_st, 64)
            sp.wait_ge(res_parked, 16)

        @block.tensor
        def _(pe):
            def arrive(n, i=None, per=0):
                for half in range(2):
                    wait_landed(pe, n, half, i, per)

            def slot(n, k, m=P, rows=slice(0, P)):
                return ring[rows, n % SLOTS, k * P:k * P + m]

            def project(n, p, src, i=None, pern=0, perp=0, norm=None):
                arrive(n, i, pern)
                if i is not None:
                    pe.wait_ge(evac_done, i * perp + (p - 3))
                elif p >= 4:
                    pe.wait_ge(evac_done, p - 3)
                for k in range(KD):
                    if norm is not None and k % 4 == 0:
                        pe.wait_ge(rms_out, 4 * norm + k // 4 + 1)
                    mm = pe.matmul(ps[:, p % 4, 0:T], slot(n, k), src[:, k * T:(k + 1) * T],
                                   start=(k == 0), stop=(k == KD - 1))
                mm.then_inc(panel_done, 1)

            def quarter_ready(n, g, i=None, per=0):
                pe.wait_ge((w_lo_pool, w_lo_dve)[g % 2], turn(i, 2 * per, 2 * split_index(n) + g // 2 + 1))

            def products(out, k, hi, lo, start, stop, **kw):
                b = slice(k * P, (k + 1) * P)
                pe.matmul(out, whi[:, b], hi, start=start, stop=False, **kw)
                pe.matmul(out, whi[:, b], lo, start=False, stop=False, **kw)
                return pe.matmul(out, wlo[:, b], hi, start=False, stop=stop, **kw)

            def project_split(n, p, name, i=None):
                pe.wait_ge(evac_done, turn(i, 4, p - 3))
                for g in range(4):
                    quarter_ready(n, g, i, 4)
                    if name:
                        pe.wait_ge((x_lo_pool, x_lo_dve)[g % 2], XQ[name] // 2 + g // 2 + 1)
                    for k in range(4 * g, 4 * g + 4):
                        t = slice(k * T, (k + 1) * T)
                        mm = products(ps[:, p % 4, 0:T], k, xhi[:, t], xlo[:, t], k == 0, k == KD - 1)
                    mm.then_inc(quarter_used if g < 3 else panel_done, 1)

            def split_loop(n, p, count, name=None):
                if name:
                    project_split(n, p, name)
                done = 1 if name else 0
                turns = (count - done) // 4
                with pe.Fori(0, turns) as i:
                    for j in range(done, done + 4):
                        project_split(n + j, p + j, None, i)
                for j in range(done + 4 * turns, count):
                    project_split(n + j, p + j, None)

            def project_loop(n, p, count, src, first=None):
                done = 4 if p == 0 else 0
                turns = (count - done) // 4
                for j in range(done):
                    project(n + j, p + j, src, norm=first if j == 0 else None)
                if turns > 1:
                    with pe.Fori(0, turns) as i:
                        for j in range(done, done + 4):
                            project(n + j, p + j, src, i, 4, 4)
                    done += 4 * turns
                for j in range(done, count):
                    project(n + j, p + j, src)

            def square_quarter(r, sq, tiles, q, bank=4, i=None):
                pe.wait_ge(rms_sq, turn(i, 1, 4 * r + q + 1))
                n = tiles // 4
                for k in range(n * q, n * q + n):
                    x = sq[:, k * T:(k + 1) * T] if i is None else sq[:, bass.ds(i * (n * T) + k * T, T)]
                    mm = pe.matmul(ps[:, bank, 0:T], ones, x, start=(k == 0), stop=(k == tiles - 1))
                if q == 3:
                    mm.then_inc(rms_ss, 1)

            def sum_squares(r, sq, tiles, bank=4):
                for q in range(4):
                    square_quarter(r, sq, tiles, q, bank)

            def split_residual(n, p, name, r):
                for j in range(6):
                    project_split(n + j, p + j, name if j == 0 else None)
                square_quarter(r, nx(), KD, 0)
                with pe.Fori(0, 2) as i:
                    for j in range(6, 10):
                        project_split(n + j, p + j, None, i)
                    square_quarter(r, nx(), KD, 1, i=i)
                for j in range(14, KD):
                    project_split(n + j, p + j, None)
                square_quarter(r, nx(), KD, 3)

            def accumulate_all(n, count, tiles_before):
                def one(k, i=None, first=False, end=False):
                    pe.wait_ge(tile_lo, turn(i, 4, tiles_before + k + 1))
                    for g in range(4):
                        quarter_ready(n + k, g, i, 4)
                        for m in range(4 * g, 4 * g + 4):
                            mm = products(ps[:, m // 2, (m % 2) * T:(m % 2 + 1) * T], m, thi[k % 2], tlo[k % 2],
                                          first and m % 2 == 0, end, skip_group_check=True)
                        mm.then_inc(quarter_used if g < 3 else panel_done, 1)
                one(0, first=True)
                turns = (count - 2) // 4
                with pe.Fori(0, turns) as i:
                    for k in range(1, 5):
                        one(k, i)
                for k in range(1 + 4 * turns, count):
                    one(k, end=(k == count - 1))

            pe.wait_ge(con_in, 16)
            sum_squares(0, hn1, KD)
            project_loop(PANELS["u"], 0, 4, hn1, first=0)
            pe.wait_ge(S["s5_bcopied"], 1)
            pe.wait_ge(panel_done, PANELS["s5"])
            pe.sem_inc(panel_done, 1)

            def s5_inputs(g):
                pe.wait_ge(evac_done, g + 1)
                if g:
                    pe.wait_ge(S["s5_pre"], g)
                for j in range(4):
                    rows = slice(32 * j, 32 * j + 32)
                    for c in range(2):
                        mm = pe.matmul(ps[:, 4 + j, c * T:(c + 1) * T], s5b[rows, c * 512 + g * P:c * 512 + (g + 1) * P],
                                       zt(ZU + g)[rows, :], start=True, stop=True, skip_group_check=True)
                mm.then_inc(S["s5_bu"], 1)

            def s5_outputs(g):
                pe.wait_ge(S["s5_state"], g + 1)
                for j in range(4):
                    out = ps[32 * j:32 * j + 32, 4, 0:T]
                    at = (4 * g + j) * 32
                    pe.matmul(out, s5c[:, at:at + 32], s5re[:, j * T:(j + 1) * T], start=True, stop=False)
                    mm = pe.matmul(out, s5c[:, 512 + at:512 + at + 32], s5im[:, j * T:(j + 1) * T], start=False, stop=True)
                mm.then_inc(S["s5_y"], 1)

            for g in range(4):
                s5_inputs(g)
                project_loop(PANELS["q"] + 6 * g, ZQ + 6 * g, 6, hn1)
                s5_outputs(g)
            project_loop(ml_panel(0), ZC, ML_FIRST, hn1)
            n = PANELS["glu"]
            arrive(n)
            pe.wait_ge(S["s5_gelu"], 4)
            for m in range(4):
                for k in range(4):
                    mm = pe.matmul(ps[:, 4 + m, 0:T], slot(n, 4 * m + k), yt(k), start=(k == 0), stop=(k == 3))
                mm.then_inc(S["s5_glu"] if m < 3 else panel_done, 1)

            def hg_values(h):
                if h == 0:
                    pe.wait_ge(evac_done, ZG)
                    pe.wait_ge(S["ya_done"], 1)
                else:
                    pe.wait_ge(S["hg_masked"], 3 * h)
                for b in range(2):
                    mm = pe.transpose(ps[:, 6, b * P:(b + 1) * P], zt(ZI + h)[:, b * P:(b + 1) * P], ident)
                mm.then_inc(S["hg_vt"], 1)

            def hg_scores(h):
                pe.wait_ge(S["hg_eq"], h + 1)
                pe.wait_ge(S["hg_ek"], h + 1)
                pe.wait_ge(S["hg_vtc"], h + 1)
                if h:
                    pe.wait_ge(S["hg_oc"], h)
                for b in range(2):
                    for l in range(8):
                        at = l * T + b * P
                        lhs, rhs = hd[:, at:at + P], heq[:, at:at + P]
                        if l == 7:
                            at = h * T + b * P
                            lhs, rhs = hk[:, at:at + P], zt(ZQ, HG)[:, at:at + P]
                        mm = pe.matmul(ps[:, 4 + 2 * b + l // 4, (l % 4) * P:(l % 4 + 1) * P], lhs, rhs,
                                       start=True, stop=True, skip_group_check=True)
                    mm.then_inc(S["hg_sc"], 1)
                pe.wait_ge(S["hg_masked"], 3 * h + 1)
                pe.matmul(ps[:, 4, 0:P], hd[:, 7 * T:7 * T + P], heq[:, 7 * T + P:8 * T], start=True, stop=True) \
                    .then_inc(S["hg_sc"], 1)

            def hg_output(h):
                pe.wait_ge(S["hg_masked"], 3 * h + 3)
                pe.matmul(ps[:, 5, 0:P], hvt[:, 0:P], hms[:, 0:P], start=True, stop=True, skip_group_check=True)
                pe.matmul(ps[:, 5, P:T], hvt[:, P:T], hms[:, P:T], start=True, stop=False, skip_group_check=True)
                pe.matmul(ps[:, 5, P:T], hvt[:, 0:P], hms[:, T:T + P], start=False, stop=True,
                          skip_group_check=True).then_inc(S["hg_o"], 1)

            project_loop(ml_panel(ML_FIRST), ZC + ML_FIRST, ML_HEADS - ML_FIRST, hn1)
            for h in range(HG):
                hg_values(h)
                hg_scores(h)
                j = ML_HEADS + ML_PER_HEAD * h
                project_loop(ml_panel(j), ZC + j, ML_PER_HEAD, hn1)
                hg_output(h)
            j = ML_HEADS + ML_PER_HEAD * HG
            project_loop(ml_panel(j), ZC + j, 3, hn1)
            pe.wait_ge(S["hg_sq"], 1)
            for h in range(HG):
                mm = pe.matmul(ps[:, 4 + h // 2, (h % 2) * T:(h % 2 + 1) * T], ones, zt(ZF + h), start=True, stop=True,
                               skip_group_check=True)
            mm.then_inc(S["hg_ss"], 1)

            project_loop(ml_panel(j + 3), ZC + j + 3, ML_ALL - j - 3, hn1)
            pe.wait_ge(S["ml_ca"], 1)
            pe.wait_ge(S["yb_done"], 1)
            for c in range(2 * MH):
                h, half = c % MH, c // MH
                n = PANELS["qk"] + h // 2
                arrive(n)
                if c >= 4:
                    pe.wait_ge(S["ml_qkc"], c - 3)
                for mi, (tile, r0, rows, _) in enumerate(head_parts(h)):
                    for ki, (kt, k0, kr, _) in enumerate(head_parts(h)):
                        blk = (h % 2) * 8 + half * 4 + mi * 2 + ki
                        mm = pe.matmul(ps[r0:r0 + rows, 4 + c % 4, mi * T:(mi + 1) * T],
                                       slot(n, blk, rows, slice(k0, k0 + kr)), mca[k0:k0 + kr, kt * T:(kt + 1) * T],
                                       start=(ki == 0), stop=(ki == 1), skip_group_check=True)
                mm.then_inc(S["ml_qk"], 1)
            pe.wait_ge(S["ml_qk"], 2 * MH)
            pe.sem_inc(panel_done, 2)
            pe.wait_ge(S["ml_qkc"], 2 * MH)
            pe.wait_ge(S["ml_rows"], 1)
            for b in range(2):
                mm = pe.transpose(ps[:, 4, b * MH:(b + 1) * MH], mrow[:, 2 * T + b * P:2 * T + (b + 1) * P], ident[0:MH, 0:MH])
            mm.then_inc(S["ml_at"], 1)
            for k in range(HG):
                at = k // 3 * T
                if k >= 3:
                    pe.wait_ge(S["ml_vtc"], k - 2)
                for b in range(2):
                    mm = pe.transpose(ps[:, 5 + k % 3, at + b * P:at + (b + 1) * P], zt(ZV + k)[:, b * P:(b + 1) * P], ident)
                mm.then_inc(S["ml_vt"], 1)
            pe.wait_ge(S["ml_vtc"], HG)
            pe.wait_ge(S["ml_atc"], 1)

            def ml_scores(h):
                if h:
                    pe.wait_ge(S["ml_w"], h)
                    pe.wait_ge(S["ml_p"], h)
                sel = mc("sel", P, h * P, MH)
                pe.matmul(ps[:, 4, 0:T], sel, mrow[:, 4 * T:5 * T], start=True, stop=True, skip_group_check=True)
                pe.matmul(ps[:, 4, T:2 * T], sel, mrow[:, 5 * T:6 * T], start=True, stop=True,
                          skip_group_check=True).then_inc(S["ml_bc"], 1)
                for b in range(2):
                    for ki, (kt, k0, kr, _) in enumerate(head_parts(h)):
                        mm = pe.matmul(ps[:, 5, b * T:b * T + T - b * P],
                                       mca[k0:k0 + kr, kt * T + b * P:kt * T + (b + 1) * P],
                                       zt(ZC + kt)[k0:k0 + kr, b * P:T], start=(ki == 0), stop=(ki == 1),
                                       skip_group_check=True)
                mm.then_inc(S["ml_sc"], 1)

            def ml_sums(h):
                pe.wait_ge(S["ml_p"], h + 1)
                pe.matmul(ps[:, 6, 0:T], ones, mp[:, 0:T], start=True, stop=False, skip_group_check=True)
                pe.matmul(ps[:, 6, P:T], ones, mp[:, T:3 * P], start=False, stop=True, skip_group_check=True)
                for mi, (tile, r0, rows, _) in enumerate(head_parts(h)):
                    c = tile * P + r0
                    pe.matmul(ps[r0:r0 + rows, 7, mi * T:(mi + 1) * T], mvt[:, c:c + rows], mp[:, 0:T],
                              start=True, stop=False, skip_group_check=True)
                    mm = pe.matmul(ps[r0:r0 + rows, 7, mi * T + P:(mi + 1) * T], mvt[:, HG * P + c:HG * P + c + rows],
                                   mp[:, T:3 * P], start=False, stop=True, skip_group_check=True)
                mm.then_inc(S["ml_nd"], 1)

            def gates(j, count):
                project_loop(PANELS["ga2"] + j, ZGA + GATES_1 + j, count, hn1)

            for h in range(MH):
                ml_scores(h)
                gates(GATES_HEAD * h, GATES_HEAD)
                ml_sums(h)
            gates(GATES_HEAD * MH, 3)
            pe.wait_ge(S["ml_sq"], 1)
            for h in range(MH):
                for ki, (kt, k0, kr, _) in enumerate(head_parts(h)):
                    mm = pe.matmul(ps[:, 4 + h, 0:T], ones[k0:k0 + kr, :],
                                   mca[k0:k0 + kr, kt * T:(kt + 1) * T], start=(ki == 0), stop=(ki == 1),
                                   skip_group_check=True)
            mm.then_inc(S["ml_ss"], 1)
            gates(GATES_HEAD * MH + 3, 32 - GATES_1 - GATES_HEAD * MH - 3)

            def merge(m, i=None):
                n = PANELS["merge"] + 2 * m
                project(n, OUT["gc"] + m, hn1, i, 8, 4)
                arrive(n + 1, i, 8)
                if m == 0:
                    pe.wait_ge(S["yc_done"], 1)
                if m >= 2:
                    pe.wait_ge(S["branch_read"], m - 1 if i is None else i * 4 + (m - 1))
                for k in range(KD):
                    part = 0 if k < 4 else 1 if k < 10 else 2
                    mm = pe.matmul(ps[:, 4 + 2 * (m % 2) + part // 2, (part % 2) * T:(part % 2 + 1) * T], slot(n + 1, k),
                                   yt(k), start=k in (0, 4, 10), stop=k in (3, 9, 15), skip_group_check=True)
                mm.then_inc(panel_done, 1)

            for m in range(4):
                merge(m)
            with pe.Fori(0, 3) as i:
                for m in range(4, 8):
                    merge(m, i)
            split_residual(PANELS["wout"], OUT["wout"], "merged", 1)

            split_loop(PANELS["up"], OUT["up"], 2 * FT, "ffn")
            pe.wait_ge(S["ff_out"], FT)
            pe.wait_ge(evac_done, OUT["in2"])
            accumulate_all(PANELS["down"], FT, 0)
            sum_squares(2, nx(), KD, 0)
            sum_squares(3, nx(), KD)

            split_loop(PANELS["in2"], OUT["in2"], 17, "mix2")
            n = PANELS["pool"]
            arrive(n)
            pe.wait_ge(S["po_d"], 1)
            for c in range(8):
                if c >= 4:
                    pe.wait_ge(S["po_yc"], c - 3)
                for k in range(2):
                    mm = pe.matmul(ps[:, 4 + c % 4, 0:T], slot(n, 2 * c + k), pb[2][:, (c // 2 * 2 + k) * T:(c // 2 * 2 + k + 1) * T],
                                   start=(k == 0), stop=(k == 1))
                mm.then_inc(S["po_y"] if c < 7 else panel_done, 1)
            pe.wait_ge(S["po_yc"], 8)
            sum_squares(4, sq, 4)
            sum_squares(5, sq[:, 4 * T:8 * T], 4, 5)
            pe.wait_ge(rms_out, 24)
            o = 0

            def small(n, blocks, src, m=P, width=P, last=False):
                nonlocal o
                if o >= 4:
                    pe.wait_ge(S["at_qc"], o - 3)
                for k in range(4):
                    at = (blocks * 4 + k) * width
                    mm = pe.matmul(ps[0:m, 4 + o % 4, 0:T], ring[:, n % SLOTS, at:at + m], src[:, k * T:(k + 1) * T],
                                   start=(k == 0), stop=(k == 3))
                mm.then_inc(S["at_q"], 1)
                o += 1
                if last:
                    pe.wait_ge(S["at_q"], o)
                    pe.sem_inc(panel_done, 1)

            for h in range(AH):
                arrive(PANELS["uq"] + h // 4)
                small(PANELS["uq"] + h // 4, h % 4, z2t(8, 4), last=h % 4 == 3)
            arrive(PANELS["uqr"])
            for h in range(AH):
                small(PANELS["uqr"], h, z2t(8, 4), m=64, width=64, last=h == 7)
            def head_sums(r):
                pe.wait_ge(S["at_sq"], r + 1)
                for h in range(AH):
                    out = ps[:, 4 * r + h // 2, (h % 2) * T:(h % 2 + 1) * T]
                    c = h * T if r == 0 else 0
                    pe.matmul(out, ones, sq[:, h * T:(h + 1) * T], start=True, stop=False, skip_group_check=True)
                    mm = pe.matmul(out, ones[0:64, :], vsq[0:64, c:c + T], start=False, stop=True, skip_group_check=True)
                mm.then_inc(S["at_ss"], 1)

            def other_half(r):
                pe.wait_ge(S["at_qn"], r + 1)
                perm = con[0:64, CC["perm"]:CC["perm"] + 64]
                if r == 0:
                    for c in range(4):
                        mm = pe.matmul(ps[0:64, c, :], perm, qrope[0:64, c * BANK:(c + 1) * BANK], start=True, stop=True)
                else:
                    mm = pe.matmul(ps[0:64, 4, 0:T], perm, rope[4], start=True, stop=True)
                mm.then_inc(S["at_rot"], 1)

            pe.wait_ge(evac_done, OUT["wout2"])
            for h in range(AH):
                arrive(PANELS["ukn"] + h // 4)
                small(PANELS["ukn"] + h // 4, h % 4, z2t(12, 4), last=h % 4 == 3)
                if h == 3:
                    head_sums(0)
            for c in range(2):
                n = PANELS["ukv"] + c
                arrive(n)
                for b in range(2):
                    pe.wait_ge(S["at_qc"], o - 3)
                    for k in range(4):
                        at = (12 + k) * T + b * P
                        mm = pe.matmul(ps[:, 4 + o % 4, :], z2[:, at:at + P], ring[:, n % SLOTS, k * BANK:(k + 1) * BANK],
                                       start=(k == 0), stop=(k == 3))
                    mm.then_inc(S["at_q"], 1)
                    o += 1
                pe.wait_ge(S["at_q"], o)
                pe.sem_inc(panel_done, 1)
            other_half(0)
            pe.wait_ge(S["at_qc"], o)
            head_sums(1)
            other_half(1)
            pe.wait_ge(S["at_done"], 1)

            def at_scores(h):
                u = h % 2
                if h >= 2:
                    pe.wait_ge(S["at_e"], 2 * h - 2)
                q, k, qq, kk = (a[:, h * T:(h + 1) * T] for a in (qn, kn, qrope, krope))
                bank = ps[:, 4 + u, :]
                for b in range(2):
                    out = bank[:, b * P:b * P + P + b * P]
                    pe.matmul(out, q[:, b * P:(b + 1) * P], k[:, 0:P + b * P], start=True, stop=False, skip_group_check=True)
                    mm = pe.matmul(out, qq[0:64, b * P:(b + 1) * P], kk[0:64, 0:P + b * P], start=False, stop=True,
                                   skip_group_check=True)
                mm.then_inc(S["at_s"], 1)

            def at_values(h):
                u = h % 2
                pe.wait_ge(S["at_p"], h + 1)
                if h:
                    pe.wait_ge(S["at_tc"], h)
                for c in range(3):
                    mm = pe.transpose(ps[:, 6, c * P:(c + 1) * P], sc[u][:, c * P:(c + 1) * P], ident)
                mm.then_inc(S["at_t"], 1)
                pe.wait_ge(S["at_tc"], h + 1)
                if h:
                    pe.wait_ge(S["at_oc"], h)
                pe.matmul(ps[:, 7, 0:T], vtm[:, h * P:(h + 1) * P], pt[u][:, 0:T], start=True, stop=False, skip_group_check=True)
                pe.matmul(ps[:, 7, P:T], vtm[:, 1024 + h * P:1024 + (h + 1) * P], pt[u][:, T:3 * P], start=False, stop=True,
                          skip_group_check=True).then_inc(S["at_o"], 1)

            at_scores(0)
            for h in range(AH):
                if h + 1 < AH:
                    at_scores(h + 1)
                at_values(h)
            split_residual(PANELS["wout2"], OUT["wout2"], "y", 6)

            split_loop(PANELS["pq"], OUT["pq"], KD, "ffn2")
            n = PANELS["subk"]
            arrive(n)
            for b in range(2):
                if b:
                    pe.wait_ge(S["pk_sc"], 4)
                for c in range(16):
                    if c % 4 == 0 and b == 0:
                        pe.wait_ge(evac_done, OUT["eu"])
                    mm = pe.matmul(ps[:, 4 + c // 4, (c % 4) * P:(c % 4 + 1) * P], q2[:, c * T + b * P:c * T + (b + 1) * P],
                                   slot(n, c), start=True, stop=True, skip_group_check=True)
                    if c % 4 == 3 and (b, c) != (1, 15):
                        mm.then_inc(S["pk_s"], 1)
            mm.then_inc(panel_done, 1)
            split_loop(PANELS["eu"], OUT["eu"], NK // 2)
            pe.wait_ge(S["pk_et"], 1)
            for k in range(3):
                for b in range(2):
                    mm = pe.transpose(ps[:, 4 + k, b * P:(b + 1) * P], etm[:, k * T + b * P:k * T + (b + 1) * P], ident)
            mm.then_inc(S["pk_t"], 1)
            split_loop(PANELS["eu"] + NK // 2, OUT["eu"] + NK // 2, NK // 2)
            pe.wait_ge(S["pk_tc"], 1)

            def token(t, i=None):
                v = (lambda c: c if i is None else i * 16 + c)
                pe.wait_ge(S["oh1_done"], v(t + 1))
                if t % 4 < 2:
                    pe.wait_ge(S["oh2_done"], turn(i, 8, t // 4 * 2 + t % 4 + 1))
                else:
                    pe.wait_ge(S["oh2_act"], turn(i, 4, t // 4 + 1))
                if t % 4 == 0 and t >= 16:
                    pe.wait_ge(S["tok_ev"], t // 4 - 3 if i is None else i * 4 + (t // 4 - 3))
                pe.matmul(ps[:, 4 + t // 4 % 4, (t % 4) * P:(t % 4 + 1) * P], oh2[:, (t % 8) * P:(t % 8 + 1) * P],
                          oh1[:, (t % 4) * P:(t % 4 + 1) * P], start=True, stop=True, skip_group_check=True) \
                    .then_inc(S["tok_mm"], 1)

            for t in range(16):
                token(t)
            with pe.Fori(0, T // 16 - 1) as i:
                for t in range(16, 32):
                    token(t, i)
            pe.wait_ge(S["tok_ev"], T // 4)
            accumulate_all(PANELS["ev"], NK, FT)

            pe.wait_ge(S["res_done"], 16)
            pe.wait_ge(p_in, 16)
            for half in range(2):
                n = PANELS["pp"] + half
                arrive(n)
                if half:
                    sum_squares(7, nx(), KD)
                    pe.wait_ge(rms_ms, 8)
                for m in range(8 * half, 8 * half + 8):
                    for k in range(2):
                        mm = pe.matmul(ps[:, m // 2, (m % 2) * T:(m % 2 + 1) * T], slot(n, m % 8 * 2 + k), pTs[:, k * T:(k + 1) * T],
                                       start=(k == 0), stop=(k == 1), skip_group_check=True)
                mm.then_inc(panel_done, 1)
            pe.wait_ge(S["pp_ev"], 4)
            split_loop(PANELS["pg"], OUT["pg"], KD, "ple")

        @block.vector
        def _(dve):
            step = Count(dve, dve_step)
            evac = Count(dve, evac_done)
            L = step.link
            N = {}

            def tell(name, ins):
                if name not in N:
                    N[name] = Count(dve, S[name])
                N[name].link(ins)

            def tt(out, a, b, op):
                return dve.tensor_tensor(out, a, b, op)

            def ts(out, a, s1, s2, op0, op1=None):
                return dve.tensor_scalar(out, a, s1, s2, op0) if op1 is None else dve.tensor_scalar(out, a, s1, s2, op0, op1)

            def stt(out, a, s, b, op0, op1):
                return dve.scalar_tensor_tensor(out, a, s, b, op0, op1)

            rms_c = {k: Count(dve, s) for k, s in (("ms", rms_ms), ("out", rms_out))}

            def normalise(r, src, dst, gain, tiles, bank=4):
                dve.wait_ge(rms_ss, r + 1)
                rms_c["ms"].link(ts(rstd[:], ps[:, bank, 0:T], 1.0 / (tiles * P), EPS, ALU.mult, ALU.add))
                dve.wait_ge(rms_rt, r + 1)
                L(dve.reciprocal(rstd[:], rstd[:]))
                for k in range(tiles):
                    c = slice(k * T, (k + 1) * T)
                    last = stt(dst[:, c], src[:, c], pc(gain, k), rstd[:], ALU.mult, ALU.mult)
                    if (k + 1) % (tiles // 4) == 0:
                        rms_c["out"].link(last)
                    else:
                        step.mark(last)

            def reduce_angle(ang, turns):
                L(ts(turns, ang, 1 / TWO_PI, ROUND, ALU.mult, ALU.add))
                L(ts(turns, turns, ROUND, None, ALU.subtract))
                for part in (PI_A, PI_B, PI_C):
                    L(stt(ang, turns, -part, ang, ALU.mult, ALU.add))
                return ts(ang, ang, 3.1415925, -3.1415925, ALU.min, ALU.max)

            def add_residual(p, count):
                for j in range(4):
                    evac_add(p + j, j)
                with dve.Fori(0, count // 4 - 1) as i:
                    evac.enter(i, 4)
                    for j in range(4, 8):
                        evac_add(p + j, j, i)
                    evac.leave(count // 4 - 1)

            def evac_add(p, j, i=None):
                n = panel_of(p)
                rests(dve, n + 1, i, 4)
                dve.wait_ge(panel_done, turn(i, 4, n + 1))
                c = res[:, j * T:(j + 1) * T] if i is None else res[:, bass.ds(i * (4 * T) + j * T, T)]
                evac.link(tt(c, c, ps[:, p % 4, 0:T], ALU.add))

            def panel_of(p):
                return p - OUT["wout"] + PANELS["wout"] if p < OUT["up"] else p - OUT["wout2"] + PANELS["wout2"]

            dve.wait_ge(par_in, 16)
            dve.wait_ge(x_in, 16)
            s = [s5s[:, 16 * k:16 * k + 16] for k in range(16)]
            lr, li = pc("lam_re", 0, 16), pc("lam_im", 0, 16)
            dve.wait_ge(S["s5_dt"], 1)
            L(tt(s[1], lr, s[0], ALU.mult))
            L(tt(s[2], li, s[0], ALU.mult))
            tell("s5_mi", reduce_angle(s[2], s[5]))
            normalise(0, res, hn1, "mix", KD)
            dve.wait_ge(S["s5_ma"], 1)
            L(stt(s[5], s[3], -2.0, s[3], ALU.mult, ALU.mult))
            L(ts(s[5], s[5], 1.0, None, ALU.add))
            L(tt(s[6], s[1], s[4], ALU.mult))
            L(tt(s[5], s[1], s[5], ALU.mult))
            L(ts(s[7], s[5], -1.0, None, ALU.add))
            L(tt(s[8], lr, lr, ALU.mult))
            L(tt(s[9], li, li, ALU.mult))
            L(tt(s[8], s[8], s[9], ALU.add))
            L(dve.reciprocal(s[8], s[8]))
            for out, a, b, op in ((s[9], s[7], s[6], ALU.add), (s[10], s[6], s[7], ALU.subtract)):
                L(tt(s[11], a, lr, ALU.mult))
                L(tt(s[12], b, li, ALU.mult))
                L(tt(out, s[11], s[12], op))
                L(tt(out, out, s[8], ALU.mult))
            n = PANELS["s5"]
            for half in range(2):
                wait_landed(dve, n, half)
            L(dve.tensor_copy(s5b, ring[:, n % SLOTS, 0:1024]))
            cre, cim = (ring[:, n % SLOTS, 1024 + 512 * k:1536 + 512 * k].rearrange("p (t c) -> p t c", c=32) for k in range(2))
            fr, fi = (s[k].unsqueeze(2).to_broadcast([P, 16, 32]) for k in (9, 10))
            ta, tb = (s5tmp[:, 512 * k:512 * k + 512].rearrange("p (t c) -> p t c", c=32) for k in range(2))
            o1, o2 = (s5c[:, 512 * k:512 * k + 512].rearrange("p (t c) -> p t c", c=32) for k in range(2))
            L(tt(ta, cre, fr, ALU.mult))
            L(tt(tb, cim, fi, ALU.mult))
            L(tt(o1, ta, tb, ALU.subtract))
            L(tt(ta, cre, fi, ALU.mult))
            L(tt(tb, cim, fr, ALU.mult))
            L(stt(s5c[:, 512:1024], s5tmp[:, 0:512], -1.0, s5tmp[:, 512:1024], ALU.mult, ALU.subtract))
            tell("s5_bcopied", dve.tensor_copy(s5tmp[:, 0:1], s5c[:, 0:1]))

            dve.wait_ge(mix_in, 16)
            vr, vi = (ps[:, 4:8, k * T:(k + 1) * T] for k in range(2))

            def quad(a):
                return a.rearrange("p (t c) -> p t c", c=T)

            for g in range(4):
                for j in range(4):
                    L(ts(s5re[:, j * T:(j + 1) * T], mc("tidx", T), s[2][:, 4 * g + j:4 * g + j + 1], None, ALU.mult))
                tell("s5_angle", reduce_angle(s5re, s5im))
                dve.wait_ge(S["s5_sin"], g + 1)
                L(stt(s5cos, s5tmp, -2.0, s5tmp, ALU.mult, ALU.mult))
                L(ts(s5cos, s5cos, 1.0, None, ALU.add))
                dve.wait_ge(S["s5_bu"], g + 1)
                L(tt(quad(s5re), vr, quad(s5cos), ALU.mult))
                L(tt(quad(s5tmp), vi, quad(s5sin), ALU.mult))
                L(tt(s5re, s5re, s5tmp, ALU.add))
                L(tt(quad(s5im), vi, quad(s5cos), ALU.mult))
                L(tt(quad(s5tmp), vr, quad(s5sin), ALU.mult))
                L(tt(s5im, s5im, s5tmp, ALU.subtract))
                for w in (s5re, s5im):
                    for j in range(4):
                        c = w[:, j * T:(j + 1) * T]
                        mag = s[1][:, 4 * g + j:4 * g + j + 1].to_broadcast([P, T])
                        L(dve.tensor_tensor_scan(c, mag, c, 0.0, ALU.mult, ALU.add))
                L(tt(s5tmp, s5re, s5sin, ALU.mult))
                L(tt(s5re, s5re, s5cos, ALU.mult))
                L(tt(s5sin, s5im, s5sin, ALU.mult))
                L(tt(s5re, s5re, s5sin, ALU.subtract))
                L(tt(s5im, s5im, s5cos, ALU.mult))
                tell("s5_state", tt(s5im, s5im, s5tmp, ALU.add))
                dve.wait_ge(S["s5_y"], g + 1)
                tell("s5_pre", stt(s5tmp[:, 0:T], zt(ZU + g), pc("s5_d", g), ps[:, 4, 0:T], ALU.mult, ALU.add))
            dve.wait_ge(S["s5_sig"], 4)
            tell("ya_done", tt(yt(0, 4), yt(0, 4), s5sin, ALU.mult))

            c6 = [cols[:, 6 * k:6 * k + 6] for k in range(5)]
            tell("hg_lbx", tt(c6[0], pc("hg_lb", 0, 6), pc("hg_lb", 0, 6), ALU.subtract))
            dve.wait_ge(S["hg_lbe"], 1)
            L(dve.reciprocal(c6[2], c6[1]))
            L(tt(c6[2], c6[2], c6[1], ALU.mult))
            L(tt(c6[3], c6[2], c6[2], ALU.subtract))
            L(ts(c6[4], c6[3], -1.0, 1.0, ALU.mult, ALU.add))
            dve.wait_ge(S["hg_sig"], 1)
            for h in range(HG):
                L(ts(zt(ZF + h), zt(ZF + h), c6[4][:, h:h + 1], c6[3][:, h:h + 1], ALU.mult, ALU.add))
            tell("hg_f", ts(hcum, hk, 2.0 ** -63, None, ALU.max))
            L(ts(hk, hk, -1.0, 1.0, ALU.mult, ALU.add))
            dve.wait_ge(S["hg_ln"], 1)
            one = ones[:, 0:1].to_broadcast([P, 64])
            for c in range(HG * 4):
                w = hcum[:, 64 * c:64 * c + 64]
                L(dve.tensor_tensor_scan(w, one, w, 0.0, ALU.mult, ALU.add))
            dve.wait_ge(S["hg_silu"], 1)

            def decays(h):
                cum = hcum[:, h * T:(h + 1) * T]
                for l in range(7):
                    m = 32 >> l if l < 6 else 64
                    v = cum.rearrange("p (a b m) -> p a b m", b=2, m=m)
                    d = hd[:, l * T:(l + 1) * T].rearrange("p (a b m) -> p a b m", b=2, m=m)
                    ref = v[:, :, 0, m - 1:m].to_broadcast([P, T // (2 * m), m])
                    if l < 6:
                        step.mark(tt(d[:, :, 1, :], v[:, :, 1, :], ref, ALU.subtract))
                    else:
                        step.mark(dve.tensor_copy(d[:, :, 1, :], v[:, :, 1, :]))
                    step.mark(tt(d[:, :, 0, :], ref, v[:, :, 0, :], ALU.subtract))
                d = hd[:, 7 * T:8 * T]
                step.mark(dve.tensor_copy(d[:, 128:192], cum[:, 128:192]))
                step.mark(ts(d[:, 192:256], cum[:, 192:256], cum[:, 191:192], None, ALU.add))
                step.mark(ts(d[:, 64:128], cum[:, 64:128], -1.0, cum[:, 127:128], ALU.mult, ALU.add))
                L(ts(d[:, 0:64], cum[:, 0:64], -1.0, cum[:, 63:64], ALU.mult, ALU.add))
                tell("hg_exp", ts(d[:, 0:64], d[:, 0:64], cum[:, 127:128], None, ALU.add))
                dve.wait_ge(S["hg_decay"], h + 1)
                tell("hg_eq", tt(heq.rearrange("p (l t) -> p l t", t=T), hd.rearrange("p (l t) -> p l t", t=T),
                                 zt(ZQ + h).unsqueeze(1).to_broadcast([P, 8, T]), ALU.mult))

            decays(0)
            for h in range(HG):
                for b in range(2):
                    dve.wait_ge(S["hg_sc"], 3 * h + b + 1)
                    L(tt(hmk.rearrange("p (l t) -> p l t", t=BANK), ps[:, 4 + 2 * b:6 + 2 * b, :],
                         mc("hgmask", 8 * P).rearrange("p (l t) -> p l t", t=BANK), ALU.mult))
                    tell("hg_masked", dve.tensor_reduce(hms[:, b * P:(b + 1) * P], hmk.rearrange("p (l t) -> p t l", t=P),
                                                        AX.X, ALU.add))
                dve.wait_ge(S["hg_sc"], 3 * h + 3)
                tell("hg_masked", dve.tensor_copy(hms[:, T:3 * P], ps[:, 4, 0:P]))
                if h + 1 < HG:
                    decays(h + 1)
                dve.wait_ge(S["hg_o"], h + 1)
                tell("hg_oc", dve.tensor_copy(yt(4 + h), ps[:, 5, 0:T]))
            dve.wait_ge(S["hg_ss"], 1)
            r6 = heq[:, 0:HG * T]
            tell("hg_ms", ts(r6.rearrange("p (a t) -> p a t", t=BANK), ps[:, 4:7, :], 1.0 / P, EPS, ALU.mult, ALU.add))
            dve.wait_ge(S["hg_rt"], 1)
            L(dve.reciprocal(r6, r6))
            for h in range(HG):
                L(stt(yt(4 + h), yt(4 + h), pc("hg_norm", h), r6[:, h * T:(h + 1) * T], ALU.mult, ALU.mult))
            tell("yb_done", tt(yt(4, 6), yt(4, 6), zt(ZG, 6), ALU.mult))

            for k in range(6):
                x, w = zt(ZC + k), mca[:, k * T:(k + 1) * T]
                dve.wait_ge(evac_done, ZC + k + 1)
                L(ts(w, x, pc("conv_w", 18 + k), pc("conv_b", k), ALU.mult, ALU.add))
                for d in range(1, 4):
                    last = stt(w[:, d:T], x[:, 0:T - d], pc("conv_w", (3 - d) * 6 + k), w[:, d:T], ALU.mult, ALU.add)
                    if (k, d) == (5, 3):
                        tell("ml_conv", last)
                    else:
                        L(last)
            dve.wait_ge(evac_done, ZIF + 1)
            r = [mrow[:, k * T:(k + 1) * T] for k in range(6)]
            L(ts(r[0], zt(ZIF)[32:36, :], par[32:36, COL["b_fg"]:COL["b_fg"] + 1], None, ALU.add))
            L(ts(r[3], r[0], -1.0, None, ALU.mult))
            tell("ml_ax", tt(r[1], r[0], r[3], ALU.max))
            dve.wait_ge(S["ml_e"], 1)
            tell("ml_e1", ts(r[1], r[1], 1.0, None, ALU.add))
            L(ts(r[0], r[0], 0.0, None, ALU.min))
            dve.wait_ge(S["ml_ln"], 1)
            L(tt(r[0], r[0], r[1], ALU.subtract))
            L(dve.tensor_tensor_scan(r[1], ones[0:MH, 0:1].to_broadcast([MH, T]), r[0], 0.0, ALU.mult, ALU.add))
            L(stt(r[2], zt(ZIF)[0:MH, :], par[0:MH, COL["b_ig"]:COL["b_ig"] + 1], r[1], ALU.add, ALU.subtract))
            L(dve.tensor_tensor_scan(r[3], r[2], r[2], 0.0, ALU.max, ALU.max))
            L(ts(r[4], r[3], -1.0, None, ALU.mult))
            tell("ml_rows", stt(r[5], r[1], -1.0, r[3], ALU.mult, ALU.subtract))
            dve.wait_ge(S["ml_at"], 1)
            tell("ml_atc", dve.tensor_copy(macol, ps[:, 4, 0:2 * MH]))
            for h in range(MH):
                dve.wait_ge(S["ml_bc"], h + 1)
                L(tt(mx[:, 0:P], ps[:, 4, 0:P], mc("causal", P), ALU.add))
                L(dve.tensor_copy(mx[:, P:T], ps[:, 4, P:T]))
                tell("ml_x", tt(mx[:, T:3 * P], ps[:, 4, P:T], mc("causal", P), ALU.add))
                dve.wait_ge(S["ml_w"], h + 1)
                dve.wait_ge(S["ml_sc"], h + 1)
                tell("ml_p", tt(mp, mx, ps[:, 5, 0:3 * P], ALU.mult))
                dve.wait_ge(S["ml_nd"], h + 1)
                L(ts(mden, ps[:, 6, 0:T], -1.0, None, ALU.mult))
                L(tt(mden, mden, ps[:, 6, 0:T], ALU.max))
                L(tt(mden, mden, men, ALU.max))
                L(dve.reciprocal(mden, mden))
                for mi, (tile, r0, rows, _) in enumerate(head_parts(h)):
                    tell("ml_h", tt(yt(10 + tile)[r0:r0 + rows, :], ps[r0:r0 + rows, 7, mi * T:(mi + 1) * T],
                                    mden[r0:r0 + rows, :], ALU.mult))
            dve.wait_ge(S["ml_ss"], 1)
            r4 = mvt[:, 0:MH * T]
            tell("ml_ms", ts(r4.rearrange("p (a t) -> p a t", t=T), ps[:, 4:8, 0:T], 1.0 / MD, EPS, ALU.mult, ALU.add))
            dve.wait_ge(S["ml_rt"], 1)
            L(dve.reciprocal(r4, r4))
            for h in range(MH):
                for tile, r0, rows, _ in head_parts(h):
                    yy = yt(10 + tile)[r0:r0 + rows, :]
                    L(stt(yy, yy, par[r0:r0 + rows, COL["ml_norm"] + tile:COL["ml_norm"] + tile + 1],
                          r4[r0:r0 + rows, h * T:(h + 1) * T], ALU.mult, ALU.mult))
            dve.wait_ge(S["ml_og"], 1)
            tell("yc_done", tt(yt(10, 6), yt(10, 6), zt(ZO, 6), ALU.mult))

            dve.wait_ge(S["sig_ab"], 1)
            N["branch_read"], N["merged_done"] = Count(dve, S["branch_read"]), Count(dve, S["merged_done"])

            def merge(m, i=None):
                v = (lambda c, per: c if i is None else i * per + c)
                gate = (lambda k: zt(k + m) if i is None else z[:, bass.ds(i * (4 * T) + (k + m) * T, T)])
                out = merged[:, m * T:(m + 1) * T] if i is None else merged[:, bass.ds(i * (4 * T) + m * T, T)]
                a, b = ps[:, 4 + 2 * (m % 2), 0:T], ps[:, 4 + 2 * (m % 2), T:2 * T]
                dve.wait_ge(panel_done, v(PANELS["merge"] + 2 * m + 2, 8))
                L(tt(mg[0], a, gate(ZGA), ALU.mult))
                L(tt(mg[1], b, gate(ZGB), ALU.mult))
                dve.wait_ge(evac_done, v(OUT["gc"] + m + 1, 4))
                tell("branch_read", tt(mg[2], ps[:, 5 + 2 * (m % 2), 0:T], mg[3 + m % 2], ALU.mult))
                L(tt(mg[0], mg[0], mg[1], ALU.add))
                tell("merged_done", tt(out, mg[0], mg[2], ALU.add))

            for m in range(4):
                merge(m)
            with dve.Fori(0, 3) as i:
                cs = (step, N["branch_read"], N["merged_done"])
                for c, per in zip(cs, (12, 4, 4)):
                    c.enter(i, per)
                for m in range(4, 8):
                    merge(m, i)
                for c in cs:
                    c.leave(3)
            x_rest(dve, "merged", merged, 1)
            rests(dve, PANELS["wout"])
            x_rest(dve, "merged", merged, 3)
            dve.wait_ge(evac_done, OUT["wout"])
            evac.base = OUT["wout"]
            add_residual(OUT["wout"], KD)
            normalise(1, res, nx(), "ffn", KD)
            for q in (1, 3):
                x_rest(dve, "ffn", nx(), q)

            N["ff_out"] = Count(dve, S["ff_out"])

            def ffn_pair(u, i):
                for half, f in ((0, fa), (1, fb)):
                    p = OUT["up"] + 2 * u + half
                    rests(dve, PANELS["up"] + 2 * u + half + 1, i, 4)
                    w = (lambda c: par[:, bass.ds(i * 16 + (COL["fconv"] + 8 * u + 4 * half + c), 1)])
                    x = ps[:, p % 4, 0:T]
                    dve.wait_ge(panel_done, i * 4 + (PANELS["up"] + 2 * u + half + 1))
                    L(ts(f, x, w(2), w(3), ALU.mult, ALU.add))
                    L(stt(f[:, 1:T], x[:, 0:T - 1], w(1), f[:, 1:T], ALU.mult, ALU.add))
                    evac.link(stt(f[:, 2:T], x[:, 0:T - 2], w(0), f[:, 2:T], ALU.mult, ALU.add))
                dve.wait_ge(S["ff_silu"], i * 2 + (u + 1))
                tell("ff_out", tt(gff[:, bass.ds(i * (2 * T) + u * T, T)], fa, fb, ALU.mult))

            with dve.Fori(0, FT // 2) as i:
                for c, per in ((step, 8), (evac, 4), (N["ff_out"], 2)):
                    c.enter(i, per)
                for u in range(2):
                    ffn_pair(u, i)
                for c in (step, evac, N["ff_out"]):
                    c.leave(FT // 2)

            def add_all(n, src):
                dve.wait_ge(panel_done, n)
                for b in range(8):
                    c = slice(b * BANK, (b + 1) * BANK)
                    tell("res_done", tt(res[:, c], src[:, c], ps[:, b, :], ALU.add))

            tile_c = Count(dve, tile_lo)

            def tile_rest(k, src, before, i=None):
                dve.wait_ge(tile_hi, turn(i, 4, before + k + 1))
                c = src[:, k * T:(k + 1) * T] if i is None else src[:, bass.ds(i * (4 * T) + k * T, T)]
                tile_c.mark(tt(tlo[k % 2], c, thi[k % 2].bitcast(F32), ALU.subtract))

            def accumulation_rests(n, count, src, before):
                tile_rest(0, src, before)
                turns = (count - 1) // 4
                with dve.Fori(0, turns) as i:
                    tile_c.enter(i, 4)
                    for k in range(1, 5):
                        tile_rest(k, src, before, i)
                        rests(dve, n + k, i, 4)
                    tile_c.leave(turns)
                for k in range(1 + 4 * turns, count):
                    tile_rest(k, src, before)
                    rests(dve, n + k)

            accumulation_rests(PANELS["down"], FT, gff, 0)
            rests(dve, PANELS["in2"])
            add_all(PANELS["down"] + FT, res)
            normalise(2, res, res, "final", KD, 0)
            normalise(3, res, nx(), "mix2", KD)
            for q in (1, 3):
                x_rest(dve, "mix2", nx(), q)

            rests_loop(dve, PANELS["in2"] + 1, 8)
            dve.wait_ge(evac_done, OUT["in2"] + 8)
            src = z2
            for k in range(4):
                dst, d, a = pb[k % 2], 1 << k, 2 * k
                s3 = src[:, a * T:8 * T].rearrange("p (c t) -> p c t", t=T)
                d3 = dst[:, a * T:8 * T].rearrange("p (c t) -> p c t", t=T)
                L(tt(d3[:, :, d:T], s3[:, :, d:T], s3[:, :, 0:T - d], ALU.add))
                L(dve.tensor_copy(d3[:, :, 0:d], s3[:, :, 0:d]))
                rests(dve, PANELS["in2"] + 9 + 2 * k)
                c = slice(a * T, (a + 2) * T)
                cnt = mc("invcnt", T, k * T).unsqueeze(1).to_broadcast([P, 2, T])
                L(tt(pb[2][:, c].rearrange("p (c t) -> p c t", t=T), dst[:, c].rearrange("p (c t) -> p c t", t=T), cnt, ALU.mult))
                rests(dve, PANELS["in2"] + 10 + 2 * k)
                last = tt(pb[2][:, c], pb[2][:, c], z2[:, c], ALU.subtract)
                if k < 3:
                    L(last)
                else:
                    tell("po_d", last)
                src = dst
            for c in range(8):
                if c < 7:
                    dve.wait_ge(S["po_y"], c + 1)
                else:
                    dve.wait_ge(panel_done, PANELS["pool"] + 1)
                tell("po_yc", ts(y2t(c), ps[:, 4 + c % 4, 0:T], pc("pool_scale", c), None, ALU.mult))
            normalise(4, z2t(8, 4), z2t(8, 4), "q_lat", 4, 4)
            normalise(5, z2t(12, 4), z2t(12, 4), "kv_lat", 4, 5)
            ang, turns, cos, sin, kro = rope
            dve.wait_ge(pos_in, 16)
            L(dve.tensor_copy(ang, posi))
            L(ts(ang, ang, con[0:64, CC["invfreq"]:CC["invfreq"] + 1], None, ALU.mult))
            tell("rp_angle", reduce_angle(ang, turns))
            dve.wait_ge(S["rp_sin"], 1)
            L(stt(cos, cos, -2.0, cos, ALU.mult, ALU.mult))
            L(ts(cos, cos, 1.0, None, ALU.add))
            qr3, kr3, rq3 = (a[0:64, :].rearrange("p (h t) -> p h t", t=T) for a in (qrope, krope, rq))
            cb, sbr = (a.unsqueeze(1).to_broadcast([64, AH, T]) for a in (cos, sin))

            for o in range(16):
                dve.wait_ge(S["at_q"], o + 1)
                bank = ps[:, 4 + o % 4, 0:T]
                if o < 8:
                    out, x = qn[:, o * T:(o + 1) * T], bank
                else:
                    out, x = qrope[0:64, (o - 8) * T:(o - 7) * T], bank[0:64, :]
                tell("at_qc", dve.tensor_copy(out, x))

            def head_mean(r):
                dve.wait_ge(S["at_ss"], r + 1)
                tell("at_ms", ts(rq.rearrange("p (a t) -> p a t", t=BANK), ps[:, 4 * r:4 * r + 4, :], 1.0 / 192, EPS, ALU.mult, ALU.add))

            head_mean(0)
            dve.wait_ge(S["at_rt"], 1)
            L(dve.reciprocal(rq, rq))
            L(stt(qn, qn, pc("qn_n"), rq, ALU.mult, ALU.mult))
            tell("at_qn", stt(qrope[0:64, :], qrope[0:64, :], par[0:64, COL["qn_r"]:COL["qn_r"] + 1], rq[0:64, :], ALU.mult, ALU.mult))
            dve.wait_ge(S["at_rot"], 1)
            tell("at_rotc", tt(kr3, ps[0:64, 0:4, :].rearrange("p a (c t) -> p (a c) t", t=T), sbr, ALU.mult))
            head_mean(1)
            tell("at_qn", ts(kro, z2t(16)[0:64, :], par[0:64, COL["kn_r"]:COL["kn_r"] + 1], None, ALU.mult))
            L(tt(qr3, qr3, cb, ALU.mult))
            L(tt(qr3, qr3, kr3, ALU.add))
            dve.wait_ge(S["at_rt"], 2)
            L(dve.reciprocal(rq, rq))
            L(stt(kn, kn, pc("kn_n"), rq, ALU.mult, ALU.mult))
            dve.wait_ge(S["at_rot"], 2)
            L(tt(ang, ps[0:64, 4, 0:T], sin, ALU.mult))
            L(tt(kro, kro, cos, ALU.mult))
            L(tt(kro, kro, ang, ALU.add))
            tell("at_done", tt(kr3, kro.unsqueeze(1).to_broadcast([64, AH, T]), rq3, ALU.mult))
            rests(dve, PANELS["wout2"])
            x_rest(dve, "y", y2, 1)
            scale = 192 ** -0.5
            for h in range(AH):
                u, k = h % 2, sm[:, 8 * h:8 * h + 8]
                dve.wait_ge(S["at_s"], h + 1)
                if h >= 2:
                    dve.wait_ge(S["at_t"], h - 1)
                L(tt(sc[u], ps[:, 4 + u, 0:384], mc("chunkmask", 384), ALU.add))
                L(dve.tensor_reduce(k[:, 0:1], sc[u][:, 0:P], AX.X, ALU.max))
                L(dve.tensor_reduce(k[:, 1:2], sc[u][:, P:384], AX.X, ALU.max))
                tell("at_mx", ts(k[:, 2:4], k[:, 0:2], -scale, None, ALU.mult))
                dve.wait_ge(S["at_e"], 2 * h + 2)
                L(dve.reciprocal(k[:, 6:8], k[:, 4:6]))
                L(ts(sc[u][:, 0:P], sc[u][:, 0:P], k[:, 6:7], None, ALU.mult))
                tell("at_p", ts(sc[u][:, P:384], sc[u][:, P:384], k[:, 7:8], None, ALU.mult))
                if h:
                    dve.wait_ge(S["at_o"], h)
                    tell("at_oc", dve.tensor_copy(y2t(7 + h), ps[:, 7, 0:T]))
            dve.wait_ge(S["at_o"], AH)
            tell("at_oc", dve.tensor_copy(y2t(15), ps[:, 7, 0:T]))
            x_rest(dve, "y", y2, 3)
            dve.wait_ge(evac_done, OUT["wout2"])
            evac.base, evac.k = OUT["wout2"], 0
            add_residual(OUT["wout2"], KD)
            normalise(6, res, nx(), "ffn2", KD)
            for q in (1, 3):
                x_rest(dve, "ffn2", nx(), q)
            rests_loop(dve, PANELS["pq"] + 1, 16 - 1)
            rests(dve, PANELS["eu"])

            def top16(vals, idx, src):
                L(dve.max(vals[:, 0:8], src))
                L(dve.max_index(idx[:, 0:8], vals[:, 0:8], src))
                L(dve.match_replace(src, vals[:, 0:8], src, -3e38))
                L(dve.max(vals[:, 8:16], src))
                L(dve.max_index(idx[:, 8:16], vals[:, 8:16], src))

            eu = PANELS["eu"] + 1
            for b in range(2):
                for c in range(16):
                    k = 16 * b + c
                    if c % 2:
                        rests(dve, eu)
                        eu += 1
                    if c % 4 == 0:
                        dve.wait_ge(S["pk_sc"], 4 * b + c // 4 + 1)
                    top16(val[:, 16 * k:16 * k + 16], vidx[:, 16 * k:16 * k + 16], s12[:, k * NK:(k + 1) * NK])
                v4 = val[:, 256 * b:256 * b + 256].rearrange("p (h s k) -> p h s k", s=2, k=16)
                cb4 = cand[:, 2048 * b:2048 * b + 2048].rearrange("p (h i j) -> p h i j", i=16, j=16)
                L(tt(cb4, v4[:, :, 0, :].unsqueeze(3).to_broadcast([P, PH, 16, 16]),
                     v4[:, :, 1, :].unsqueeze(2).to_broadcast([P, PH, 16, 16]), ALU.add))
                for h in range(PH):
                    k = PH * b + h
                    if h % 2:
                        rests(dve, eu)
                        eu += 1
                    top16(cval[:, 16 * k:16 * k + 16], cidx[:, 16 * k:16 * k + 16], cand[:, 256 * k:256 * k + 256])
            c3 = cval.rearrange("p (h k) -> p h k", k=16)
            top = cval.rearrange("p (h k) -> p h k", k=16)[:, :, 0:1]
            L(dve.tensor_copy(gsum.unsqueeze(2), top))
            tell("pk_g", tt(c3, c3, gsum.unsqueeze(2).to_broadcast([P, 16, 16]), ALU.subtract))
            L(ts(cdu[0], cidx, 4, None, ALU.logical_shift_right))
            L(ts(cdu[1], cidx, 15, None, ALU.bitwise_and))
            L(dve.tensor_copy(cdf[0], cdu[0]))
            L(dve.tensor_copy(cdf[1], cdu[1]))
            L(dve.tensor_copy(vidf, vidx))
            e3 = eqt.rearrange("p (a j) -> p a j", j=16)
            e4 = eqt.rearrange("p (h k j) -> p h k j", k=16, j=16)
            for half in range(2):
                for b in range(2):
                    rests(dve, eu)
                    eu += 1
                    L(tt(e3, cdf[half][:, P * b:P * b + P].unsqueeze(2).to_broadcast([P, P, 16]),
                         iota[:, 0:16].unsqueeze(1).to_broadcast([P, P, 16]), ALU.is_equal))
                    i4 = vidf[:, 256 * b:256 * b + 256].rearrange("p (h s k) -> p h s k", s=2, k=16)[:, :, half, :]
                    L(tt(e4, e4, i4.unsqueeze(2).to_broadcast([P, PH, 16, 16]), ALU.mult))
                    L(dve.tensor_reduce(etm[:, half * T + b * P:half * T + (b + 1) * P], e3, AX.X, ALU.add))
            dve.wait_ge(S["pk_e"], 1)
            L(dve.tensor_reduce(gsum, c3, AX.X, ALU.add))
            L(dve.reciprocal(gsum, gsum))
            tell("pk_et", tt(etm[:, 2 * T:3 * T].rearrange("p (h k) -> p h k", k=16), c3,
                             gsum.unsqueeze(2).to_broadcast([P, 16, 16]), ALU.mult))
            rests_loop(dve, eu, PANELS["eu"] + NK // 2 + 1 - eu)
            dve.wait_ge(S["pk_t"], 1)
            dve.wait_ge(res_parked, 16)
            for k in range(2):
                L(dve.tensor_copy(et[:, k * T:(k + 1) * T], ps[:, 4 + k, 0:T]))
            tell("pk_tc", dve.tensor_copy(et[:, 2 * T:3 * T], ps[:, 6, 0:T]))
            rests_loop(dve, PANELS["eu"] + NK // 2 + 1, NK // 2)

            N["oh1_done"], N["tok_ev"] = Count(dve, S["oh1_done"]), Count(dve, S["tok_ev"])
            a3 = A.rearrange("p (e t) -> p t e", t=T)

            def rows(g, i=None):
                if g:
                    dve.wait_ge(S["tok_mm"], 4 * g if i is None else i * 16 + 4 * g)
                for t in range(4 * g, 4 * g + 4):
                    e = (lambda k: et[:, k * T + t:k * T + t + 1] if i is None else et[:, bass.ds(i * 16 + (k * T + t), 1)])
                    N["oh1_done"].mark(ts(oh1[:, t % 4 * P:(t % 4 + 1) * P], iota, e(0), e(2), ALU.is_equal, ALU.mult))

            def weigh(g, i=None):
                c = a3[:, 4 * g:4 * g + 4, :] if i is None else a3[:, bass.ds(i * 16 + 4 * g, 4), :]
                N["tok_ev"].mark(tt(c, c, ps[:, 4 + g % 4, :].rearrange("p (t e) -> p t e", e=P), ALU.mult))

            dve.wait_ge(evac_done, OUT["pg"])
            rows(0)
            for g in range(3):
                rows(g + 1)
                weigh(g)
            with dve.Fori(0, T // 16 - 1) as i:
                N["oh1_done"].enter(i, 16)
                N["tok_ev"].enter(i, 4)
                for g in range(3, 7):
                    rows(g + 1, i)
                    weigh(g, i)
                N["oh1_done"].leave(T // 16 - 1)
                N["tok_ev"].leave(T // 16 - 1)
            dve.wait_ge(S["tok_mm"], T)
            weigh(T // 4 - 1)
            accumulation_rests(PANELS["ev"], NK, A, FT)
            dve.wait_ge(res_back, 16)
            add_all(PANELS["ev"] + NK, res2)
            def projected(half):
                dve.wait_ge(panel_done, PANELS["pp"] + half + 1)
                for b in range(4 * half, 4 * half + 4):
                    tell("pp_ev", dve.tensor_copy(ppj[:, b * BANK:(b + 1) * BANK], ps[:, b, :]))

            projected(0)
            normalise(7, res, nx(), "ple", KD)
            x_rest(dve, "ple", nx(), 1)
            rests(dve, PANELS["pg"])
            dve.wait_ge(panel_done, PANELS["pg"])
            x_rest(dve, "ple", nx(), 3)
            projected(1)
            N["out_ready"] = Count(dve, S["out_ready"])

            def finish(j, i=None):
                if j < KD - 1:
                    rests(dve, PANELS["pg"] + j + 1, i, 4)
                dve.wait_ge(evac_done, turn(i, 4, OUT["pg"] + j + 1))
                c, r = (a[:, j * T:(j + 1) * T] if i is None else a[:, bass.ds(i * (4 * T) + j * T, T)] for a in (ppj, res))
                L(tt(c, c, gt[:, j % 4 * T:(j % 4 + 1) * T], ALU.mult))
                tell("out_ready", tt(r, r, c, ALU.add))

            with dve.Fori(0, KD // 4 - 1) as i:
                step.enter(i, 4)
                N["out_ready"].enter(i, 4)
                for j in range(4):
                    finish(j, i)
                step.leave(KD // 4 - 1)
                N["out_ready"].leave(KD // 4 - 1)
            for j in range(KD - 4, KD):
                finish(j)

        @block.scalar
        def _(act):
            step = Count(act, act_step)
            evac = Count(act, evac_done)
            sq_c, rt_c = Count(act, rms_sq), Count(act, rms_rt)
            N = {}

            def tell(name, ins):
                if name not in N:
                    N[name] = Count(act, S[name])
                N[name].link(ins)

            def fn(out, x, f, **kw):
                return act.activation(out, x, f, **kw)

            def squares(src, dst, tiles, ready=None):
                for q in range(4):
                    if ready:
                        ready(q)
                    c = slice(q * tiles // 4 * T, (q + 1) * tiles // 4 * T)
                    sq_c.link(fn(dst[:, c], src[:, c], ACT.Square))

            def root(r):
                act.wait_ge(rms_ms, r + 1)
                rt_c.link(fn(rstd[:], rstd[:], ACT.Sqrt))

            def high_and_squares(n, p):
                with act.Fori(0, 4) as i:
                    sq_c.enter(i, 1)
                    for j in range(4):
                        high_parts(act, n + j, i, 4)
                    act.wait_ge(evac_done, i * 4 + (p + 4))
                    c = bass.ds(i * (4 * T), 4 * T)
                    sq_c.link(fn(nx()[:, c], res[:, c], ACT.Square))
                    sq_c.leave(4)

            def x_high_norm(r, name):
                for q in range(4):
                    act.wait_ge(rms_out, 4 * r + q + 1)
                    x_high(act, name, q, nx())

            def accumulation_high(n, count, src, before):
                def tile(k, i=None):
                    act.wait_ge(panel_done, turn(i, 4, n + k - 1))
                    c = src[:, k * T:(k + 1) * T] if i is None else src[:, bass.ds(i * (4 * T) + k * T, T)]
                    fn(thi[k % 2], c, ACT.Copy).then_inc(tile_hi, 1)
                tile(0)
                turns = (count - 1) // 4
                with act.Fori(0, turns) as i:
                    for k in range(1, 5):
                        tile(k, i)
                        high_parts(act, n + k, i, 4)
                for k in range(1 + 4 * turns, count):
                    tile(k)
                    high_parts(act, n + k)

            def read_outputs(n, p, count, dst, at):
                turns = 0 if count < 8 else (count - 1) // 4 if is_split(n) else count // 4
                if turns:
                    with act.Fori(0, turns) as i:
                        evac.enter(i, 4)
                        for j in range(4):
                            if is_split(n):
                                high_parts(act, n + j + 1, i, 4)
                            act.wait_ge(panel_done, i * 4 + (n + j + 1))
                            evac.link(fn(dst[:, bass.ds(i * (4 * T) + (at + j) * T, T)], ps[:, (p + j) % 4, 0:T], ACT.Copy))
                        evac.leave(turns)
                for j in range(4 * turns, count):
                    if is_split(n) and j < count - 1:
                        high_parts(act, n + j + 1)
                    act.wait_ge(panel_done, n + j + 1)
                    evac.link(fn(dst[:, (at + j) * T:(at + j + 1) * T], ps[:, (p + j) % 4, 0:T], ACT.Copy))

            s = [s5s[:, 16 * k:16 * k + 16] for k in range(5)]
            act.wait_ge(par_in, 16)
            tell("s5_dt", fn(s[0], pc("log_dt", 0, 16), ACT.Exp))
            act.wait_ge(x_in, 16)
            squares(res, hn1, KD)
            root(0)
            act.wait_ge(S["s5_mi"], 1)
            step.link(fn(s[1], s[1], ACT.Exp))
            step.link(fn(s[3], s[2], ACT.Sin, scale=0.5))
            tell("s5_ma", fn(s[4], s[2], ACT.Sin))
            read_outputs(PANELS["u"], 0, 4, z, ZU)
            for g in range(4):
                act.wait_ge(S["s5_angle"], g + 1)
                step.link(fn(s5tmp, s5re, ACT.Sin, scale=0.5))
                tell("s5_sin", fn(s5sin, s5re, ACT.Sin))
                read_outputs(PANELS["q"] + 6 * g, ZQ + 6 * g, 6, z, ZQ + 6 * g)
                act.wait_ge(S["s5_pre"], g + 1)
                tell("s5_gelu", fn(yt(g), s5tmp[:, 0:T], ACT.Gelu_apprx_tanh))
            read_outputs(ml_panel(0), ZC, ML_FIRST, z, ZC)
            for m in range(4):
                if m < 3:
                    act.wait_ge(S["s5_glu"], m + 1)
                else:
                    act.wait_ge(panel_done, PANELS["glu"] + 1)
                tell("s5_sig", fn(s5sin[:, m * T:(m + 1) * T], ps[:, 4 + m, 0:T], ACT.Sigmoid, bias=pc("b_glu", m)))

            act.wait_ge(S["hg_lbx"], 1)
            tell("hg_lbe", fn(cols[:, 6:12], cols[:, 0:6], ACT.Exp))
            tell("hg_sig", fn(zt(ZF, HG), zt(ZF, HG), ACT.Sigmoid))
            tell("hg_silu", fn(zt(ZQ, HG), zt(ZQ, HG), ACT.Silu))
            step.link(fn(zt(ZG, HG), zt(ZG, HG), ACT.Silu))
            act.wait_ge(S["hg_f"], 1)
            tell("hg_ln", fn(hcum, hcum, ACT.Ln))
            read_outputs(ml_panel(ML_FIRST), ZC + ML_FIRST, ML_HEADS - ML_FIRST - 2, z, ZC + ML_FIRST)

            def decay(h):
                act.wait_ge(S["hg_exp"], h + 1)
                tell("hg_decay", fn(hd, hd, ACT.Exp))

            decay(0)
            read_outputs(ml_panel(ML_HEADS - 2), ZC + ML_HEADS - 2, 2, z, ZC + ML_HEADS - 2)
            for h in range(HG):
                act.wait_ge(S["hg_vt"], h + 1)
                if h:
                    act.wait_ge(S["hg_o"], h)
                tell("hg_vtc", fn(hvt, ps[:, 6, 0:T], ACT.Copy))
                if h + 1 < HG:
                    decay(h + 1)
                j = ML_HEADS + ML_PER_HEAD * h
                read_outputs(ml_panel(j), ZC + j, ML_PER_HEAD, z, ZC + j)
            act.wait_ge(S["hg_oc"], HG)
            tell("hg_sq", fn(zt(ZF, HG), yt(4, HG), ACT.Square))
            act.wait_ge(S["hg_ms"], 1)
            tell("hg_rt", fn(heq[:, 0:HG * T], heq[:, 0:HG * T], ACT.Sqrt))

            j = ML_HEADS + ML_PER_HEAD * HG
            read_outputs(ml_panel(j), ZC + j, 4, z, ZC + j)

            act.wait_ge(S["ml_conv"], 1)
            tell("ml_ca", fn(mca, mca, ACT.Silu))
            r1 = mrow[:, T:2 * T]
            act.wait_ge(S["ml_ax"], 1)
            tell("ml_e", fn(r1, r1, ACT.Exp, scale=-1.0))
            act.wait_ge(S["ml_e1"], 1)
            tell("ml_ln", fn(r1, r1, ACT.Ln))
            read_outputs(ml_panel(j + 4), ZC + j + 4, ML_ALL - j - 4, z, ZC + j + 4)
            for c in range(2 * MH):
                h, half = c % MH, c // MH
                act.wait_ge(S["ml_qk"], c + 1)
                for mi, (tile, r0, rows, _) in enumerate(head_parts(h)):
                    x = ps[r0:r0 + rows, 4 + c % 4, mi * T:(mi + 1) * T]
                    dst = (mca[:, tile * T:(tile + 1) * T] if half else zt(ZC + tile))[r0:r0 + rows, :]
                    ins = fn(dst, x, ACT.Copy, scale=MD ** -0.5 if half else 1.0)
                    if mi == 0:
                        step.link(ins)
                    else:
                        tell("ml_qkc", ins)
            m3 = mvt.rearrange("p (b c) -> p b c", b=2)
            for k in range(HG):
                act.wait_ge(S["ml_vt"], k + 1)
                at = k // 3 * T
                tell("ml_vtc", fn(m3[:, :, k * P:(k + 1) * P], ps[:, 5 + k % 3, at:at + T].rearrange("p (b c) -> p b c", b=2), ACT.Copy))

            def gates(j, count):
                read_outputs(PANELS["ga2"] + j, ZGA + GATES_1 + j, count, z, ZGA + GATES_1 + j)

            for h in range(MH):
                act.wait_ge(S["ml_x"], h + 1)
                step.link(fn(mx[:, 0:T], mx[:, 0:T], ACT.Exp, bias=macol[:, h:h + 1]))
                step.link(fn(mx[:, T:3 * P], mx[:, T:3 * P], ACT.Exp, bias=macol[:, MH + h:MH + h + 1]))
                tell("ml_w", fn(men, ps[:, 4, T:2 * T], ACT.Exp))
                gates(GATES_HEAD * h, GATES_HEAD)
            act.wait_ge(S["ml_h"], 2 * MH)
            tell("ml_sq", fn(mca, yt(10, 6), ACT.Square))
            gates(GATES_HEAD * MH, 3)
            act.wait_ge(S["ml_ms"], 1)
            tell("ml_rt", fn(mvt[:, 0:MH * T], mvt[:, 0:MH * T], ACT.Sqrt))
            tell("ml_og", fn(zt(ZO, 6), zt(ZO, 6), ACT.Sigmoid))
            gates(GATES_HEAD * MH + 3, 32 - GATES_1 - GATES_HEAD * MH - 3)
            for k in range(4):
                ins = fn(zt(ZGA + 8 * k, 8), zt(ZGA + 8 * k, 8), ACT.Sigmoid)
                step.link(ins) if k < 3 else tell("sig_ab", ins)

            def gate(m, i=None):
                act.wait_ge(panel_done, PANELS["merge"] + 2 * m + 1 if i is None else i * 8 + (PANELS["merge"] + 2 * m + 1))
                if m >= 2:
                    act.wait_ge(S["branch_read"], m - 1 if i is None else i * 4 + (m - 1))
                evac.link(fn(mg[3 + m % 2], ps[:, (OUT["gc"] + m) % 4, 0:T], ACT.Sigmoid))

            for m in range(4):
                gate(m)
            with act.Fori(0, 3) as i:
                evac.enter(i, 4)
                for m in range(4, 8):
                    gate(m, i)
                act.wait_ge(S["merged_done"], i * 4 + 4)
                x_high(act, "merged", 0, merged, i)
                evac.leave(3)
            act.wait_ge(panel_done, PANELS["merge"] + 31)
            high_parts(act, PANELS["wout"])
            act.wait_ge(S["merged_done"], KD)
            x_high(act, "merged", 3, merged)
            high_and_squares(PANELS["wout"] + 1, OUT["wout"])
            root(1)
            x_high_norm(1, "ffn")
            N["ff_silu"] = Count(act, S["ff_silu"])
            with act.Fori(0, FT // 2) as i:
                N["ff_silu"].enter(i, 2)
                for u in range(2):
                    high_parts(act, PANELS["up"] + 2 * u + 1, i, 4)
                    high_parts(act, PANELS["up"] + 2 * u + 2, i, 4)
                    act.wait_ge(evac_done, i * 4 + (OUT["up"] + 2 * u + 1))
                    tell("ff_silu", fn(fa, fa, ACT.Silu))
                N["ff_silu"].leave(FT // 2)
            act.wait_ge(S["ff_out"], FT)
            accumulation_high(PANELS["down"], FT, gff, 0)
            high_parts(act, PANELS["in2"])
            squares(res, nx(), KD, lambda q: act.wait_ge(S["res_done"], 2 * q + 2))
            root(2)
            squares(res, nx(), KD, lambda q: act.wait_ge(rms_out, 9 + q))
            root(3)
            x_high_norm(3, "mix2")

            evac.base, evac.k = OUT["in2"], 0
            read_outputs(PANELS["in2"], OUT["in2"], 17, z2, 0)
            for r in range(2):
                squares(z2t(8 + 4 * r, 4), sq[:, 4 * r * T:(4 * r + 4) * T], 4)
                root(4 + r)
            ang, _, cos, sin, _ = rope
            act.wait_ge(S["rp_angle"], 1)
            step.link(fn(cos, ang, ACT.Sin, scale=0.5))
            tell("rp_sin", fn(sin, ang, ACT.Sin))
            N["at_qc"] = Count(act, S["at_qc"])
            N["at_qc"].base = 16

            def take(o):
                act.wait_ge(S["at_q"], o + 1)
                bank = ps[:, 4 + o % 4, :]
                if o < 24:
                    out, x = kn[:, (o - 16) * T:(o - 15) * T], bank[:, 0:T]
                else:
                    c, b = divmod(o - 24, 2)
                    out, x = vtm[:, b * 1024 + c * BANK:b * 1024 + (c + 1) * BANK], bank
                tell("at_qc", fn(out, x, ACT.Copy))

            act.wait_ge(S["at_qc"], 16)
            step.link(fn(sq, qn, ACT.Square))
            tell("at_sq", fn(vsq[0:64, :], qrope[0:64, :], ACT.Square))
            for o in range(16, 20):
                take(o)
            act.wait_ge(S["at_ms"], 1)
            tell("at_rt", fn(rq, rq, ACT.Sqrt))
            for o in range(20, 24):
                take(o)
            act.wait_ge(S["at_ss"], 1)
            step.link(fn(sq, kn, ACT.Square))
            tell("at_sq", fn(vsq[0:64, 0:T], z2t(16)[0:64, :], ACT.Square))
            for o in range(24, 28):
                take(o)
            act.wait_ge(S["at_ms"], 2)
            tell("at_rt", fn(rq, rq, ACT.Sqrt))
            high_parts(act, PANELS["wout2"])
            act.wait_ge(S["po_yc"], 8)
            for q in range(2):
                x_high(act, "y", q, y2)
            for h in range(AH):
                u, k = h % 2, sm[:, 8 * h:8 * h + 8]
                act.wait_ge(S["at_mx"], h + 1)
                tell("at_e", fn(sc[u][:, 0:P], sc[u][:, 0:P], ACT.Exp, bias=k[:, 2:3], scale=192 ** -0.5, accum_out=k[:, 4:5]))
                tell("at_e", fn(sc[u][:, P:384], sc[u][:, P:384], ACT.Exp, bias=k[:, 3:4], scale=192 ** -0.5, accum_out=k[:, 5:6]))
                act.wait_ge(S["at_t"], h + 1)
                if h >= 2:
                    act.wait_ge(S["at_o"], h - 1)
                tell("at_tc", fn(pt[u], ps[:, 6, 0:384], ACT.Copy))
                if h == 5:
                    act.wait_ge(S["at_oc"], 4)
                    x_high(act, "y", 2, y2)
            act.wait_ge(S["at_oc"], AH)
            x_high(act, "y", 3, y2)
            high_and_squares(PANELS["wout2"] + 1, OUT["wout2"])
            root(6)
            x_high_norm(6, "ffn2")
            evac.base, evac.k = OUT["pq"], 0
            read_outputs(PANELS["pq"], OUT["pq"], 16, q2, 0)
            high_parts(act, PANELS["eu"])
            for g in range(8):
                if g < 7:
                    act.wait_ge(S["pk_s"], g + 1)
                else:
                    act.wait_ge(panel_done, PANELS["subk"] + 1)
                tell("pk_sc", fn(s12[:, g * BANK:(g + 1) * BANK], ps[:, 4 + g % 4, :], ACT.Copy))

            def experts(e, count):
                with act.Fori(0, count // 4) as i:
                    evac.enter(i, 4)
                    for j in range(4):
                        high_parts(act, PANELS["eu"] + e + j + 1, i, 4)
                        act.wait_ge(panel_done, i * 4 + (PANELS["eu"] + e + j + 1))
                        evac.link(fn(A[:, bass.ds(i * (4 * T) + (e + j) * T, T)], ps[:, j, 0:T], ACT.Gelu_apprx_tanh))
                    evac.leave(count // 4)

            experts(0, 24)
            act.wait_ge(S["pk_g"], 1)
            tell("pk_e", fn(cval, cval, ACT.Exp))
            experts(24, 40)
            act.wait_ge(S["pk_tc"], 1)
            experts(64, 64)
            N["oh2_act"], N["oh2_sq"] = Count(act, S["oh2_act"]), Count(act, S["oh2_sq"])

            def two(g, i=None):
                for t in range(2):
                    c = T + 4 * g + 2 + t
                    e = et[:, c:c + 1] if i is None else et[:, bass.ds(i * 8 + c, 1)]
                    ins = fn(osq[:, t * P:(t + 1) * P], iota, ACT.Square, bias=e, scale=-1.0)
                    N["oh2_sq"].mark(ins) if t == 0 else N["oh2_sq"].link(ins)
                if g >= 2:
                    act.wait_ge(S["tok_mm"], turn(i, 8, 4 * g - 4))
                c = (g % 2 * 4 + 2) * P
                N["oh2_act"].link(fn(oh2[:, c:c + 2 * P], osq, ACT.Relu, bias=ones[:, 0:1], scale=-2.0))

            for g in range(2):
                two(g)
            with act.Fori(0, T // 8 - 1) as i:
                N["oh2_act"].enter(i, 2)
                N["oh2_sq"].enter(i, 4)
                for g in range(2, 4):
                    two(g, i)
                N["oh2_act"].leave(T // 8 - 1)
                N["oh2_sq"].leave(T // 8 - 1)
            act.wait_ge(S["tok_ev"], T // 4)
            accumulation_high(PANELS["ev"], NK, A, FT)
            squares(res, nx(), KD, lambda q: act.wait_ge(S["res_done"], 2 * q + 10))
            root(7)
            x_high_norm(7, "ple")
            high_parts(act, PANELS["pg"])

            def embed(m, i=None):
                if m < KD - 1:
                    high_parts(act, PANELS["pg"] + m + 1, i, 4)
                act.wait_ge(panel_done, turn(i, 4, PANELS["pg"] + m + 1))
                if m >= 4:
                    act.wait_ge(S["out_ready"], turn(i, 4, m - 3))
                evac.link(fn(gt[:, m % 4 * T:(m % 4 + 1) * T], ps[:, m % 4, 0:T], ACT.Sigmoid))

            for m in range(4):
                embed(m)
            with act.Fori(0, 2) as i:
                evac.enter(i, 4)
                for m in range(4, 8):
                    embed(m, i)
                evac.leave(2)
            for m in range(KD - 4, KD):
                embed(m)

        @block.gpsimd
        def _(pool):
            ek = Count(pool, S["hg_ek"])
            for h in range(HG):
                pool.wait_ge(S["hg_eq"], h + 1)
                ek.link(pool.tensor_tensor(hd.rearrange("p (l t) -> p l t", t=T), hd.rearrange("p (l t) -> p l t", t=T),
                                           hk[:, h * T:(h + 1) * T].unsqueeze(1).to_broadcast([P, 8, T]), ALU.mult))
            for q in (0, 2):
                x_rest(pool, "merged", merged, q)
            rests(pool, PANELS["wout"])
            rests_loop(pool, PANELS["wout"] + 1, KD)
            for q in (0, 2):
                x_rest(pool, "ffn", nx(), q)
            pool.dma_start(posi, pos).then_inc(pos_in, 16)
            rests_loop(pool, PANELS["up"] + 1, 2 * FT + FT)
            for q in (0, 2):
                x_rest(pool, "mix2", nx(), q)
            rests_loop(pool, PANELS["in2"] + 1, 16)
            rests(pool, PANELS["wout2"])
            for q in (0, 2):
                x_rest(pool, "y", y2, q)
            rests_loop(pool, PANELS["wout2"] + 1, KD)
            for q in (0, 2):
                x_rest(pool, "ffn2", nx(), q)
            pool.dma_start(outT, res[:]).then_inc(res_parked, 16)
            rests_loop(pool, PANELS["pq"] + 1, KD - 1)
            rests_loop(pool, PANELS["eu"], NK + 1)
            pool.wait_ge(panel_done, PANELS["ev"])
            pool.wait_ge(res_parked, 16)
            pool.dma_start(res2, outT).then_inc(res_back, 16)
            pool.dma_start(pTs, pT).then_inc(p_in, 16)
            o2 = Count(pool, S["oh2_done"])
            pool.wait_ge(S["pk_tc"], 1)

            def two(g, i=None):
                e = et[:, T + 4 * g:T + 4 * g + 2] if i is None else et[:, bass.ds(i * 8 + (T + 4 * g), 2)]
                if g >= 2:
                    pool.wait_ge(S["tok_mm"], 4 * g - 4 if i is None else i * 8 + (4 * g - 4))
                pstep.link(pool.tensor_copy(e4, e))
                pool.sem_inc(S["oh2_turn"], 1)
                for t in range(2):
                    c = (g % 2 * 4 + t) * P
                    o2.mark(pool.tensor_scalar(oh2[:, c:c + P], iota, e4[:, t:t + 1], None, ALU.is_equal))
                pool.wait_ge(o2.sem, o2.value())

            pstep, e4 = Count(pool, pool_step), cols[:, 32:34]
            for g in range(2):
                two(g)
            with pool.Fori(0, T // 8 - 1) as i:
                o2.enter(i, 4)
                pstep.enter(i, 2)
                for g in range(2, 4):
                    two(g, i)
                o2.leave(T // 8 - 1)
                pstep.leave(T // 8 - 1)
            rests_loop(pool, PANELS["ev"] + 1, NK - 1)
            for q in (0, 2):
                x_rest(pool, "ple", nx(), q)
            rests_loop(pool, PANELS["pg"], KD)


def _tiles(v):
    return v.reshape(-1, P).T


def _columns(w, width=P):
    k, m = w.shape
    return w.reshape(k // P, P, m // width, width).transpose(2, 1, 0, 3).reshape(m // width, P, -1)


def _pack(blocks):
    a = blocks.transpose(1, 0, 2).reshape(P, -1)
    n = -(-a.shape[1] // D)
    out = np.zeros((n, P, D), a.dtype)
    for i in range(n):
        part = a[:, i * D:(i + 1) * D]
        out[i, :, :part.shape[1]] = part
    return out


def _layout(i):
    f32 = np.float32
    a = {k: np.asarray(v) for k, v in i.items()}
    a = {k: (v if k in ("x", "positions_2", "final_norm") else v[0]) for k, v in a.items()}
    stream = np.zeros((NPANELS, P, D), f32)

    def put(name, panels, at=0, step=1):
        n = PANELS[name] + at
        stream[n:n + step * len(panels):step] = panels

    w = a["w_in"]
    at = (4 + 4 * HG) * P
    put("cx", _columns(w[:, at:at + 2 * P]))
    put("cx2", _columns(w[:, at + 2 * P:at + 6 * P]))
    at = 0
    for name, n in (("u", 4), ("q", 6), ("f", 6), ("i", 6), ("og", 6), ("cx", 6), ("v", 6), ("o", 6)):
        if name != "cx":
            put(name, _columns(w[:, at:at + n * P]))
        at += n * P
    gates = np.zeros((D, P), f32)
    gates[:, 0:4], gates[:, 32:36] = w[:, at:at + 4], w[:, at + 4:at + 8]
    put("if", _columns(gates))
    at += 8
    put("ga", _columns(w[:, at:at + GATES_1 * P]))
    put("ga2", _columns(w[:, at + GATES_1 * P:at + D]))
    put("gb", _columns(w[:, at + D:at + 2 * D]))
    put("merge", _columns(w[:, at + 2 * D:at + 3 * D]), 0, 2)
    put("merge", _columns(a["w_branch"]), 1, 2)
    b = np.zeros((2, P, 4, P), f32)
    c = np.zeros((2, P, 16, 32), f32)
    for k, (bn, cn) in enumerate((("s5_b_re", "s5_c_re"), ("s5_b_im", "s5_c_im"))):
        for g in range(32):
            j, gi = g // 2, g % 2
            r = 32 * (j % 4) + 16 * gi
            b[k, r:r + 16, j // 4, 64 * gi:64 * gi + 64] = a[bn][g].T
            c[k, 64 * gi:64 * gi + 64, j, 16 * gi:16 * gi + 16] = a[cn][g].T
    stream[PANELS["s5"]] = np.concatenate([b[0].reshape(P, -1), b[1].reshape(P, -1), c[0].reshape(P, -1), c[1].reshape(P, -1)], 1)
    put("glu", _pack(_columns(a["s5_w_glu"])))
    qk = np.zeros((32, P, P), f32)
    for h in range(MH):
        for half in range(2):
            for mi, (_, _, mr, m0) in enumerate(head_parts(h)):
                for ki, (_, k0, kr, c0) in enumerate(head_parts(h)):
                    qk[h * 8 + half * 4 + mi * 2 + ki, k0:k0 + kr, :mr] = \
                        a["ml_w_qk"][h, c0:c0 + kr, half * MD + m0:half * MD + m0 + mr]
    put("qk", _pack(qk))
    put("wout", _columns(a["w_out"]))
    f = FT * P
    put("up", _columns(a["ffn_w_up"][:, :f]), 0, 2)
    put("up", _columns(a["ffn_w_up"][:, f:]), 1, 2)
    put("down", a["ffn_w_down"].reshape(FT, P, D))
    w = a["w_in_2"]
    put("in2", _columns(w[:, :2048]))
    kr = np.zeros((D, P), f32)
    kr[:, :64] = w[:, 2048:]
    put("in2", _columns(kr), 16)
    wp = a["w_pool_2"].reshape(4, 2, P, 2, P)
    put("pool", _pack(wp.transpose(0, 3, 1, 2, 4).reshape(16, P, P)))
    uq = a["w_uq_2"].reshape(512, AH, 192)
    put("uq", _pack(_columns(uq[:, :, :P].reshape(512, -1))))
    put("uqr", _pack(_columns(uq[:, :, P:].reshape(512, -1), 64)))
    ukv = a["w_ukv_2"].reshape(512, AH, 256)
    put("ukn", _pack(_columns(ukv[:, :, :P].reshape(512, -1))))
    put("ukv", _columns(ukv[:, :, P:].reshape(512, -1), BANK))
    put("wout2", _columns(a["w_out_2"]))
    put("pq", _columns(a["w_pq_2"]))
    sk = np.stack([a["sub_k1_2"], a["sub_k2_2"]], 1).reshape(16, NK, P)
    put("subk", _pack(sk.transpose(0, 2, 1)))
    put("eu", _columns(a["expert_u_2"].T))
    put("ev", a["expert_v_2"].reshape(NK, P, D))
    put("pp", _pack(_columns(a["w_ple_proj_2"])))
    put("pg", _columns(a["w_ple_gate_2"]))

    par = np.zeros((P, NCOL), f32)

    def col(name, v, at=0):
        par[:v.shape[0], COL[name] + at:COL[name] + at + v.shape[1]] = v

    for name, src in (("mix", "mix_norm"), ("ffn", "ffn_norm"), ("final", "final_norm"), ("mix2", "mix_norm_gain_2"),
                      ("ffn2", "ffn_norm_gain_2"), ("ple", "ple_norm_gain_2"), ("s5_d", "s5_d"), ("b_glu", "s5_b_glu"),
                      ("hg_lb", "hg_lower_bounds"), ("hg_norm", "hg_norm"), ("conv_b", "ml_conv_b"), ("ml_norm", "ml_norm"),
                      ("pool_scale", "pool_scale_2"), ("q_lat", "q_lat_gain_2"), ("kv_lat", "kv_lat_gain_2")):
        col(name, _tiles(a[src]))
    col("lam_re", _tiles(a["s5_lam_re"].reshape(-1)))
    col("lam_im", _tiles(a["s5_lam_im"].reshape(-1)))
    col("log_dt", _tiles(np.repeat(a["s5_log_dt"], 64)))
    for t in range(4):
        col("conv_w", _tiles(a["ml_conv_w"][t]), 6 * t)
    col("b_ig", a["ml_b_ig"].reshape(4, 1))
    par[32:36, COL["b_fg"]] = a["ml_b_fg"]
    fc = np.concatenate([a["ffn_conv_w"], a["ffn_conv_b"][None]]).reshape(4, 2, FT, P)
    col("fconv", fc.transpose(3, 2, 1, 0).reshape(P, -1))
    for name, src in (("qn", "q_norm_gain_2"), ("kn", "k_norm_gain_2")):
        col(name + "_n", a[src][:P].reshape(P, 1))
        col(name + "_r", a[src][P:].reshape(64, 1))

    con = np.zeros((P, NCONST), f32)
    con[:, CC["ident"]:CC["ident"] + P] = np.eye(P)
    con[:, CC["ones"]:CC["ones"] + P] = 1
    con[:, CC["iota"]:CC["iota"] + P] = np.arange(P)
    con[:64, CC["invfreq"]] = np.tile(f32(10000.0) ** (-np.arange(0, 64, 2, dtype=f32) / f32(64)), 2)
    for m in range(32):
        con[m + 32, CC["perm"] + m] = -1
        con[m, CC["perm"] + m + 32] = 1
    mix = np.zeros((P, NMIX), f32)
    s, t = np.arange(P)[:, None], np.arange(P)[None]
    for l in range(8):
        m = 32 >> l if l < 6 else 64
        ok = (s // (2 * m) == t // (2 * m)) & (s % (2 * m) < m) & (t % (2 * m) >= m) if l < 7 else s == t
        mix[:, MC["hgmask"] + l * P:MC["hgmask"] + (l + 1) * P] = ok
    mix[:, MC["causal"]:MC["causal"] + P] = np.where(s <= t, 0, NEG)
    for h in range(MH):
        mix[h, MC["sel"] + h * P:MC["sel"] + (h + 1) * P] = 1
    mix[:, MC["tidx"]:MC["tidx"] + T] = np.arange(T)
    chunk = np.where(t // 64 <= s // 64, 0, NEG)
    mix[:, MC["chunkmask"]:MC["chunkmask"] + P] = chunk
    mix[:, MC["chunkmask"] + T:MC["chunkmask"] + T + P] = chunk
    for k in range(4):
        mix[:, MC["invcnt"] + k * T:MC["invcnt"] + (k + 1) * T] = 1 / np.minimum(np.arange(T) + 1, 2 << k).astype(f32)

    def channel_major(v):
        return np.ascontiguousarray(v.T.reshape(-1, P, T).transpose(1, 0, 2).reshape(P, -1))

    pos = np.ascontiguousarray(np.broadcast_to(a["positions_2"].astype(np.int32), (64, T)))
    return {"xT": channel_major(a["x"][0]), "stream": stream, "params": par, "consts": con, "mixc": mix,
            "pT": channel_major(a["p_2"][0]), "pos": pos}


_SHAPES = (("xT", (P, KD * T)), ("stream", (NPANELS, P, D)), ("params", (P, NCOL)), ("consts", (P, NCONST)),
           ("mixc", (P, NMIX)), ("pT", (P, 2 * T)), ("pos", (64, T)))


def kernel(**inputs):
    import concourse.bacc as _bacc
    from concourse.bass_utils import run_bass_kernel_spmd as _run

    nc = _bacc.Bacc("TRN2", target_bir_lowering=False, num_devices=1)
    args = [nc.dram_tensor(name, shape, I32 if name == "pos" else F32, kind="ExternalInput").ap() for name, shape in _SHAPES]
    args.append(nc.dram_tensor("outT", (P, KD * T), F32, kind="ExternalOutput").ap())
    two_blocks_kernel(nc, *args)
    r = _run(nc, [_layout(inputs)], core_ids=[0])
    out = r.results[0]["outT"]
    return np.ascontiguousarray(out.reshape(P, KD, T).transpose(2, 1, 0).reshape(1, T, D))
```
